# Optimizing a Trainium2 kernel written in Bass

```python
import jax, jax.numpy as jnp
from jax import lax
import numpy as np
import jax
import jax.numpy as jnp

D_MODEL = 1024
BATCH = 1
SEQ = 512
DEPTH = 2

CHUNK = 64
EPS = 1e-6

A_HEADS = 4
A_WIDTH = D_MODEL
A_HEAD_DIM = A_WIDTH // A_HEADS
CONV_WIDTH = 4

B_HEADS = 8
B_WIDTH = D_MODEL
B_HEAD_DIM = B_WIDTH // B_HEADS
SB_BLOCK = 128

POOL_WINDOWS = (2, 4, 8, 16)
C_GROUPS = len(POOL_WINDOWS)
C_WIDTH = 2 * D_MODEL
C_GROUP_DIM = C_WIDTH // C_GROUPS

N_EVEN = (DEPTH + 1) // 2
N_ODD = DEPTH // 2
EVEN_SPLITS = [A_WIDTH] * 5 + [A_HEADS] * 2 + [B_WIDTH] * 4
EVEN_IN = sum(EVEN_SPLITS)
EVEN_OUT = A_WIDTH + B_WIDTH
ODD_IN = 2 * C_WIDTH


def rmsnorm(x, g):
    xf = x.astype(jnp.float32)
    y = xf * lax.rsqrt(jnp.mean(xf * xf, axis=-1, keepdims=True) + EPS)
    return y * g.astype(jnp.float32)

def causal_dwconv(x, w):
    K = w.shape[0]
    S = x.shape[1]
    xp = jnp.pad(x, ((0, 0), (K - 1, 0), (0, 0)))
    return sum(xp[:, k:k + S] * w[k].astype(jnp.float32) for k in range(K))

def split_cols(u, sizes):
    idx = list(np.cumsum(sizes)[:-1])
    return jnp.split(u, idx, axis=-1)

def mlstm(q, k, v, ig, lf):
    Bn, S, H, dh = q.shape
    nc = S // CHUNK
    k = k * (dh ** -0.5)

    def chunks4(t):
        return t.reshape(Bn, nc, CHUNK, H, dh).transpose(1, 0, 3, 2, 4)

    def chunks3(t):
        return t.reshape(Bn, nc, CHUNK, H).transpose(1, 0, 3, 2)

    xs = (chunks4(q), chunks4(k), chunks4(v), chunks3(ig), chunks3(lf))
    tri = jnp.tril(jnp.ones((CHUNK, CHUNK), dtype=bool))

    def step(carry, inp):
        C, n, m = carry
        qc, kc, vc, ic, fc = inp
        b = jnp.cumsum(fc, axis=-1)
        Dm = jnp.where(tri, b[..., :, None] - b[..., None, :] + ic[..., None, :], -1e30)
        m_inter = b + m[..., None]
        m_t = jnp.maximum(m_inter, jnp.max(Dm, axis=-1))
        W = jnp.exp(Dm - m_t[..., None])
        Sc = jnp.einsum('bhtd,bhsd->bhts', qc, kc) * W
        s_inter = jnp.exp(m_inter - m_t)
        num = (jnp.einsum('bhts,bhsd->bhtd', Sc, vc)
               + s_inter[..., None] * jnp.einsum('bhvk,bhtk->bhtv', C, qc))
        den = jnp.sum(Sc, axis=-1) + s_inter * jnp.einsum('bhk,bhtk->bht', n, qc)
        h = num / jnp.maximum(jnp.abs(den), jnp.exp(-m_t))[..., None]
        g = b[..., -1]
        a = g[..., None] - b + ic
        m_new = jnp.maximum(g + m, jnp.max(a, axis=-1))
        decay = jnp.exp(g + m - m_new)
        wa = jnp.exp(a - m_new[..., None])
        C_new = decay[..., None, None] * C + jnp.einsum('bhs,bhsv,bhsk->bhvk', wa, vc, kc)
        n_new = decay[..., None] * n + jnp.einsum('bhs,bhsk->bhk', wa, kc)
        return (C_new, n_new, m_new), h

    init = (jnp.zeros((Bn, H, dh, dh), jnp.float32),
            jnp.zeros((Bn, H, dh), jnp.float32),
            jnp.zeros((Bn, H), jnp.float32))
    _, hs = lax.scan(step, init, xs)
    return hs.transpose(1, 0, 3, 2, 4).reshape(Bn, S, H * dh)

def stick_breaking(q, k, v):
    S, dh = q.shape[2], q.shape[3]
    scale = dh ** -0.5
    outs = []
    for blk in range(S // SB_BLOCK):
        q0 = blk * SB_BLOCK
        q1 = q0 + SB_BLOCK
        z = jnp.einsum('bhqd,bhkd->bhqk', q[:, :, q0:q1], k[:, :, :q1]) * scale
        mask = jnp.arange(q1)[None, :] < (q0 + jnp.arange(SB_BLOCK))[:, None]
        log_1mb = jnp.where(mask, jax.nn.log_sigmoid(-z), 0.0)
        after = lax.cumsum(log_1mb, axis=3, reverse=True) - log_1mb
        A = jnp.where(mask, jnp.exp(jax.nn.log_sigmoid(z) + after), 0.0)
        outs.append(jnp.einsum('bhqk,bhkd->bhqd', A, v[:, :, :q1]))
    return jnp.concatenate(outs, axis=2)

def multiscale_pool(p):
    S = p.shape[1]
    cs = jnp.cumsum(p, axis=1)
    cs0 = jnp.pad(cs, ((0, 0), (1, 0), (0, 0), (0, 0)))
    t = jnp.arange(S)
    outs = []
    for g, w in enumerate(POOL_WINDOWS):
        upper = cs0[:, 1:, g]
        lower = jnp.pad(cs0[:, :S + 1 - w, g], ((0, 0), (w - 1, 0), (0, 0)))
        cnt = jnp.minimum(t + 1, w).astype(jnp.float32)
        outs.append((upper - lower) / cnt[None, :, None] - p[:, :, g])
    return jnp.stack(outs, axis=2)

def head_norm(h, g, n_heads):
    Bn, S, W = h.shape
    hh = h.reshape(Bn, S, n_heads, W // n_heads)
    hh = hh * lax.rsqrt(jnp.mean(hh * hh, axis=-1, keepdims=True) + EPS)
    return hh.reshape(Bn, S, W) * g.astype(jnp.float32)

def even_layer(x, pre_g, post_g, w_in, conv_w, b_i, b_f, hn_g, w_out):
    Bn, S, _ = x.shape
    h = rmsnorm(x, pre_g)
    u = h @ w_in.astype(jnp.float32)
    qa, ka, va, oa, za, ia, fa, qb, kb, vb, zb = split_cols(u, EVEN_SPLITS)
    qk = jax.nn.silu(causal_dwconv(jnp.concatenate([qa, ka], axis=-1), conv_w))
    qa, ka = qk[..., :A_WIDTH], qk[..., A_WIDTH:]
    ig = ia + b_i.astype(jnp.float32)
    lf = jax.nn.log_sigmoid(fa + b_f.astype(jnp.float32))
    hs = (Bn, S, A_HEADS, A_HEAD_DIM)
    ha = mlstm(qa.reshape(hs), ka.reshape(hs), va.reshape(hs), ig, lf)
    ha = jax.nn.sigmoid(oa) * ha
    ya = head_norm(ha, hn_g, A_HEADS) * jax.nn.silu(za)
    def heads(t):
        return t.reshape(Bn, S, B_HEADS, B_HEAD_DIM).transpose(0, 2, 1, 3)
    hb = stick_breaking(heads(qb), heads(kb), heads(vb))
    hb = hb.transpose(0, 2, 1, 3).reshape(Bn, S, B_WIDTH)
    yb = hb * jax.nn.silu(zb)
    y = jnp.concatenate([ya, yb], axis=-1) @ w_out.astype(jnp.float32)
    return x + rmsnorm(y, post_g).astype(x.dtype)

def odd_layer(x, pre_g, post_g, w_in, pool_w, pool_scale, w_out):
    Bn, S, _ = x.shape
    h = rmsnorm(x, pre_g)
    u = h @ w_in.astype(jnp.float32)
    p, z = u[..., :C_WIDTH], u[..., C_WIDTH:]
    pooled = multiscale_pool(p.reshape(Bn, S, C_GROUPS, C_GROUP_DIM))
    mixed = jnp.einsum('bsgc,gce->bsge', pooled, pool_w.astype(jnp.float32))
    mixed = mixed.reshape(Bn, S, C_WIDTH) * pool_scale.astype(jnp.float32)
    y = (mixed * jax.nn.silu(z)) @ w_out.astype(jnp.float32)
    return x + rmsnorm(y, post_g).astype(x.dtype)

def first_inputs(seed: int = 0) -> dict:
    key = jax.random.key(seed)
    ks = jax.random.split(key, 14)
    f32 = jnp.float32
    x = jax.random.normal(ks[0], (BATCH, SEQ, D_MODEL), f32)
    pre_norm_g = 1.0 + 0.02 * jax.random.normal(ks[1], (DEPTH, D_MODEL), f32)
    post_norm_g = 1.0 + 0.02 * jax.random.normal(ks[2], (DEPTH, D_MODEL), f32)
    w_in_ab = jax.random.normal(ks[3], (N_EVEN, D_MODEL, EVEN_IN), f32) * D_MODEL ** -0.5
    conv_qk = jax.random.normal(ks[4], (N_EVEN, CONV_WIDTH, 2 * A_WIDTH), f32) * CONV_WIDTH ** -0.5
    bias_i = 0.1 * jax.random.normal(ks[5], (N_EVEN, A_HEADS), f32)
    bias_f = 3.0 + 3.0 * jax.random.uniform(ks[6], (N_EVEN, A_HEADS), f32)
    head_norm_g = 1.0 + 0.02 * jax.random.normal(ks[7], (N_EVEN, A_WIDTH), f32)
    w_out_ab = jax.random.normal(ks[8], (N_EVEN, EVEN_OUT, D_MODEL), f32) * EVEN_OUT ** -0.5
    w_in_c = jax.random.normal(ks[9], (N_ODD, D_MODEL, ODD_IN), f32) * D_MODEL ** -0.5
    pool_w = jax.random.normal(ks[10], (N_ODD, C_GROUPS, C_GROUP_DIM, C_GROUP_DIM), f32) * C_GROUP_DIM ** -0.5
    pool_scale = 1.0 + 0.1 * jax.random.normal(ks[11], (N_ODD, C_WIDTH), f32)
    w_out_c = jax.random.normal(ks[12], (N_ODD, C_WIDTH, D_MODEL), f32) * C_WIDTH ** -0.5
    return {"x": x, "pre_norm_g": pre_norm_g, "post_norm_g": post_norm_g,
            "w_in_ab": w_in_ab, "conv_qk": conv_qk, "bias_i": bias_i, "bias_f": bias_f,
            "head_norm_g": head_norm_g, "w_out_ab": w_out_ab,
            "w_in_c": w_in_c, "pool_w": pool_w, "pool_scale": pool_scale, "w_out_c": w_out_c}

def first_block(x, pre_norm_g, post_norm_g, w_in_ab, conv_qk, bias_i, bias_f, head_norm_g,
              w_out_ab, w_in_c, pool_w, pool_scale, w_out_c):
    for layer in range(DEPTH):
        if layer % 2 == 0:
            e = layer // 2
            x = even_layer(x, pre_norm_g[layer], post_norm_g[layer], w_in_ab[e], conv_qk[e],
                           bias_i[e], bias_f[e], head_norm_g[e], w_out_ab[e])
        else:
            o = layer // 2
            x = odd_layer(x, pre_norm_g[layer], post_norm_g[layer], w_in_c[o], pool_w[o],
                          pool_scale[o], w_out_c[o])
    return x


DEPTH_2 = 1

HQ_A = 8
HKV_A = 2
DH_A = 64
WINDOW = 128
BLOCK_A = 128
H_B = 4
DK_B = 128
DV_B = 256
GK_RANK = 16
GATE_NORMALIZER = 16.0
CHUNK_B = 64
SUB_B = 16
D_FF = 2816
CONV_W = 3

QA_W = HQ_A * DH_A
KVA_W = HKV_A * DH_A
QKB_W = H_B * DK_B
VB_W = H_B * DV_B
SPLITS = (QA_W, KVA_W, KVA_W, QKB_W, QKB_W, VB_W, VB_W, GK_RANK, D_MODEL, D_MODEL)
IN_W = QA_W + 2 * KVA_W + 2 * QKB_W + 2 * VB_W + GK_RANK + 2 * D_MODEL


def rmsnorm_2(x, g):
    xf = x.astype(jnp.float32)
    y = xf * lax.rsqrt(jnp.mean(xf * xf, axis=-1, keepdims=True) + EPS)
    return (y * g.astype(jnp.float32)).astype(x.dtype)

def split_cols_2(z):
    idx = []
    acc = 0
    for w in SPLITS[:-1]:
        acc += w
        idx.append(acc)
    return jnp.split(z, idx, axis=-1)

def sliding_window_sink_attention(q, k, v, sinks):
    B, S = q.shape[0], q.shape[1]
    nb = S // BLOCK_A
    G = HQ_A // HKV_A
    qb = q.reshape(B, nb, BLOCK_A, HKV_A, G, DH_A)
    kb = k.reshape(B, nb, BLOCK_A, HKV_A, DH_A)
    vb = v.reshape(B, nb, BLOCK_A, HKV_A, DH_A)
    shift = lambda t: jnp.concatenate([jnp.zeros_like(t[:, :1]), t[:, :-1]], axis=1)
    kk = jnp.concatenate([shift(kb), kb], axis=2)
    vv = jnp.concatenate([shift(vb), vb], axis=2)
    s = jnp.einsum("bnqhgd,bnkhd->bnhgqk", qb, kk).astype(jnp.float32) * (DH_A ** -0.5)
    qpos = jnp.arange(BLOCK_A)[:, None]
    kpos = jnp.arange(2 * BLOCK_A)[None, :] - BLOCK_A
    band = (kpos <= qpos) & (kpos > qpos - WINDOW)
    kabs = (jnp.arange(nb) * BLOCK_A)[:, None, None] + kpos[None]
    mask = band[None] & (kabs >= 0)
    s = jnp.where(mask[None, :, None, None], s, -jnp.inf)
    sink = sinks.astype(jnp.float32).reshape(HKV_A, G)[None, None, :, :, None, None]
    m = jnp.maximum(jnp.max(s, axis=-1, keepdims=True), sink)
    p = jnp.exp(s - m)
    p = p / (jnp.sum(p, axis=-1, keepdims=True) + jnp.exp(sink - m))
    o = jnp.einsum("bnhgqk,bnkhd->bnqhgd", p.astype(v.dtype), vv)
    return o.reshape(B, S, QA_W)

def gla_chunked(q, k, v, gk):
    out_dtype = v.dtype
    f32 = jnp.float32
    B, S = q.shape[0], q.shape[1]
    N = S // CHUNK_B
    NS = CHUNK_B // SUB_B
    to_chunks = lambda t: t.astype(f32).reshape(B, N, CHUNK_B, H_B, t.shape[-1]).transpose(0, 3, 1, 2, 4)
    q = to_chunks(q) * (DK_B ** -0.5)
    k = to_chunks(k)
    v = to_chunks(v)
    b = jnp.cumsum(to_chunks(gk), axis=3)
    b_last = b[:, :, :, -1:]
    kv = jnp.einsum("bhncd,bhnce->bhnde", k * jnp.exp(b_last - b), v)
    decay = jnp.exp(b_last[:, :, :, 0])

    def step(state, inp):
        kv_n, d_n = inp
        return d_n[..., None] * state + kv_n, state

    _, s_prev = lax.scan(step, jnp.zeros((B, H_B, DK_B, DV_B), f32),
                         (jnp.moveaxis(kv, 2, 0), jnp.moveaxis(decay, 2, 0)))
    s_prev = jnp.moveaxis(s_prev, 0, 2)
    o_inter = jnp.einsum("bhncd,bhnde->bhnce", q * jnp.exp(b), s_prev)
    sub = lambda t: t.reshape(B, H_B, N, NS, SUB_B, t.shape[-1])
    qs, ks, bs = sub(q), sub(k), sub(b)
    r = bs[:, :, :, :, -1]
    lower = jnp.arange(NS)[:, None] > jnp.arange(NS)[None, :]
    dq = jnp.where(lower[:, :, None, None], bs[:, :, :, :, None] - r[:, :, :, None, :, None], 0.0)
    q_ref = qs[:, :, :, :, None] * jnp.exp(dq)
    k_ref = ks * jnp.exp(r[:, :, :, :, None] - bs)
    a_off = jnp.einsum("bhnijtd,bhnjsd->bhnijts", q_ref, k_ref)
    a_off = jnp.where(lower[:, :, None, None], a_off, 0.0)
    tri = jnp.arange(SUB_B)[:, None] >= jnp.arange(SUB_B)[None, :]
    dd = jnp.where(tri[:, :, None], bs[..., :, None, :] - bs[..., None, :, :], 0.0)
    a_diag = jnp.einsum("bhnitsd,bhnisd->bhnits", qs[..., :, None, :] * jnp.exp(dd), ks)
    a_diag = jnp.where(tri, a_diag, 0.0)
    a_blocks = a_off + jnp.eye(NS, dtype=f32)[:, :, None, None] * a_diag[:, :, :, :, None]
    a_intra = a_blocks.transpose(0, 1, 2, 3, 5, 4, 6).reshape(B, H_B, N, CHUNK_B, CHUNK_B)
    o = o_inter + jnp.einsum("bhnts,bhnse->bhnte", a_intra, v)
    return o.transpose(0, 2, 3, 1, 4).reshape(B, S, H_B, DV_B).astype(out_dtype)

def causal_dwconv_2(a, w, bias):
    y = lax.conv_general_dilated(a, w[:, None, :].astype(a.dtype), window_strides=(1,),
                                 padding=[(CONV_W - 1, 0)], dimension_numbers=("NWC", "WIO", "NWC"),
                                 feature_group_count=a.shape[-1])
    return y + bias

def second_inputs(seed: int = 0) -> dict:
    key = jax.random.key(seed)
    ks = jax.random.split(key, 17)
    nrm = lambda k, shape, scale: jax.random.normal(k, shape, jnp.float32) * scale
    return {
        "x": nrm(ks[0], (BATCH, SEQ, D_MODEL), 1.0),
        "ln_mix_g": 1.0 + nrm(ks[1], (DEPTH_2, D_MODEL), 0.05),
        "w_in": nrm(ks[2], (DEPTH_2, D_MODEL, IN_W), D_MODEL ** -0.5),
        "q_norm_g": 1.0 + nrm(ks[3], (DEPTH_2, DH_A), 0.05),
        "k_norm_g": 1.0 + nrm(ks[4], (DEPTH_2, DH_A), 0.05),
        "sinks": nrm(ks[5], (DEPTH_2, HQ_A), 1.0),
        "w_gk_up": nrm(ks[6], (DEPTH_2, GK_RANK, QKB_W), GK_RANK ** -0.5),
        "b_gk": nrm(ks[7], (DEPTH_2, QKB_W), 0.1),
        "gla_norm_g": 1.0 + nrm(ks[8], (DEPTH_2, DV_B), 0.05),
        "w_branch_a": nrm(ks[9], (DEPTH_2, QA_W, D_MODEL), QA_W ** -0.5),
        "w_branch_b": nrm(ks[10], (DEPTH_2, VB_W, D_MODEL), VB_W ** -0.5),
        "w_out": nrm(ks[11], (DEPTH_2, D_MODEL, D_MODEL), D_MODEL ** -0.5),
        "ln_ffn_g": 1.0 + nrm(ks[12], (DEPTH_2, D_MODEL), 0.05),
        "w_ffn_in": nrm(ks[13], (DEPTH_2, D_MODEL, 2 * D_FF), D_MODEL ** -0.5),
        "conv_w": nrm(ks[14], (DEPTH_2, CONV_W, D_FF), CONV_W ** -0.5),
        "conv_b": nrm(ks[15], (DEPTH_2, D_FF), 0.02),
        "w_ffn_out": nrm(ks[16], (DEPTH_2, D_FF, D_MODEL), D_FF ** -0.5),
    }

def second_block(x, ln_mix_g, w_in, q_norm_g, k_norm_g, sinks, w_gk_up, b_gk, gla_norm_g,
              w_branch_a, w_branch_b, w_out, ln_ffn_g, w_ffn_in, conv_w, conv_b, w_ffn_out):
    B, S = x.shape[0], x.shape[1]
    for l in range(DEPTH_2):
        h = rmsnorm_2(x, ln_mix_g[l])
        z = h @ w_in[l]
        qa, ka, va, qb, kb, vb, rb, gk_lr, ga, gb = split_cols_2(z)
        qa = rmsnorm_2(qa.reshape(B, S, HQ_A, DH_A), q_norm_g[l])
        ka = rmsnorm_2(ka.reshape(B, S, HKV_A, DH_A), k_norm_g[l])
        ya = sliding_window_sink_attention(qa, ka, va.reshape(B, S, HKV_A, DH_A), sinks[l])
        gk = jax.nn.log_sigmoid((gk_lr @ w_gk_up[l] + b_gk[l]).astype(jnp.float32)) / GATE_NORMALIZER
        yb = gla_chunked(qb.reshape(B, S, H_B, DK_B), kb.reshape(B, S, H_B, DK_B),
                         vb.reshape(B, S, H_B, DV_B), gk.reshape(B, S, H_B, DK_B))
        yb = rmsnorm_2(yb, gla_norm_g[l]) * jax.nn.silu(rb.reshape(B, S, H_B, DV_B))
        yb = yb.reshape(B, S, VB_W)
        merged = jax.nn.sigmoid(ga) * (ya @ w_branch_a[l]) + jax.nn.sigmoid(gb) * (yb @ w_branch_b[l])
        x = x + merged @ w_out[l]
        h = rmsnorm_2(x, ln_ffn_g[l])
        a, u = jnp.split(h @ w_ffn_in[l], 2, axis=-1)
        a = causal_dwconv_2(a, conv_w[l], conv_b[l])
        x = x + (jax.nn.silu(a) * u) @ w_ffn_out[l]
    return x


def setup_inputs(seed=0):
    out = dict(first_inputs(seed))
    for name, value in second_inputs(seed + 1).items():
        if name != "x":
            out[name + "_2"] = value
    return out


def reference(
    x, pre_norm_g, post_norm_g, w_in_ab, conv_qk, bias_i, bias_f, head_norm_g, w_out_ab, w_in_c,
    pool_w, pool_scale, w_out_c, ln_mix_g_2, w_in_2, q_norm_g_2, k_norm_g_2, sinks_2, w_gk_up_2,
    b_gk_2, gla_norm_g_2, w_branch_a_2, w_branch_b_2, w_out_2, ln_ffn_g_2, w_ffn_in_2, conv_w_2,
    conv_b_2, w_ffn_out_2,
):
    x = first_block(
        x, pre_norm_g, post_norm_g, w_in_ab, conv_qk, bias_i, bias_f, head_norm_g, w_out_ab,
        w_in_c, pool_w, pool_scale, w_out_c,
    )
    return second_block(
        x, ln_mix_g_2, w_in_2, q_norm_g_2, k_norm_g_2, sinks_2, w_gk_up_2, b_gk_2, gla_norm_g_2,
        w_branch_a_2, w_branch_b_2, w_out_2, ln_ffn_g_2, w_ffn_in_2, conv_w_2, conv_b_2,
        w_ffn_out_2,
    )


_drawn_inputs = setup_inputs


def setup_inputs(seed=0):
    import zlib

    import numpy as np

    out = dict(_drawn_inputs(seed))
    spreads = {}
    factors = {'bias_i': 200.0,
     'head_norm_g': 3.841,
     'q_norm_g_2': 8.0,
     'k_norm_g_2': 8.0,
     'sinks_2': 200.0,
     'b_gk_2': 6.998,
     'gla_norm_g_2': 6.047,
     'conv_b_2': 8.0,
     'ln_ffn_g_2': 3.463}
    for name, (base, spread) in spreads.items():
        noise = np.random.default_rng([zlib.crc32(name.encode()), seed]).standard_normal(out[name].shape)
        drawn = base * np.exp(spread * noise) if base else spread * noise
        out[name] = jnp.asarray(drawn.astype(out[name].dtype))
    for name, factor in factors.items():
        out[name] = (out[name] * factor).astype(out[name].dtype)
    return out
```

```python
from contextlib import ExitStack

import numpy as np

import concourse.bass as bass
from concourse import mybir

F32 = mybir.dt.float32
F32R = mybir.dt.float32r
I32 = mybir.dt.int32
ALU = mybir.AluOpType
ACT = mybir.ActivationFunctionType
AX = mybir.AxisListType.X

P = 128
S = 512
NT = S // P
D = 1024
KC = D // P
EPS = 1e-6
KB = 1024

HA, DA = 4, 256
HB, DB = 8, 128
WINDOWS = (2, 4, 8, 16)
HQ, HKV, DH = 8, 2, 64
HG, DK, DV, RANK = 4, 128, 256, 16
GATE = 16.0
LEVELS = (64, 32, 16, 8, 4, 2, 1)
DFF = 2816
FC = DFF // P
FI = FC // 2

PLAN = [
    ("turn0", 1, 0),
    ("qb", 2, 2), ("kb", 2, 2), ("vb", 2, 2), ("zb", 2, 2),
    ("qa", 2, 2), ("ka", 2, 2), ("va", 2, 2), ("oa", 2, 2), ("za", 2, 2),
    ("a_out", HA, 0),
    ("y0", 2, 4), ("turn2", 1, 0),
    ("mix", 4, 5),
    ("y1", 2, 4), ("turn3", 1, 0),
    ("wq", 1, 2), ("wkv", 1, 2), ("gq", 1, 2), ("gk", 1, 2),
    ("w_out", NT, 0),
    ("gv", 2, 2), ("gr", 2, 2), ("ga", 2, 2),
    ("g_out", HG, 0), ("gb", 2, 2), ("turn4", 1, 0),
    ("bra", 2, 1), ("brb", 2, 2), ("y2", 2, 2), ("turn5", 1, 0),
    ("ffn", FI, 2), ("y3", 2, 6),
]
UNIT, GROUP = {}, {}
_u = _g = 0
for _name, _n, _per in PLAN:
    UNIT[_name], GROUP[_name] = _u, _g
    _u += _n * _per
    _g += _n * (3 if _name == "mix" else 1)
UNITS = _u
assert UNITS % 2 == 0
TURNS = {"turn0": 0, "turn2": 1, "turn3": 2, "turn4": 3, "turn5": 4}

VECS = [("pre", 16), ("lnmix", 8), ("lnffn", 8), ("convqk", 64), ("pscale", 16), ("bgk", 4),
        ("hn", 8), ("qn", 1), ("kn", 1), ("gla", 2)]
VECS2 = [("cw", 66), ("cb", 22)]
COL = {}
_c = 0
for _name, _n in VECS + VECS2:
    COL[_name] = _c
    _c += _n
NV1 = sum(n for _, n in VECS)
NV2 = sum(n for _, n in VECS2)
assert NV1 == P

IN_AB_B = 5 * D + 2 * HA
C2 = {"qa": 0, "kv": 512, "gq": 768, "gk": 1280, "gv": 1792, "gr": 2816, "lr": 3840, "ga": 3856, "gb": 4880}
SEG_T = {3: 0, 2: 512, 0: 896, 1: 1024}
SEG_S = {0: 0, 1: 512, 3: 896, 2: 1024}
CAUSAL = 1280


A_OFF = (0, 512, 896, 1152)
STEPS_NEAR = len(LEVELS) * HG
FAR = STEPS_NEAR


def gla_schedule(evacuate, step):
    s = 0
    for name in ("gv", "gr"):
        for n in range(2):
            for j in range(4):
                group = 2 * (name == "gr") + n
                while s < min(STEPS_NEAR, STEPS_NEAR * group // 4 + 4 + 3 * j // 4):
                    step(s)
                    s += 1
                evacuate(name, n, j)
    while s < STEPS_NEAR:
        step(s)
        s += 1


class Line:

    def __init__(self, engine, sem):
        self.engine, self.sem, self.base, self.k = engine, sem, 0, 0

    def step(self, ins):
        ins.then_inc(self.sem, 1)
        self.k += 1
        self.engine.wait_ge(self.sem, self.base + self.k)

    def tell(self, ins, sem, value):
        ins.then_inc(sem, 1)
        self.engine.wait_ge(sem, value)

    def enter(self, i, per):
        self.start = self.base + self.k
        self.base, self.k, self.per = self.start + i * per, 0, per

    def leave(self, times):
        assert self.k == self.per, (self.k, self.per)
        self.base, self.k = self.start + times * self.per, 0


def build(nc, A, out, dbg=None, upto=None):
    with ExitStack() as ctx:
        def sem(name):
            return ctx.enter_context(nc.semaphore(name))

        base = (nc.sbuf_base + 31) // 32 * 32

        def at(name, shape, dtype, kb):
            off = base + int(kb * KB) // 32 * 32
            return nc.alloc_sbuf_tensor_at(name, shape, dtype, offset=off)

        raw = [at(f"raw{s}", [P, 4, 512], F32, 8 * s) for s in range(2)]
        whi = [at(f"whi{s}", [P, 4, 512], F32R, 16 + 8 * s) for s in range(2)]
        wlo = [at(f"wlo{s}", [P, 4, 512], F32R, 32 + 8 * s) for s in range(2)]
        h_hi = at("h_hi", [P, KC, S], F32R, 48)
        h_lo = at("h_lo", [P, KC, S], F32R, 64)
        x = at("x", [P, NT, D], F32, 80)
        C0 = 96
        ident = at("ident", [P, P], F32, C0)
        tri = at("tri", [P, P], F32, C0 + .5)
        below = at("below", [P, P], F32, C0 + 1)
        band = at("band", [P, 2 * P], F32, C0 + 1.5)
        level = at("level", [P, 7, P], F32, C0 + 2.5)
        vcol = at("vcol", [P, NV1 + NV2], F32, C0 + 6)
        invc = at("invc", [P, 16], F32, C0 + 6.875)
        small = at("small", [P, 256], F32, C0 + 7)
        postg = at("postg", [P, D], F32, C0 + 8)
        g_lf = at("g_lf", [HA, S], F32, C0 + 8)
        sel = at("sel", [HA, HA, P], F32, C0 + 10)
        y32 = at("y32", [P, S], F32, C0 + 12)
        AR = C0 + 14
        ss, var, std, rs, nwt = (small[:, 40 * i:40 * i + 40] for i in range(5))
        sinkb = small[:, 200:208]
        den, rden = small[:, 208:212], small[:, 212:216]
        cT = small[:, 216:232].rearrange("p (t h) -> p t h", h=HA)
        emT = small[:, 232:248].rearrange("p (t h) -> p t h", h=HA)
        spare = small[:, 248:256]
        xn = at("xn", [P, NT, D], F32, AR)
        xn2 = at("xn2", [P, NT, D], F32, AR + 32)
        g_ig, g_t, g_b, g_m = (at(n, [HA, S], F32, AR + 80.25 + 2 * i)
                               for i, n in enumerate(("g_ig", "g_t", "g_b", "g_m")))
        wgate = at("wgate", [P, KC, 2 * HA], F32, AR + 92)
        gtok = at("gtok", [P, NT, 2 * HA], F32, AR + 92.5)
        bias4 = at("bias4", [HA, 2], F32, AR + 92.75)
        qB = at("qB", [P, HB, S], F32, AR + 32)
        kB = at("kB", [P, HB, S], F32, AR + 48)
        yB_hi = at("yB_hi", [P, HB, S], F32R, AR + 32)
        yB_lo = at("yB_lo", [P, HB, S], F32R, AR + 48)
        vB = at("vB", [P, NT, D], F32, 80)
        szB = at("szB", [P, HB, S], F32, AR + 64)
        tB1 = at("tB1", [P, CAUSAL], F32, AR + 80)
        tB2 = at("tB2", [P, CAUSAL], F32, AR + 85)
        aTB = at("aTB", [P, CAUSAL], F32, AR + 90)
        qA = at("qA", [P, KC, S], F32, AR)
        kA = at("kA", [P, KC, S], F32, AR + 16)
        soA = at("soA", [P, NT, D], F32, AR + 64)
        vA = at("vA", [P, NT, HA, DA + 1], F32, AR + 80)
        szA = at("szA", [P, NT, D], F32, 80)
        WA = [at(f"WA{b}", [P, CAUSAL], F32, 48 + 5 * b) for b in range(2)]
        junkA = at("junkA", [P, DA], F32, 60)
        nMb = at("nMb", [P, HA, S], F32, 64)
        yA_hi = at("yA_hi", [P, KC, S], F32R, AR)
        yA_lo = at("yA_lo", [P, KC, S], F32R, AR + 16)
        y_half = at("y_half", [P, NT, 512], F32, AR + 64.25)
        ytmp = at("ytmp", [P, D], F32, AR + 80.25)
        rawv = at("rawv", [P, 2, P], F32, AR + 72)
        junk = at("junk", [P, D], F32, AR + 93.75)
        notfirst = at("notfirst", [P, S], F32, AR + 94)
        m_hi = at("m_hi", [P, 16, S], F32R, AR)
        m_lo = at("m_lo", [P, 16, S], F32R, AR + 32)
        pool_hi = at("pool_hi", [P, 4, S], F32R, AR + 64)
        pool_lo = at("pool_lo", [P, 4, S], F32R, AR + 72)
        PAD = 16
        pw = [at(f"pw{b}", [P, PAD + S], F32, AR + 80 + 2.0625 * b) for b in range(3)]
        szC = at("szC", [P, 4, S], F32, AR + 86.25)
        y_half1 = at("y_half1", [P, NT, 512], F32, AR + 64)
        ytmp1 = at("ytmp1", [P, D], F32, AR + 80)
        ya32 = at("ya32", [P, 4, S], F32, AR)
        qG = at("qG", [P, HG, S], F32, AR + 8)
        kG = at("kG", [P, HG, S], F32, AR + 16)
        bG = at("bG", [P, HG, S], F32, AR + 24)
        vG = at("vG", [P, NT, D], F32, AR + 32)
        rG = at("rG", [P, NT, D], F32, AR + 48)
        atD = at("atD", [P, HG, 4, P], F32, AR + 64)
        atO = at("atO", [P, HG, 6, P], F32, AR + 72)
        dG = [at(f"dG{b}", [P, S], F32, AR + 84 + 2 * b) for b in range(2)]
        qE = [at(f"qE{b}", [P, S], F32, AR + 88 + 2 * b) for b in range(2)]
        kE = [at(f"kE{b}", [P, S], F32, AR + 92 + 2 * b) for b in range(2)]
        qkv = at("qkv", [P, NT, 768], F32, AR + 32)
        qn = at("qn", [P, NT, 640], F32, AR + 44)
        qkT = at("qkT", [P, 5, S], F32, AR + 54)
        sm = at("sm", [P, HQ, 2 * P], F32, AR + 64)
        pT = at("pT", [P, 2, HKV, 4, P], F32, AR + 72)
        junk2 = at("junk2", [P, 5 * P], F32, AR + 80)
        wstat = at("wstat", [P, 5, HQ], F32, AR + 83)
        lrT = at("lrT", [RANK, S], F32, AR + 84)
        lrtok = at("lrtok", [P, NT, RANK], F32, AR + 86)
        wlr = at("wlr", [P, KC, RANK], F32, AR + 86.5)
        wup = at("wup", [RANK, HG * DK], F32, AR + 88)
        gtmp = [at(f"gtmp{b}", [P, S], F32, AR + 90 + 2 * b) for b in range(2)]
        bend = at("bend", [P, 2, HG, NT], F32, AR + 83.5)
        sga = at("sga", [P, KC, S], F32, AR + 8)
        sgb = at("sgb", [P, KC, S], F32, AR + 64)
        mg_hi = at("mg_hi", [P, KC, S], F32R, AR + 24)
        mg_lo = at("mg_lo", [P, KC, S], F32R, AR + 40)
        ya_hi = at("ya_hi", [P, 4, S], F32R, AR + 80)
        ya_lo = at("ya_lo", [P, 4, S], F32R, AR + 88)
        f_hi = at("f_hi", [P, FC, S], F32R, AR)
        f_lo = at("f_lo", [P, FC, S], F32R, AR + 44)
        facc = [at(f"facc{b}", [P, S], F32, AR + 88 + 2 * b) for b in range(2)]

        ps = ctx.enter_context(nc.psum_tensor("ps", [P, 8, 512], F32))
        psf = ps[:].rearrange("p b n -> p (b n)")

        x_in = [sem(f"x_in{t}") for t in range(NT)]
        small_in = sem("small_in")
        postg_in = sem("postg_in")
        lr_in = sem("lr_in")
        const_made = sem("const_made")
        raw_full = [sem(f"raw_full{s}") for s in range(2)]
        hi_made = sem("hi_made")
        unit_taken = sem("unit_taken")
        split_ready = sem("split_ready")
        steps = sem("steps")
        bank_free = [sem(f"bank_free{j}") for j in range(4)]
        act_line = sem("act_line")
        dve_line = sem("dve_line")
        pool_line = sem("pool_line")
        vt_done = sem("vt_done")
        vcol_ready = sem("vcol_ready")
        ss_ready, var_ready, std_ready = sem("ss_ready"), sem("var_ready"), sem("std_ready")
        src_ready = sem("src_ready")
        turned_pe, turned_hi, turned_lo = sem("turned_pe"), sem("turned_hi"), sem("turned_lo")
        x_ready = sem("x_ready")
        gate_pe, gate_dve, gate_act = sem("gate_pe"), sem("gate_dve"), sem("gate_act")
        qk_ready = sem("qk_ready")
        a_s, a_arg, a_exp, a_st, a_o = sem("a_s"), sem("a_arg"), sem("a_exp"), sem("a_st"), sem("a_o")
        a_src, a_turned, a_hi, a_lo = sem("a_src"), sem("a_turned"), sem("a_hi"), sem("a_lo")
        b_z, b_rest, b_beta, b_a, b_t, b_copied, b_o, b_y, b_hi, b_lo = (
            sem(n) for n in ("b_z", "b_rest", "b_beta", "b_a", "b_t", "b_copied", "b_o", "b_y", "b_hi", "b_lo"))
        p_in, p_out, pool_h, pool_ready, m_y, m_hi_done, m_lo_done = (
            sem(n) for n in ("p_in", "p_out", "pool_h", "pool_ready", "m_y", "m_hi_done", "m_lo_done"))
        w_qkv, w_sq, w_n, w_tp, w_qk, w_s, w_sm, w_neg, w_exp, w_p, w_t, w_o, w_ya = (
            sem(n) for n in ("w_qkv", "w_sq", "w_n", "w_tp", "w_qk", "w_s", "w_sm", "w_neg", "w_exp", "w_p",
                             "w_t", "w_o", "w_ya"))
        l_pe, l_dve, l_act = sem("l_pe"), sem("l_dve"), sem("l_act")
        e_d, e_exp, e_qk, e_pe, e_at = sem("e_d"), sem("e_exp"), sem("e_qk"), sem("e_pe"), sem("e_at")
        g_o = sem("g_o")
        c_y, c_hi, c_lo = sem("c_y"), sem("c_hi"), sem("c_lo")
        f_acc, f_silu, f_y, f_hi_done, f_lo_done = (
            sem(n) for n in ("f_acc", "f_silu", "f_y", "f_hi_done", "f_lo_done"))
        stored = sem("stored")

        def col(name, k=0):
            return vcol[:, COL[name] + k:COL[name] + k + 1]

        def rows(v, n):
            return v.rearrange("(r p) -> r p", p=P)

        def wview(w):
            return w.rearrange("(k p) n -> p k n", p=P)

        w_ab, w_oab, w_c, w_pool, w_oc = (
            wview(A["w_in_ab"][0]), wview(A["w_out_ab"][0]), wview(A["w_in_c"][0]), A["pool_w"][0],
            wview(A["w_out_c"][0]))
        w_2, w_ba, w_bb, w_o2, w_fi, w_fo = (
            wview(A[n][0]) for n in ("w_in_2", "w_branch_a_2", "w_branch_b_2", "w_out_2", "w_ffn_in_2",
                                     "w_ffn_out_2"))

        def cols(w, k0, nk, c0, n=512):
            return w[:, k0:k0 + nk, c0:c0 + n]

        block = ctx.enter_context(nc.Block())

        @block.sync
        def _(sp):
            for t in range(NT):
                sp.dma_start(x[:, t], A["x"][0, t * P:(t + 1) * P, :]).then_inc(x_in[t], 16)

            def load(u, slot, src, width=512, nk=4, c0=0, inc=32):
                if isinstance(u, int):
                    if u >= 2:
                        sp.wait_ge(split_ready, u - 1)
                else:
                    sp.wait_ge(split_ready, u - 1)
                sp.dma_start(raw[slot][:, 0:nk, c0:c0 + width], src).then_inc(raw_full[slot], inc)

            def stream(name, w, c0, per, groups):
                u0 = UNIT[name]

                def one(i):
                    for q in range(per):
                        load(u0 + i * per + q, (u0 + q) % 2,
                             w[:, 4 * q:4 * q + 4, bass.ds(c0 + i * 512, 512)])
                if groups == 1:
                    one(0)
                elif u0 == 0:
                    one(0)
                    with sp.Fori(1, groups) as i:
                        one(i)
                else:
                    with sp.Fori(0, groups) as i:
                        one(i)

            stream("qb", w_ab, IN_AB_B, 2, 8)
            stream("qa", w_ab, 0, 2, 10)
            for n in range(2):
                for q in range(4):
                    load(UNIT["y0"] + 4 * n + q, q % 2, cols(w_oab, 4 * (q ^ 2), 4, 512 * n))
            for G in range(4):
                u = UNIT["mix"] + 5 * G
                load(u, u % 2, cols(w_c, 0, 4, 512 * G))
                load(u + 1, (u + 1) % 2, cols(w_c, 4, 4, 512 * G))
                load(u + 2, u % 2, cols(w_c, 0, 4, 2048 + 512 * G))
                load(u + 3, (u + 1) % 2, cols(w_c, 4, 4, 2048 + 512 * G))
                load(u + 4, u % 2, w_pool[G].rearrange("(k p) n -> p k n", p=P))
            stream("y1", w_oc, 0, 4, 2)
            stream("wq", w_2, C2["qa"], 2, 1)
            for q in range(2):
                load(UNIT["wkv"] + q, q, cols(w_2, 4 * q, 4, C2["kv"], 256), width=256)
            stream("gq", w_2, C2["gq"], 2, 1)
            stream("gk", w_2, C2["gk"], 2, 1)
            stream("gv", w_2, C2["gv"], 2, 4)
            stream("ga", w_2, C2["ga"], 2, 4)
            stream("bra", w_ba, 0, 1, 1)
            load(UNIT["bra"] + 1, 1, cols(w_ba, 0, 4, 512))
            stream("brb", w_bb, 0, 2, 2)
            stream("y2", w_o2, 0, 2, 2)
            with sp.Fori(0, FI) as i:
                for q in range(2):
                    u = UNIT["ffn"] + 2 * i + q
                    load(u, q, w_fi[:, 4 * q:4 * q + 4, bass.ds(i * 256, 256)], width=256, inc=16)
                    sp.dma_start(raw[q][:, :, 256:512], w_fi[:, 4 * q:4 * q + 4, bass.ds(DFF + i * 256, 256)])\
                        .then_inc(raw_full[q], 16)
            for n in range(2):
                for q in range(6):
                    nk = min(4, FC - 4 * q)
                    load(UNIT["y3"] + 6 * n + q, q % 2, cols(w_fo, 4 * q, nk, 512 * n), nk=nk)
            for n in range(2):
                for t in range(NT):
                    sp.wait_ge(bank_free[t], GROUP["y3"] + n + 1)
                    sp.dma_start(out[0, t * P:(t + 1) * P, n * 512:(n + 1) * 512],
                                 x[:, t, n * 512:(n + 1) * 512]).then_inc(stored, 16)
            sp.wait_ge(stored, 16 * 2 * NT)

        @block.gpsimd
        def _(pool):
            line = Line(pool, pool_line)

            def select(view, pattern, base, channel, compare=ALU.is_ge, fill=0.0):
                line.step(pool.affine_select(out=view, in_=view, pattern=pattern, base=base,
                                             channel_multiplier=channel, compare_op=compare, fill=fill))

            line.step(pool.memset(ident[:], 0.0))
            select(ident[:], [[-1, P]], 0, 1, ALU.not_equal, 1.0)
            line.step(pool.memset(sel[:], 0.0))
            pool.affine_select(out=sel[:], in_=sel[:], pattern=[[-1, HA], [0, P]], base=0, channel_multiplier=1,
                               compare_op=ALU.not_equal, fill=1.0).then_inc(const_made, 1)

            def split(u, slot, first=False):
                pool.wait_ge(raw_full[slot], (u // 2) * 32 + 32 if isinstance(u, int) else (u[0]) * 32 + 32)
                n = u if isinstance(u, int) else 2 * u[0] + u[1]
                if not first:
                    pool.wait_ge(steps, 4 * (n - 1))
                    pool.sem_inc(unit_taken, 1)
                pool.tensor_scalar(whi[slot][:], raw[slot][:], 1.0, 0.0, ALU.mult, ALU.add).then_inc(hi_made, 1)
                pool.wait_ge(hi_made, n + 1)
                pool.tensor_tensor(wlo[slot][:], raw[slot][:], whi[slot][:].bitcast(F32), ALU.subtract)\
                    .then_inc(split_ready, 1)

            split(0, 0, first=True)
            split(1, 1, first=True)
            line.step(pool.memset(tri[:], 1.0))
            select(tri[:], [[1, P]], 0, -1)
            line.step(pool.memset(below[:], 1.0))
            select(below[:], [[-1, P]], -1, 1)
            line.step(pool.memset(band[:], 0.0))
            select(band[:, 0:P], [[1, P]], -1, -1, fill=-1e30)
            select(band[:, P:], [[-1, P]], 0, 1, fill=-1e30)
            line.step(pool.memset(level[:], 0.0))
            for n, L in enumerate(LEVELS):
                v = level[:, n, :].rearrange("p (a two l) -> p a two l", two=2, l=L)[:, :, 1, :]
                line.step(pool.memset(v, 1.0))
                select(v, [[-2 * L, P // (2 * L)], [0, L]], 0, 1)
                select(v, [[2 * L, P // (2 * L)], [0, L]], L - 1, -1)
            pool.memset(spare[:, 0:4], 1.0).then_inc(const_made, 1)
            with pool.Fori(1, UNITS // 2) as i:
                split((i, 0), 0)
                split((i, 1), 1)

        @block.scalar
        def _(act):
            line = Line(act, act_line)
            stats = [0]

            def fn(out_, in_, f, **kw):
                return act.activation(out_, in_, f, **kw)

            def copy(out_, in_, **kw):
                return act.activation(out_, in_, ACT.Copy, **kw)

            def root(width):
                stats[0] += 1
                act.wait_ge(var_ready, stats[0])
                line.tell(fn(std[:, 0:width], var[:, 0:width], ACT.Sqrt), std_ready, stats[0])

            squares = [0]

            def square(in_, col_, last, width=D, junk=junk):
                squares[0] += 1
                line.tell(fn(junk[:, 0:width], in_, ACT.Square, accum_out=ss[:, col_:col_ + 1]), ss_ready, squares[0])

            def turn_hi(name, dst, c0, gname):
                T = TURNS[name]
                for c in range(KC):
                    act.wait_ge(turned_pe, 8 * T + c + 1)
                    line.tell(copy(dst[:, c0 + c], ps[:, c], scale=gname(c)), turned_hi, 8 * T + c + 1)

            def prenorm():
                for t in range(NT):
                    square(x[:, t], 0, True)
                    root(1)

            vec_rows = [(A["pre_norm_g"].rearrange("a (r p) -> (a r) p", p=P), 16),
                        (rows(A["ln_mix_g_2"][0], 8), 8), (rows(A["ln_ffn_g_2"][0], 8), 8),
                        (A["conv_qk"][0].rearrange("w (r p) -> (w r) p", p=P), 64),
                        (rows(A["pool_scale"][0], 16), 16), (rows(A["b_gk_2"][0], 4), 4),
                        (rows(A["head_norm_g"][0], 8), 8)]
            r = 0
            for src, n in vec_rows:
                act.dma_start(rawv[r:r + n, 0, :], src).then_inc(small_in, 16)
                r += n
            for g in ("q_norm_g_2", "k_norm_g_2"):
                for half in range(2):
                    act.dma_start(rawv[r:r + 1, 0, DH * half:DH * half + DH], A[g]).then_inc(small_in, 16)
                r += 1
            act.dma_start(rawv[r:r + 2, 0, :], rows(A["gla_norm_g_2"][0], 2)).then_inc(small_in, 16)
            act.dma_start(rawv[0:66, 1, :], A["conv_w_2"][0].rearrange("w (r p) -> (w r) p", p=P)).then_inc(small_in, 16)
            act.dma_start(rawv[66:88, 1, :], rows(A["conv_b_2"][0], 22)).then_inc(small_in, 16)
            act.dma_start(sinkb, A["sinks_2"][0].partition_broadcast(P)).then_inc(small_in, 16)
            act.dma_start(wgate[:], cols(w_ab, 0, KC, 5 * D, 2 * HA)).then_inc(small_in, 16)
            for n, b in enumerate(("bias_i", "bias_f")):
                act.dma_start(bias4[:, n:n + 1], A[b].rearrange("a h -> h a")).then_inc(small_in, 16)

            for t in range(NT):
                act.wait_ge(x_in[t], 16)
                square(x[:, t], 0, True)
                root(1)
            act.wait_ge(vcol_ready, 1)
            turn_hi("turn0", h_hi, 0, lambda c: col("pre", c))

            for name, dst, f, sc in (("qb", qB, ACT.Copy, DB ** -0.5), ("kb", kB, ACT.Copy, 1.0),
                                     ("vb", vB, ACT.Copy, 1.0), ("zb", szB, ACT.Silu, 1.0)):
                for n in range(2):
                    u, g = UNIT[name] + 2 * n + 1, GROUP[name] + n
                    for j in range(4):
                        act.wait_ge(steps, 4 * u + j + 1)
                        o = vB[:, j, n * 512:n * 512 + 512] if name == "vb" else dst[:, 4 * n + j]
                        line.tell(fn(o, ps[:, j], f, scale=sc), bank_free[j], g + 1)
                if name == "qb":
                    act.wait_ge(gate_dve, 3)
                    line.tell(fn(g_t[:], g_lf[:], ACT.Abs), gate_act, 1)
                    line.tell(fn(g_t[:], g_t[:], ACT.Exp, scale=-1.0), gate_act, 2)
                    line.tell(fn(g_t[:], g_t[:], ACT.Ln, bias=1.0), gate_act, 3)
                elif name == "kb":
                    act.wait_ge(gate_dve, 8)
                    line.tell(fn(g_t[:], g_m[:], ACT.Exp, scale=-1.0), gate_act, 4)

            def qk_silu(c):
                act.wait_ge(bank_free[c % 4], GROUP["qa"] + c // 4 + 1)
                dst = (qA if c < 8 else kA)[:, c % 8]
                line.tell(fn(dst, dst, ACT.Silu), qk_ready, c + 1)

            zps = psf[:, 2048:2048 + CAUSAL]
            for h in range(HB):
                act.wait_ge(b_z, h + 1)
                line.tell(fn(tB1[:], zps, ACT.Sigmoid, scale=-1.0), b_rest, h + 1)
                line.tell(fn(tB2[:], zps, ACT.Sigmoid), b_beta, h + 1)
                act.wait_ge(b_t, h + 1)
                line.tell(copy(aTB[:], zps), b_copied, h + 1)
                if h % 2:
                    for j in range(3):
                        qk_silu(2 * (h - 1) + j)
                act.wait_ge(b_y, h + 1)
                line.tell(copy(yB_hi[:, h], y32[:]), b_hi, h + 1)
                if h % 2:
                    qk_silu(2 * (h - 1) + 3)
            for name, dst, f in (("va", vA, ACT.Copy), ("oa", soA, ACT.Sigmoid), ("za", szA, ACT.Silu)):
                for n in range(2):
                    u, g = UNIT[name] + 2 * n + 1, GROUP[name] + n
                    for j in range(4):
                        act.wait_ge(steps, 4 * u + j + 1)
                        if name == "va":
                            o = vA[:, j, 2 * n:2 * n + 2, 0:DA]
                            i = ps[:, j].rearrange("p (h d) -> p h d", d=DA)
                        else:
                            o, i = dst[:, j, n * 512:n * 512 + 512], ps[:, j]
                        line.tell(fn(o, i, f), bank_free[j], g + 1)
            act.wait_ge(gate_pe, 8)
            line.tell(copy(nMb[:, 0:HA], ps[:, 4:8]), gate_act, 5)
            act.dma_start(postg[:], A["post_norm_g"][0].partition_broadcast(P)).then_inc(postg_in, 16)

            def a_weights(h):
                for j in range(NT):
                    act.wait_ge(a_arg, 4 * h + j + 1)
                    w = WA[h % 2][:, A_OFF[j]:A_OFF[j] + S - P * j]
                    line.tell(fn(w, w, ACT.Exp), a_exp, 4 * h + j + 1)

            def a_squares(h):
                for t in range(NT):
                    act.wait_ge(bank_free[t], GROUP["a_out"] + h + 1)
                    square(soA[:, t, h * DA:h * DA + DA], 4 * h + t, True, width=DA, junk=junkA)

            a_weights(0)
            a_weights(1)
            for h in range(HA):
                a_squares(h)
                if h + 2 < HA:
                    a_weights(h + 2)
            root(16)
            for c in range(KC):
                act.wait_ge(a_turned, c + 1)
                line.tell(copy(yA_hi[:, c], ps[:, 4 + c % 4], scale=col("hn", c)), a_hi, c + 1)
            act.wait_ge(a_src, NT)
            for t in range(NT):
                act.dma_start(x[:, t], A["x"][0, t * P:(t + 1) * P, :]).then_inc(x_in[t], 16)

            def y_post(name):
                u, per = UNIT[name], 4
                for t in range(NT):
                    act.wait_ge(steps, 4 * (u + per - 1) + t + 1)
                    square(ps[:, t], t, True, width=512)
                for t in range(NT):
                    act.wait_ge(steps, 4 * (u + 2 * per - 1) + t + 1)
                    square(ps[:, t], 4 + t, True, width=512)
                    root(1)
                    act.wait_ge(x_ready, NT * (1 if name == "y0" else 2) - NT + t + 1)
                    square(x[:, t], 0, True)
                    root(1)

            y_post("y0")
            act.wait_ge(x_ready, NT)
            act.dma_start(postg[:], A["post_norm_g"][1].partition_broadcast(P)).then_inc(postg_in, 16)
            turn_hi("turn2", h_hi, 0, lambda c: col("pre", 8 + c))

            for G in range(4):
                u, g = UNIT["mix"] + 5 * G, GROUP["mix"] + 3 * G
                for j in range(4):
                    n = 4 * G + j
                    act.wait_ge(steps, 4 * (u + 1) + j + 1)
                    if n >= 1:
                        act.wait_ge(p_out, n)
                    line.tell(copy(pw[0][:, PAD:], ps[:, j]), bank_free[j], g + 1)
                    act.wait_ge(pool_ready, 2 * n + 1)
                    line.tell(copy(pool_hi[:, j], y32[:]), pool_h, n + 1)
                for j in range(4):
                    act.wait_ge(steps, 4 * (u + 3) + j + 1)
                    line.tell(fn(szC[:, j], ps[:, j], ACT.Silu), bank_free[j], g + 2)
                for j in range(4):
                    n = 4 * G + j
                    act.wait_ge(bank_free[j], g + 3)
                    line.tell(copy(m_hi[:, n], szC[:, j]), m_hi_done, n + 1)
            y_post("y1")
            act.dma_start(wlr[:], cols(w_2, 0, KC, C2["lr"], RANK)).then_inc(lr_in, 16)
            act.dma_start(wup[:], A["w_gk_up_2"][0]).then_inc(lr_in, 16)
            turn_hi("turn3", h_hi, 0, lambda c: col("lnmix", c))

            for name, c0, w in (("wq", 0, 512), ("wkv", 512, 256)):
                u, g = UNIT[name] + 1, GROUP[name]
                for j in range(4):
                    act.wait_ge(steps, 4 * u + j + 1)
                    line.tell(copy(qkv[:, j, c0:c0 + w], ps[:, j, 0:w]), bank_free[j], g + 1)
            for t in range(NT):
                if t:
                    act.wait_ge(w_sq, t)
                line.tell(fn(junk2[:], qkv[:, t, 0:640], ACT.Square), w_qkv, t + 1)
            root(40)
            for name, dst, sc in (("gq", qG, DK ** -0.5), ("gk", kG, 1.0)):
                u, g = UNIT[name] + 1, GROUP[name]
                for j in range(4):
                    act.wait_ge(steps, 4 * u + j + 1)
                    line.tell(copy(dst[:, j], ps[:, j], scale=sc), bank_free[j], g + 1)
                if name == "gq":
                    for b in range(5):
                        act.wait_ge(w_tp, b + 1)
                        line.tell(copy(qkT[:, b], ps[:, 4 + b % 4], scale=col("qn" if b < 4 else "kn")), w_qk, b + 1)
            for h in range(HG):
                act.wait_ge(l_dve, 2 + h + 1 + h)
                b = gtmp[h % 2]
                line.step(fn(dG[1][:], b[:], ACT.Abs))
                line.step(fn(dG[1][:], dG[1][:], ACT.Exp, scale=-1.0))
                line.tell(fn(dG[1][:], dG[1][:], ACT.Ln, bias=1.0), l_act, h + 1)
                act.wait_ge(l_dve, 2 + 2 * (h + 1))
            for i in range(NT):
                k0 = P if i == 0 else 0
                act.wait_ge(w_neg, i + 1)
                for h in range(HQ):
                    n = 9 * i + h + 1
                    line.tell(fn(sm[:, h, k0:], sm[:, h, k0:], ACT.Exp, bias=wstat[:, 1, h:h + 1],
                                 accum_out=wstat[:, 2, h:h + 1]), w_exp, n)
                line.tell(fn(wstat[:, 3], wstat[:, 3], ACT.Exp), w_exp, 9 * i + 9)
                act.wait_ge(w_t, i + 1)
                for b in range(4):
                    line.tell(copy(pT[:, b // 2, b % 2].rearrange("p b q -> p (b q)"), ps[:, b]),
                              bank_free[b], GROUP["w_out"] + i + 1)
                act.wait_ge(w_o, i + 1)
                for c in range(HKV):
                    o = ps[0:DH, 4 + c].rearrange("p (b two q) -> p b two q", two=2, q=P)
                    for odd in range(2):
                        line.tell(copy(ya32[DH * odd:DH * odd + DH, 2 * c:2 * c + 2, i * P:i * P + P],
                                       o[:, :, odd, :]), w_ya, 4 * i + 2 * c + odd + 1)
            def evacuate(name, n, j):
                act.wait_ge(steps, 4 * (UNIT[name] + 2 * n + 1) + j + 1)
                if name == "gv":
                    ins = copy(vG[:, j, n * 512:n * 512 + 512], ps[:, j])
                else:
                    ins = fn(rG[:, j, n * 512:n * 512 + 512], ps[:, j], ACT.Silu)
                line.tell(ins, bank_free[j], GROUP[name] + n + 1)

            def decay(s):
                act.wait_ge(e_d, s + 1)
                line.step(fn(dG[s % 2][:], dG[s % 2][:], ACT.Abs))
                line.tell(fn(dG[s % 2][:], dG[s % 2][:], ACT.Exp, scale=-1.0 / GATE), e_exp, s + 1)

            gla_schedule(evacuate, decay)
            for h in range(HG):
                s = FAR + 2 * h
                d = dG[0][:].rearrange("p (b t) -> p b t", t=P)
                bb = bG[:, h].rearrange("p (b t) -> p b t", t=P)
                act.wait_ge(e_qk, s)
                act.wait_ge(l_dve, 12)
                line.step(fn(d[:, 0:2], bb[:, 1::2], ACT.Exp, scale=1.0 / GATE))
                line.step(fn(d[:, 2], bb[:, 2], ACT.Exp, scale=1.0 / GATE))
                line.tell(fn(d[:, 3], bb[:, 3], ACT.Exp, scale=1.0 / GATE, bias=bend[:, 0, h, 2:3]), e_exp, s + 1)
                d = dG[1][:].rearrange("p (b t) -> p b t", t=P)
                line.step(fn(d[:, 0], bb[:, 0], ACT.Exp, scale=-1.0 / GATE, bias=bend[:, 0, h, 0:1]))
                line.step(fn(d[:, 1], bb[:, 2], ACT.Exp, scale=-1.0 / GATE, bias=bend[:, 0, h, 2:3]))
                line.step(fn(d[:, 2], bb[:, 0], ACT.Exp, scale=-1.0 / GATE, bias=bend[:, 1, h, 0:1]))
                line.tell(fn(d[:, 3], bb[:, 1], ACT.Exp, scale=-1.0 / GATE, bias=bend[:, 0, h, 1:2]), e_exp, s + 2)
            act.wait_ge(e_qk, FAR + 2 * HG)

            def gate_out(name, dst):
                for n in range(2):
                    u, g = UNIT[name] + 2 * n + 1, GROUP[name] + n
                    for j in range(4):
                        act.wait_ge(steps, 4 * u + j + 1)
                        line.tell(fn(dst[:, 4 * n + j], ps[:, j], ACT.Sigmoid), bank_free[j], g + 1)
            gate_out("ga", sga)
            for h in range(HG):
                act.wait_ge(g_o, 4 * h + 4)
                for t in range(NT):
                    square(ps[:, t, 0:DV], t, True, width=DV)
                root(4)
            gate_out("gb", sgb)
            turn_hi("turn4", h_hi, 0, lambda c: col("gla", c % 2))
            for c in range(4):
                act.wait_ge(w_ya, 4 * NT)
                line.tell(copy(ya_hi[:, c], ya32[:, c]), c_hi, c + 1)
            for c in range(KC):
                act.wait_ge(c_y, c + 1)
                line.tell(copy(mg_hi[:, c], y32[:]), c_hi, 4 + c + 1)
            for t in range(NT):
                act.wait_ge(bank_free[t], GROUP["y2"] + 2)
                square(x[:, t], 0, True)
                root(1)
            turn_hi("turn5", h_hi, 0, lambda c: col("lnffn", c))
            with act.Fori(0, FI) as i:
                for j in range(2):
                    act.wait_ge(f_acc, 2 * i + j + 1)
                    line.tell(fn(facc[j][:], facc[j][:], ACT.Silu), f_silu, 2 * i + j + 1)
                for j in range(2):
                    act.wait_ge(bank_free[2 + j], GROUP["ffn"] + i + 1)
                    line.tell(copy(f_hi[:, bass.ds(2 * i + j, 1)], facc[j][:].unsqueeze(1)), f_hi_done, 2 * i + j + 1)

        @block.vector
        def _(dve):
            line = Line(dve, dve_line)
            seen = {"ss": 0, "root": 0, "src": 0}

            def tt(o, a, b, op):
                return dve.tensor_tensor(o, a, b, op)

            def stt(o, a, sc, b, op0, op1):
                return dve.scalar_tensor_tensor(o, a, sc, b, op0, op1)

            def squared(n=1):
                seen["ss"] += n
                dve.wait_ge(ss_ready, seen["ss"])

            def deviation(width, over, extra=None):
                r = seen["root"] = seen["root"] + 1
                a = slice(0, width)
                if extra is not None:
                    line.step(tt(var[:, a], ss[:, extra[0]:extra[0] + 1], ss[:, extra[1]:extra[1] + 1], ALU.add))
                    src = var[:, a]
                else:
                    src = ss[:, a]
                line.tell(dve.tensor_scalar(var[:, a], src, 1.0 / over, EPS, ALU.mult, ALU.add), var_ready, r)
                dve.wait_ge(std_ready, r)
                line.step(dve.reciprocal(rs[:, a], std[:, a]))
                line.step(tt(nwt[:, a], rs[:, a], rs[:, a], ALU.mult))
                line.step(tt(nwt[:, a], nwt[:, a], var[:, a], ALU.mult))
                line.step(dve.tensor_scalar(nwt[:, a], nwt[:, a], -0.5, 1.5, ALU.mult, ALU.add))
                line.step(tt(rs[:, a], rs[:, a], nwt[:, a], ALU.mult))

            def src_done(ins):
                seen["src"] += 1
                line.tell(ins, src_ready, seen["src"])

            def turn_lo(name, dst, hi, c0, gname):
                T = TURNS[name]
                for c in range(KC):
                    dve.wait_ge(turned_hi, 8 * T + c + 1)
                    ins = stt(dst[:, c0 + c], ps[:, c], gname(c), hi[:, c0 + c].bitcast(F32), ALU.mult, ALU.subtract)
                    if c < 4:
                        line.tell(ins, bank_free[c], GROUP[name] + 1)
                    else:
                        line.tell(ins, turned_lo, 4 * T + c - 3)

            def normed(t, xn=xn):
                squared()
                deviation(1, D)
                src_done(dve.tensor_scalar(xn[:, t], x[:, t], rs[:, 0:1], None, ALU.mult))

            for c in range(16):
                line.step(dve.memset(invc[:, c:c + 1], 1.0 / (c + 1)))
            dve.wait_ge(vt_done, 2)
            line.step(dve.tensor_copy(vcol[:, 0:NV1], ps[:, 4, 0:NV1]))
            line.tell(dve.tensor_copy(vcol[:, NV1:], ps[:, 5, 0:NV2]), vcol_ready, 1)

            for t in range(NT):
                normed(t)
            turn_lo("turn0", h_lo, h_hi, 0, lambda c: col("pre", c))

            dve.wait_ge(gate_pe, 1)
            line.tell(dve.tensor_copy(gtok[:].rearrange("p t h -> p (t h)"), ps[:, 4, 0:NT * 2 * HA]), gate_dve, 1)
            dve.wait_ge(gate_pe, 2)
            line.tell(dve.tensor_scalar(g_ig[:], ps[0:HA, 5], bias4[:, 0:1], None, ALU.add), gate_dve, 2)
            line.tell(dve.tensor_scalar(g_lf[:], ps[0:HA, 6], bias4[:, 1:2], None, ALU.add), gate_dve, 3)
            dve.wait_ge(gate_act, 3)
            line.tell(stt(g_lf[:], g_lf[:], 0.0, g_t[:], ALU.min, ALU.subtract), gate_dve, 4)
            line.tell(dve.tensor_tensor_scan(g_b[:], g_lf[:], g_lf[:], 0.0, ALU.add, ALU.bypass), gate_dve, 5)
            line.tell(tt(g_ig[:], g_ig[:], g_b[:], ALU.subtract), gate_dve, 6)
            line.tell(dve.tensor_tensor_scan(g_lf[:], g_ig[:], g_ig[:], 0.0, ALU.max, ALU.bypass), gate_dve, 7)
            line.tell(tt(g_m[:], g_b[:], g_lf[:], ALU.add), gate_dve, 8)
            line.tell(dve.tensor_scalar(g_lf[:], g_lf[:], -1.0, None, ALU.mult), gate_dve, 9)
            dve.wait_ge(gate_pe, 3)
            line.tell(dve.tensor_copy(small[:, 216:232], ps[:, 4, 0:NT * HA]), gate_dve, 10)
            dve.wait_ge(gate_pe, 4)
            line.tell(dve.tensor_copy(small[:, 232:248], ps[:, 5, 0:NT * HA]), gate_dve, 11)

            def convolve(c):
                u, g = UNIT["qa"] + 2 * (c // 4) + 1, GROUP["qa"] + c // 4
                acc, p = (qA if c < 8 else kA)[:, c % 8], ps[:, c % 4]
                dve.wait_ge(steps, 4 * u + c % 4 + 1)
                line.step(dve.tensor_scalar(acc, p, col("convqk", 48 + c), None, ALU.mult))
                for sft in (1, 2, 3):
                    ins = stt(acc[:, sft:], p[:, 0:S - sft], col("convqk", 16 * (3 - sft) + c), acc[:, sft:],
                              ALU.mult, ALU.add)
                    if sft < 3:
                        line.step(ins)
                    else:
                        line.tell(ins, bank_free[c % 4], g + 1)

            def diagonals(t_):
                return (t_[:, SEG_T[0]:SEG_T[0] + P].unsqueeze(1),
                        t_[:, P:].rearrange("p (n c) -> p n c", c=3 * P)[:, :, 2 * P:])

            dve.wait_ge(const_made, 2)
            for h in range(HB):
                dve.wait_ge(b_rest, h + 1)
                for v in diagonals(tB1):
                    line.step(tt(v, v, tri[:].unsqueeze(1).broadcast_to([P, v.shape[1], P]), ALU.max))
                for i in range(NT):
                    r = tB1[:, SEG_T[i]:SEG_T[i] + P * (i + 1)][:, ::-1]
                    line.step(dve.tensor_tensor_scan(r, r, r, 1.0, ALU.mult, ALU.bypass))
                dve.wait_ge(b_beta, h + 1)
                line.step(tt(tB2[:, 0:CAUSAL - 1], tB2[:, 0:CAUSAL - 1], tB1[:, 1:CAUSAL], ALU.mult))
                one, three = diagonals(tB2)
                line.step(tt(one, one, below[:].unsqueeze(1), ALU.mult))
                line.tell(tt(three, three, below[:].unsqueeze(1).broadcast_to([P, 3, P]), ALU.mult), b_a, h + 1)
                if h % 2:
                    for j in range(3):
                        convolve(2 * (h - 1) + j)
                dve.wait_ge(b_o, h + 1)
                line.tell(tt(y32[:], ps[:, 7], szB[:, h], ALU.mult), b_y, h + 1)
                if h % 2:
                    convolve(2 * (h - 1) + 3)
                dve.wait_ge(b_hi, h + 1)
                line.tell(tt(yB_lo[:, h], y32[:], yB_hi[:, h].bitcast(F32), ALU.subtract), b_lo, h + 1)
            line.step(dve.memset(vA[:, :, :, DA:DA + 1], 1.0))

            def a_args(h):
                if h >= 2:
                    dve.wait_ge(a_o, 4 * (h - 1))
                for j in range(NT):
                    w = WA[h % 2][:, A_OFF[j]:A_OFF[j] + S - P * j]
                    line.tell(dve.tensor_scalar(w, nMb[:, h, P * j:], cT[:, j, h:h + 1], 0.0, ALU.add, ALU.min),
                              a_arg, 4 * h + j + 1)

            def a_scores(h):
                for j in range(NT):
                    dve.wait_ge(a_exp, 4 * h + j + 1)
                    w = WA[h % 2][:, A_OFF[j]:A_OFF[j] + S - P * j]
                    line.step(tt(w[:, 0:P], w[:, 0:P], tri[:], ALU.mult))
                    dve.wait_ge(a_s, 4 * h + j + 1)
                    line.tell(stt(w, ps[:, 4 + j, 0:S - P * j], DA ** -0.5, w, ALU.mult, ALU.mult),
                              a_st, 4 * h + j + 1)

            def a_outputs(h):
                dve.wait_ge(a_o, 4 * h + 4)
                line.step(dve.tensor_copy(den, ps[:, 0:4, DA]))
                line.step(stt(rden, den, -1.0, den, ALU.mult, ALU.max))
                line.step(tt(rden, rden, emT[:, :, h], ALU.max))
                line.step(dve.reciprocal(rden, rden))
                for t in range(NT):
                    so = soA[:, t, h * DA:h * DA + DA]
                    line.tell(stt(so, ps[:, t, 0:DA], rden[:, t:t + 1], so, ALU.mult, ALU.mult), bank_free[t],
                              GROUP["a_out"] + h + 1)

            dve.wait_ge(gate_act, 5)
            a_args(0)
            a_args(1)
            a_scores(0)
            for h in range(HA):
                if h + 1 < HA:
                    a_scores(h + 1)
                a_outputs(h)
                if h + 2 < HA:
                    a_args(h + 2)
            squared(16)
            deviation(16, DA)
            for t in range(NT):
                for h in range(HA):
                    so = soA[:, t, h * DA:h * DA + DA]
                    ins = stt(so, so, rs[:, 4 * h + t:4 * h + t + 1], szA[:, t, h * DA:h * DA + DA], ALU.mult, ALU.mult)
                    if h < HA - 1:
                        line.step(ins)
                    else:
                        line.tell(ins, a_src, t + 1)
            for c in range(KC):
                dve.wait_ge(a_hi, c + 1)
                line.tell(stt(yA_lo[:, c], ps[:, 4 + c % 4], col("hn", c), yA_hi[:, c].bitcast(F32), ALU.mult,
                              ALU.subtract), a_lo, c + 1)

            def y_post(name, yh, tmp, posts, then):
                u, g, per = UNIT[name], GROUP[name], 4
                for t in range(NT):
                    squared()
                    line.tell(dve.tensor_copy(yh[:, t], ps[:, t]), bank_free[t], g + 1)
                dve.wait_ge(postg_in, 16 * posts)
                for t in range(NT):
                    squared()
                    deviation(1, D, extra=(t, 4 + t))
                    line.step(stt(tmp[:, 512:], ps[:, t], rs[:, 0:1], postg[:, 512:], ALU.mult, ALU.mult))
                    line.tell(stt(tmp[:, 0:512], yh[:, t], rs[:, 0:1], postg[:, 0:512], ALU.mult, ALU.mult),
                              bank_free[t], g + 2)
                    dve.wait_ge(x_in[t], 32)
                    line.tell(tt(x[:, t], x[:, t], tmp[:], ALU.add), x_ready, NT * (posts - 1) + t + 1)
                    normed(t, xn2 if name == "y0" else xn)
                turn_lo(then[0], h_lo, h_hi, 0, then[1])

            y_post("y0", y_half, ytmp, 1, ("turn2", lambda c: col("pre", 8 + c)))

            for b in range(3):
                line.step(dve.memset(pw[b][:, 0:PAD], 0.0))
            for G in range(4):
                w, u, g = WINDOWS[G], UNIT["mix"] + 5 * G, GROUP["mix"] + 3 * G
                for j in range(4):
                    n = 4 * G + j
                    dve.wait_ge(bank_free[j], g + 1)
                    src = 0
                    for k in range(G + 1):
                        dst = 1 + k % 2
                        line.step(tt(pw[dst][:, PAD:], pw[src][:, PAD:], pw[src][:, PAD - (1 << k):PAD - (1 << k) + S],
                                     ALU.add))
                        src = dst
                    if n:
                        dve.wait_ge(pool_h, n)
                    line.step(tt(pw[3 - src][:, PAD:PAD + w], pw[src][:, PAD:PAD + w], invc[:, 0:w], ALU.mult))
                    line.step(stt(y32[:], pw[src][:, PAD:], 1.0 / w, pw[0][:, PAD:], ALU.mult, ALU.subtract))
                    line.tell(tt(y32[:, 0:w], pw[3 - src][:, PAD:PAD + w], pw[0][:, PAD:PAD + w], ALU.subtract),
                              pool_ready, 2 * n + 1)
                    dve.wait_ge(pool_h, n + 1)
                    line.tell(tt(pool_lo[:, j], y32[:], pool_hi[:, j].bitcast(F32), ALU.subtract), pool_ready, 2 * n + 2)
                    line.tell(dve.memset(pw[0][:, 0:1], 0.0), p_out, n + 1)
                for j in range(4):
                    n = 4 * G + j
                    dve.wait_ge(steps, 4 * (u + 4) + j + 1)
                    dve.wait_ge(bank_free[j], g + 2)
                    line.tell(stt(szC[:, j], ps[:, j], col("pscale", n), szC[:, j], ALU.mult, ALU.mult),
                              bank_free[j], g + 3)
                    dve.wait_ge(m_hi_done, n + 1)
                    line.tell(tt(m_lo[:, n], szC[:, j], m_hi[:, n].bitcast(F32), ALU.subtract), m_lo_done, n + 1)
            y_post("y1", y_half1, ytmp1, 2, ("turn3", lambda c: col("lnmix", c)))

            for t in range(NT):
                dve.wait_ge(w_qkv, t + 1)
                line.tell(dve.tensor_reduce(ss[:, 10 * t:10 * t + 10], junk2[:].rearrange("p (h d) -> p h d", d=DH),
                                            AX, ALU.add), w_sq, t + 1)
            deviation(40, DH)
            for t in range(NT):
                r = rs[:, 10 * t:10 * t + 10]
                for c in range(HKV):
                    line.step(tt(
                        qn[:, t, 0:512].rearrange("p (b c d) -> p b c d", c=HKV, d=DH)[:, :, c, :],
                        qkv[:, t, 256 * c:256 * c + 256].rearrange("p (b d) -> p b d", d=DH),
                        r[:, 4 * c:4 * c + 4].unsqueeze(2).broadcast_to([P, 4, DH]), ALU.mult))
                line.tell(tt(qn[:, t, 512:640].rearrange("p (c d) -> p c d", d=DH),
                             qkv[:, t, 512:640].rearrange("p (c d) -> p c d", d=DH),
                             r[:, 8:10].unsqueeze(2).broadcast_to([P, HKV, DH]), ALU.mult), w_n, t + 1)
            line.step(dve.memset(notfirst[:], 1.0))
            line.step(dve.memset(notfirst[:].rearrange("p (b t) -> p b t", t=P)[:, :, 0:1], 0.0))
            dve.wait_ge(l_pe, 1)
            line.tell(dve.tensor_copy(lrtok[:].rearrange("p t r -> p (t r)"), ps[:, 4, 0:NT * RANK]), l_dve, 1)
            dve.wait_ge(l_pe, 2)
            line.tell(dve.tensor_copy(lrT[:], ps[0:RANK, 5]), l_dve, 2)
            for h in range(HG):
                dve.wait_ge(l_pe, 3 + h)
                gt = gtmp[h % 2]
                line.tell(dve.tensor_scalar(gt[:], ps[:, 4 + h], col("bgk", h), None, ALU.add), l_dve, 3 + 2 * h)
                dve.wait_ge(l_act, h + 1)
                line.tell(stt(gt[:], gt[:], 0.0, dG[1][:], ALU.min, ALU.subtract), l_dve, 4 + 2 * h)
                line.step(dve.tensor_tensor_scan(bG[:, h], notfirst[:], gt[:], 0.0, ALU.mult, ALU.add))
            line.tell(dve.tensor_scalar(bend[:, 0], bG[:].rearrange("p h (b t) -> p h b t", t=P)[:, :, :, P - 1],
                                        1.0 / GATE, None, ALU.mult), l_dve, 11)
            line.tell(tt(bend[:, 1, :, 0:1], bend[:, 0, :, 0:1], bend[:, 0, :, 1:2], ALU.add), l_dve, 12)
            sc4 = psf[:, 2048:4096].rearrange("p (h k) -> p h k", k=2 * P)
            for i in range(NT):
                k0 = P if i == 0 else 0
                nk = 2 * P - k0
                dve.wait_ge(w_s, i + 1)
                if i:
                    dve.wait_ge(w_t, i)
                s_ = sm[:, :, k0:]
                if i == 0:
                    line.step(dve.memset(sm[:, :, 0:P], 0.0))
                line.tell(stt(s_, sc4[:, :, k0:], DH ** -0.5, band[:, k0:].unsqueeze(1).broadcast_to([P, HQ, nk]), ALU.mult, ALU.add),
                          w_sm, i + 1)
                line.step(dve.tensor_reduce(wstat[:, 0], s_, AX, ALU.max))
                line.step(tt(wstat[:, 0], wstat[:, 0], sinkb, ALU.max))
                line.step(tt(wstat[:, 3], sinkb, wstat[:, 0], ALU.subtract))
                line.tell(dve.tensor_scalar(wstat[:, 1], wstat[:, 0], -1.0, None, ALU.mult), w_neg, i + 1)
                dve.wait_ge(w_exp, 9 * i + 9)
                line.step(tt(wstat[:, 2], wstat[:, 2], wstat[:, 3], ALU.add))
                line.step(dve.reciprocal(wstat[:, 2], wstat[:, 2]))
                line.tell(tt(s_, s_, wstat[:, 2].unsqueeze(2).broadcast_to([P, HQ, nk]), ALU.mult), w_p, i + 1)

            for h in range(HG):
                dve.wait_ge(e_pe, h + 1)
                if h == 0:
                    dve.wait_ge(w_t, NT)
                line.tell(tt(atD[:, h], ps[:, 4 + h].rearrange("p (b t) -> p b t", t=P),
                             ident[:].unsqueeze(1).broadcast_to([P, 4, P]), ALU.mult), e_at, h + 1)
            for b in range(2):
                line.step(dve.memset(qE[b][:], 0.0))
                line.step(dve.memset(kE[b][:], 0.0))

            def pairs(v, L):
                return v.rearrange("p (a two l) -> p a two l", two=2, l=L)

            def distance(s):
                L, h = LEVELS[s // HG], s % HG
                v = bG[:, h].rearrange("p (a l) -> p a l", l=2 * L)
                line.tell(tt(dG[s % 2][:].rearrange("p (a l) -> p a l", l=2 * L), v,
                             v[:, :, L - 1:L].broadcast_to([P, S // (2 * L), 2 * L]), ALU.subtract), e_d, s + 1)

            def weighted(s):
                L, h = LEVELS[s // HG], s % HG
                dve.wait_ge(e_exp, s + 1)
                if s >= 2:
                    dve.wait_ge(e_pe, HG + s - 1)
                d = pairs(dG[s % 2][:], L)
                line.step(tt(pairs(qE[s % 2][:], L)[:, :, 1], pairs(qG[:, h], L)[:, :, 1], d[:, :, 1], ALU.mult))
                line.tell(tt(pairs(kE[s % 2][:], L)[:, :, 0], pairs(kG[:, h], L)[:, :, 0], d[:, :, 0], ALU.mult),
                          e_qk, s + 1)

            def take(s):
                n, h = s // HG, s % HG
                dve.wait_ge(e_pe, HG + s + 1)
                line.tell(dve.copy_predicated(atD[:, h], level[:, n].unsqueeze(1).broadcast_to([P, 4, P]).bitcast(I32),
                                              ps[:, 4 + s % 4].rearrange("p (b t) -> p b t", t=P)), e_at, HG + s + 1)

            for s in range(STEPS_NEAR + 2):
                if s < STEPS_NEAR:
                    distance(s)
                if 1 <= s <= STEPS_NEAR:
                    weighted(s - 1)
                if s >= 2:
                    take(s - 2)
            def blocks(v):
                return v.rearrange("p (b t) -> p b t", t=P)

            for h in range(HG):
                s, b = FAR + 2 * h, h % 2
                dve.wait_ge(e_exp, s + 1)
                dve.wait_ge(e_pe, HG + FAR + max(0, h - 1))
                line.step(tt(blocks(qE[b][:])[:, 0:2], blocks(qG[:, h])[:, 1::2], blocks(dG[0][:])[:, 0:2], ALU.mult))
                line.tell(tt(blocks(qE[b][:])[:, 2:4], blocks(qG[:, h])[:, 2:4], blocks(dG[0][:])[:, 2:4], ALU.mult),
                          e_qk, s + 1)
                dve.wait_ge(e_exp, s + 2)
                line.step(tt(blocks(kE[b][:])[:, 0:2], blocks(kG[:, h])[:, 0::2], blocks(dG[1][:])[:, 0:2], ALU.mult))
                line.tell(tt(blocks(kE[b][:])[:, 2:4], blocks(kG[:, h])[:, 0:2], blocks(dG[1][:])[:, 2:4], ALU.mult),
                          e_qk, s + 2)
                if h >= 1:
                    dve.wait_ge(e_pe, HG + FAR + h)
                    line.tell(dve.tensor_copy(atO[:, h - 1].rearrange("p b t -> p (b t)"),
                                              psf[:, 2048 + 1024 * ((h - 1) % 2):2048 + 1024 * ((h - 1) % 2) + 768]),
                              e_at, HG + FAR + h)
            dve.wait_ge(e_pe, HG + FAR + HG)
            line.tell(dve.tensor_copy(atO[:, HG - 1].rearrange("p b t -> p (b t)"),
                                      psf[:, 2048 + 1024:2048 + 1024 + 768]), e_at, HG + FAR + HG)
            for h in range(HG):
                squared(4)
                deviation(4, DV)
                for t in range(NT):
                    r_ = rG[:, t, h * DV:h * DV + DV]
                    line.tell(stt(r_, ps[:, t, 0:DV], rs[:, t:t + 1], r_, ALU.mult, ALU.mult), bank_free[t],
                              GROUP["g_out"] + h + 1)
            turn_lo("turn4", h_lo, h_hi, 0, lambda c: col("gla", c % 2))

            for c in range(4):
                dve.wait_ge(c_hi, c + 1)
                line.tell(tt(ya_lo[:, c], ya32[:, c], ya_hi[:, c].bitcast(F32), ALU.subtract), c_lo, c + 1)
            for c in range(KC):
                u, g, j = UNIT["bra"] + c // 4, GROUP["bra"] + c // 4, c % 4
                dve.wait_ge(steps, 4 * u + j + 1)
                line.tell(tt(sga[:, c], ps[:, j], sga[:, c], ALU.mult), bank_free[j], g + 1)
            for c in range(KC):
                u, g, j = UNIT["brb"] + 2 * (c // 4) + 1, GROUP["brb"] + c // 4, c % 4
                dve.wait_ge(steps, 4 * u + j + 1)
                line.tell(tt(sgb[:, c], ps[:, j], sgb[:, c], ALU.mult), bank_free[j], g + 1)
                line.tell(tt(y32[:], sgb[:, c], sga[:, c], ALU.add), c_y, c + 1)
                dve.wait_ge(c_hi, 4 + c + 1)
                line.tell(tt(mg_lo[:, c], y32[:], mg_hi[:, c].bitcast(F32), ALU.subtract), c_lo, 4 + c + 1)

            def residual(name, per):
                for n in range(2):
                    for t in range(NT):
                        dve.wait_ge(steps, 4 * (UNIT[name] + per * n + per - 1) + t + 1)
                        xs = x[:, t, 512 * n:512 * n + 512]
                        line.tell(tt(xs, xs, ps[:, t], ALU.add), bank_free[t], GROUP[name] + n + 1)

            residual("y2", 2)
            for t in range(NT):
                normed(t)
            turn_lo("turn5", h_lo, h_hi, 0, lambda c: col("lnffn", c))

            for i in range(FI):
                for j in range(2):
                    c = 2 * i + j
                    dve.wait_ge(steps, 4 * (UNIT["ffn"] + 2 * i + 1) + j + 1)
                    line.step(dve.tensor_scalar(facc[j][:], ps[:, j], col("cw", 44 + c), col("cb", c), ALU.mult, ALU.add))
                    line.step(stt(facc[j][:, 1:], ps[:, j, 0:S - 1], col("cw", 22 + c), facc[j][:, 1:], ALU.mult, ALU.add))
                    line.step(stt(facc[j][:, 2:], ps[:, j, 0:S - 2], col("cw", c), facc[j][:, 2:], ALU.mult, ALU.add))
                    line.tell(dve.memset(spare[:, 4 + j:5 + j], 0.0), f_acc, 2 * i + j + 1)
                    line.tell(dve.memset(spare[:, 6 + j:7 + j], 0.0), bank_free[j], GROUP["ffn"] + i + 1)
                for j in range(2):
                    c = 2 * i + j
                    dve.wait_ge(steps, 4 * (UNIT["ffn"] + 2 * i + 1) + 2 + j + 1)
                    dve.wait_ge(f_silu, c + 1)
                    line.tell(tt(facc[j][:], ps[:, 2 + j], facc[j][:], ALU.mult), bank_free[2 + j], GROUP["ffn"] + i + 1)
                    dve.wait_ge(f_hi_done, c + 1)
                    line.tell(tt(f_lo[:, c], facc[j][:], f_hi[:, c].bitcast(F32), ALU.subtract), f_lo_done, c + 1)
            residual("y3", 6)

        @block.tensor
        def _(pe):
            def mm(o, l, r, start=True, stop=True):
                return pe.matmul(o, l, r, start=start, stop=stop)

            def unit(slot, mode, act, k0, nk, first, last, u, g, width=512, after={}):
                pe.wait_ge(split_ready, u + 1)
                n_mm = 3 * nk
                for j in range(4):
                    if first:
                        pe.wait_ge(bank_free[j], g)
                    n = 0
                    for kk in range(nk):
                        a_hi, a_lo = act(k0 + kk)
                        w_hi, w_lo = whi[slot][:, kk], wlo[slot][:, kk]
                        for w, a in ((w_hi, a_hi), (w_hi, a_lo), (w_lo, a_hi)):
                            if mode == "F":
                                ins = mm(ps[:, j], w[:, j * P:j * P + P], a, first and n == 0, last and n == n_mm - 1)
                            else:
                                ins = mm(ps[:, j, 0:width], a[:, j * P:j * P + P], w[:, 0:width],
                                         first and n == 0, last and n == n_mm - 1)
                            n += 1
                    ins.then_inc(steps, 1)
                    if j in after:
                        after[j]()

            def groups(name, mode, act, width=512, total=None, waits=None):
                n, per = next((n, per) for m, n, per in PLAN if m == name)
                total = total or 4 * per

                def one(i):
                    for q in range(per):
                        if waits:
                            waits(q)
                        unit((UNIT[name] + q + (per % 2) * (i if isinstance(i, int) else 0)) % 2, mode, act, 4 * q,
                             min(4, total - 4 * q), q == 0, q == per - 1, UNIT[name] + i * per + q, GROUP[name] + i,
                             width)
                if n > 1 and per % 2 == 0:
                    with pe.Fori(0, n) as i:
                        one(i)
                else:
                    for i in range(n):
                        one(i)

            def h_parts(k):
                return h_hi[:, k], h_lo[:, k]

            seen = {"src": 0}

            def turn(name, src):
                T, g = TURNS[name], GROUP[name]
                for t in range(NT):
                    seen["src"] += 1
                    pe.wait_ge(src_ready, seen["src"])
                    for c in range(KC):
                        if t == 0 and c < 4 and g:
                            pe.wait_ge(bank_free[c], g)
                        ins = pe.transpose(ps[:, c, t * P:t * P + P], src[:, t, c * P:c * P + P], ident[:])
                        if t == NT - 1:
                            ins.then_inc(turned_pe, 1)

            def turned(name):
                for j in range(4):
                    pe.wait_ge(bank_free[j], GROUP[name] + 1)
                pe.wait_ge(turned_lo, 4 * TURNS[name] + 4)

            pe.wait_ge(const_made, 1)
            pe.wait_ge(small_in, 16 * 18)
            pe.transpose(ps[:, 4, 0:NV1], rawv[:, 0, :], ident[:]).then_inc(vt_done, 1)
            pe.transpose(ps[:, 5, 0:NV2], rawv[0:NV2, 1, :], ident[0:NV2, 0:NV2]).then_inc(vt_done, 1)
            pe.wait_ge(vcol_ready, 1)

            turn("turn0", xn)
            turned("turn0")

            def thin(w, n):
                for t in range(NT):
                    k2 = 0
                    for part in (h_hi, h_lo):
                        for k in range(KC):
                            ins = mm(ps[:, 4, t * n:t * n + n], part[:, k, t * P:t * P + P].bitcast(F32), w[:, k],
                                     k2 == 0, k2 == 2 * KC - 1)
                            k2 += 1
                return ins

            thin(wgate, 2 * HA).then_inc(gate_pe, 1)
            unit(0, "F", h_parts, 0, 4, True, False, UNIT["qb"], GROUP["qb"])
            pe.wait_ge(gate_dve, 1)
            for b, h0 in ((5, 0), (6, HA)):
                for t in range(NT):
                    ins = pe.transpose(ps[0:HA, b, t * P:t * P + P], gtok[:, t, h0:h0 + HA], ident[:])
            ins.then_inc(gate_pe, 1)
            unit(1, "F", h_parts, 4, 4, False, True, UNIT["qb"] + 1, GROUP["qb"])
            for q in range(2):
                unit(q, "F", h_parts, 4 * q, 4, q == 0, q == 1, UNIT["qb"] + 2 + q, GROUP["qb"] + 1)
            groups("kb", "F", h_parts)
            unit(0, "T", h_parts, 0, 4, True, False, UNIT["vb"], GROUP["vb"])
            pe.wait_ge(gate_act, 4)
            for b, rows_ in ((4, g_ig), (5, g_t)):
                for t in range(NT):
                    ins = pe.transpose(ps[:, b, t * HA:t * HA + HA], rows_[:, t * P:t * P + P], ident[0:HA, 0:HA])
                ins.then_inc(gate_pe, 1)
            unit(1, "T", h_parts, 4, 4, False, True, UNIT["vb"] + 1, GROUP["vb"])
            for q in range(2):
                unit(q, "T", h_parts, 4 * q, 4, q == 0, q == 1, UNIT["vb"] + 2 + q, GROUP["vb"] + 1)
            groups("zb", "F", h_parts)

            def b_scores(h):
                if h:
                    pe.wait_ge(b_copied, h)
                else:
                    pe.wait_ge(gate_dve, 11)
                for i in range(NT):
                    a = 2048 + SEG_T[i]
                    ins = mm(psf[:, a:a + P * (i + 1)], qB[:, h, i * P:i * P + P], kB[:, h, 0:P * (i + 1)])
                ins.then_inc(b_z, 1)

            def b_transpose(h):
                pe.wait_ge(b_a, h + 1)
                for j in range(NT):
                    for i in range(j, NT):
                        a, o = SEG_T[i] + j * P, 2048 + SEG_S[j] + (i - j) * P
                        ins = pe.transpose(psf[:, o:o + P], tB2[:, a:a + P], ident[:])
                ins.then_inc(b_t, 1)

            def b_outputs(h):
                pe.wait_ge(b_copied, h + 1)
                if h:
                    pe.wait_ge(b_y, h)
                for j in range(NT):
                    ins = mm(ps[:, 7, P * j:], vB[:, j, h * DB:h * DB + DB], aTB[:, SEG_S[j]:SEG_S[j] + S - P * j],
                             j == 0, j == NT - 1)
                ins.then_inc(b_o, 1)

            b_scores(0)
            for h in range(HB):
                q = h % 2
                unit(q, "F", h_parts, 4 * q, 4, q == 0, q == 1, UNIT["qa"] + h, GROUP["qa"] + h // 2,
                     after={2: lambda: b_transpose(h)})
                b_outputs(h)
                if h + 1 < HB:
                    b_scores(h + 1)
            groups("va", "T", h_parts)
            groups("oa", "T", h_parts)
            groups("za", "T", h_parts)

            def a_scores(h):
                for j in range(NT):
                    if h:
                        pe.wait_ge(a_st, 4 * h - 4 + j + 1)
                    for c in range(2):
                        ins = mm(ps[:, 4 + j, 0:S - P * j], kA[:, 2 * h + c, j * P:j * P + P], qA[:, 2 * h + c, P * j:],
                                 c == 0, c == 1)
                    ins.then_inc(a_s, 1)

            def a_outputs(h):
                pe.wait_ge(a_st, 4 * h + 4)
                for t in range(NT):
                    pe.wait_ge(bank_free[t], GROUP["a_out"] + h)
                    for j in range(t + 1):
                        a = A_OFF[j] + (t - j) * P
                        ins = mm(ps[:, t, 0:DA + 1], WA[h % 2][:, a:a + P], vA[:, j, h], j == 0, j == t)
                    ins.then_inc(a_o, 1)

            pe.wait_ge(b_y, HB)
            for h in range(HA):
                mm(ps[:, 4 + h], sel[:, h, :], g_lf[:]).then_inc(gate_pe, 1)
            pe.wait_ge(qk_ready, 16)
            pe.wait_ge(gate_act, 5)
            a_scores(0)
            for h in range(HA):
                if h + 1 < HA:
                    a_scores(h + 1)
                a_outputs(h)

            def a_turn(half):
                for t in range(NT):
                    pe.wait_ge(a_src, t + 1)
                    for c in range(4 * half, 4 * half + 4):
                        if half and t == 0:
                            pe.wait_ge(a_lo, c - 3)
                        ins = pe.transpose(ps[:, 4 + c % 4, t * P:t * P + P], soA[:, t, c * P:c * P + P], ident[:])
                        if t == NT - 1:
                            ins.then_inc(a_turned, 1)

            def y0_parts(k):
                return (yB_hi[:, k], yB_lo[:, k]) if k < HB else (yA_hi[:, k - HB], yA_lo[:, k - HB])

            pe.wait_ge(b_lo, HB)
            for n in range(2):
                for q in range(4):
                    if n == 0 and q >= 2:
                        pe.wait_ge(a_lo, 4 * q - 4)
                    unit(q % 2, "T", y0_parts, 4 * q, 4, q == 0, q == 3, UNIT["y0"] + 4 * n + q, GROUP["y0"] + n,
                         after={1: lambda: a_turn(0), 3: lambda: a_turn(1)} if n == 0 and q == 1 else {})
            turn("turn2", xn2)
            turned("turn2")

            def pool_parts(k):
                return pool_hi[:, k], pool_lo[:, k]

            for G in range(4):
                u, g = UNIT["mix"] + 5 * G, GROUP["mix"] + 3 * G
                for q in range(4):
                    unit((u + q) % 2, "F", h_parts, 4 * (q % 2), 4, q % 2 == 0, q % 2 == 1, u + q, g + q // 2)
                pe.wait_ge(pool_ready, 8 * (G + 1))
                unit(u % 2, "F", pool_parts, 0, 4, True, True, u + 4, g + 2)
            pe.wait_ge(m_lo_done, 16)
            groups("y1", "T", lambda k: (m_hi[:, k], m_lo[:, k]))
            turn("turn3", xn)
            turned("turn3")

            groups("wq", "T", h_parts)
            groups("wkv", "T", h_parts, width=256)
            groups("gq", "F", h_parts)
            pe.wait_ge(w_n, NT)
            for b in range(5):
                if b == 4:
                    pe.wait_ge(w_qk, 1)
                for t in range(NT):
                    ins = pe.transpose(ps[:, 4 + b % 4, t * P:t * P + P], qn[:, t, b * P:b * P + P], ident[:])
                ins.then_inc(w_tp, 1)
            groups("gk", "F", h_parts)
            pe.wait_ge(w_qk, 5)
            pe.wait_ge(lr_in, 32)
            thin(wlr, RANK).then_inc(l_pe, 1)
            pe.wait_ge(l_dve, 1)
            for t in range(NT):
                ins = pe.transpose(ps[0:RANK, 5, t * P:t * P + P], lrtok[:, t], ident[:])
            ins.then_inc(l_pe, 1)
            pe.wait_ge(l_dve, 2)
            for h in range(HG):
                mm(ps[:, 4 + h], wup[:, h * DK:h * DK + DK], lrT[:]).then_inc(l_pe, 1)

            def w_scores(i):
                if i:
                    pe.wait_ge(w_ya, 4 * i)
                else:
                    pe.wait_ge(l_dve, 3 + 2 * (HG - 1))
                k0 = (i - 1) * P if i else 0
                for h in range(HQ):
                    b, c = h % 4, h // 4
                    o = psf[:, 2048 + 256 * h + (0 if i else P):2048 + 256 * h + 256]
                    ins = mm(o, qkT[DH * c:DH * c + DH, b, i * P:i * P + P], qkT[DH * c:DH * c + DH, 4, k0:(i + 1) * P])
                ins.then_inc(w_s, 1)

            for i in range(NT):
                w_scores(i)
                pe.wait_ge(w_p, i + 1)
                for kb in range(2):
                    for c in range(HKV):
                        pe.wait_ge(bank_free[2 * kb + c], GROUP["w_out"] + i)
                        for b in range(4):
                            ins = pe.transpose(ps[:, 2 * kb + c, b * P:b * P + P], sm[:, 4 * c + b, kb * P:kb * P + P],
                                               ident[:])
                ins.then_inc(w_t, 1)
                for b in range(4):
                    pe.wait_ge(bank_free[b], GROUP["w_out"] + i + 1)
                for c in range(HKV):
                    for kb in range(0 if i else 1, 2):
                        v = qkv[:, i - 1 + kb, 640 + DH * c:640 + DH * c + DH]
                        ins = mm(ps[0:DH, 4 + c], v, pT[:, kb, c].rearrange("p b q -> p (b q)"), kb == (0 if i else 1), kb == 1)
                ins.then_inc(w_o, 1)
            pe.wait_ge(w_ya, 4 * NT)
            for h in range(HG):
                for b in range(NT):
                    ins = mm(ps[:, 4 + h, b * P:b * P + P], kG[:, h, b * P:b * P + P], qG[:, h, b * P:b * P + P])
                ins.then_inc(e_pe, 1)

            def level_step(s):
                pe.wait_ge(e_qk, s + 1)
                pe.wait_ge(e_at, s + 1)
                for b in range(NT):
                    ins = mm(ps[:, 4 + s % 4, b * P:b * P + P], kE[s % 2][:, b * P:b * P + P],
                             qE[s % 2][:, b * P:b * P + P])
                ins.then_inc(e_pe, 1)

            s = 0
            for n4 in range(4):
                name = "gv" if n4 < 2 else "gr"
                for q in range(2):
                    u = UNIT["gv"] + 2 * n4 + q
                    while s < STEPS_NEAR and s < STEPS_NEAR * (2 * n4 + q) // 8 - 2:
                        level_step(s)
                        s += 1
                    unit(q, "T", h_parts, 4 * q, 4, q == 0, q == 1, u, GROUP["gv"] + n4)
            while s < STEPS_NEAR:
                level_step(s)
                s += 1
            unit(0, "F", h_parts, 0, 4, True, False, UNIT["ga"], GROUP["ga"])
            unit(1, "F", h_parts, 4, 4, False, True, UNIT["ga"] + 1, GROUP["ga"])
            for h in range(HG):
                o = 2048 + 1024 * (h % 2)
                b = h % 2
                pe.wait_ge(e_qk, FAR + 2 * h + 2)
                pe.wait_ge(e_at, HG + FAR + max(0, h - 1))
                mm(psf[:, o:o + P], kE[b][:, 0:P], qE[b][:, 0:P])
                mm(psf[:, o + P:o + 2 * P], kE[b][:, P:2 * P], qE[b][:, P:2 * P])
                mm(psf[:, o + 2 * P:o + 4 * P], kE[b][:, 2 * P:3 * P], qE[b][:, 2 * P:])
                mm(psf[:, o + 4 * P:o + 6 * P], kE[b][:, 3 * P:], qE[b][:, 2 * P:]).then_inc(e_pe, 1)
            unit(0, "F", h_parts, 0, 4, True, False, UNIT["ga"] + 2, GROUP["ga"] + 1)
            unit(1, "F", h_parts, 4, 4, False, True, UNIT["ga"] + 3, GROUP["ga"] + 1)
            pe.wait_ge(e_at, HG + FAR + HG)
            far_block = {(0, 1): 0, (2, 3): 1, (0, 2): 2, (0, 3): 3, (1, 2): 4, (1, 3): 5}
            for h in range(HG):
                for t in range(NT):
                    pe.wait_ge(bank_free[t], GROUP["g_out"] + h)
                    for j in range(t + 1):
                        w = atD[:, h, t] if j == t else atO[:, h, far_block[j, t]]
                        ins = mm(ps[:, t, 0:DV], w, vG[:, j, h * DV:h * DV + DV], j == 0, j == t)
                    ins.then_inc(g_o, 1)
            groups("gb", "F", h_parts)
            for c in range(KC):
                pass
            T, g = TURNS["turn4"], GROUP["turn4"]
            for t in range(NT):
                for c in range(KC):
                    if t == 0 and c < 4:
                        pe.wait_ge(bank_free[c], g)
                    ins = pe.transpose(ps[:, c, t * P:t * P + P], rG[:, t, c * P:c * P + P], ident[:])
                    if t == NT - 1:
                        ins.then_inc(turned_pe, 1)
            pe.wait_ge(c_lo, 4)
            groups("bra", "F", lambda k: (ya_hi[:, k], ya_lo[:, k]))
            turned("turn4")
            groups("brb", "F", h_parts)
            pe.wait_ge(c_lo, 4 + KC)
            groups("y2", "T", lambda k: (mg_hi[:, k], mg_lo[:, k]))
            turn("turn5", xn)
            turned("turn5")
            groups("ffn", "F", h_parts)
            pe.wait_ge(f_lo_done, FC)
            groups("y3", "T", lambda k: (f_hi[:, k], f_lo[:, k]), total=FC)
        if dbg:
            return dict(locals())


_INS = ["x", "pre_norm_g", "post_norm_g", "w_in_ab", "conv_qk", "bias_i", "bias_f", "head_norm_g", "w_out_ab",
        "w_in_c", "pool_w", "pool_scale", "w_out_c", "ln_mix_g_2", "w_in_2", "q_norm_g_2", "k_norm_g_2", "sinks_2",
        "w_gk_up_2", "b_gk_2", "gla_norm_g_2", "w_branch_a_2", "w_branch_b_2", "w_out_2", "ln_ffn_g_2",
        "w_ffn_in_2", "conv_w_2", "conv_b_2", "w_ffn_out_2"]


def kernel(**inputs):
    import concourse.bacc as bacc
    from concourse.bass_utils import run_bass_kernel_spmd

    nc = bacc.Bacc("TRN2", target_bir_lowering=False, num_devices=1)
    arrays, A = {}, {}
    for name in _INS:
        a = np.ascontiguousarray(inputs[name])
        arrays[f"in_{name}"] = a
        A[name] = nc.dram_tensor(f"in_{name}", a.shape, mybir.dt.from_np(a.dtype), kind="ExternalInput").ap()
    out = nc.dram_tensor("out_x", (1, S, D), F32, kind="ExternalOutput").ap()
    build(nc, A, out)
    r = run_bass_kernel_spmd(nc, [arrays], core_ids=[0])
    return r.results[0]["out_x"]
```

```python
from contextlib import ExitStack

import numpy as np

import concourse.bass as bass
from concourse import mybir

F32 = mybir.dt.float32
F32R = mybir.dt.float32r
I32 = mybir.dt.int32
ALU = mybir.AluOpType
ACT = mybir.ActivationFunctionType
AX = mybir.AxisListType.X

P = 128
S = 512
NT = S // P
D = 1024
KC = D // P
EPS = 1e-6
KB = 1024

HA, DA = 4, 256
HB, DB = 8, 128
WINDOWS = (2, 4, 8, 16)
HQ, HKV, DH = 8, 2, 64
HG, DK, DV, RANK = 4, 128, 256, 16
GATE = 16.0
LEVELS = (64, 32, 16, 8, 4, 2, 1)
DFF = 2816
FC = DFF // P
FI = FC // 2

PLAN = [
    ("turn0", 1, 0),
    ("qb", 2, 2), ("kb", 2, 2), ("vb", 2, 2), ("zb", 2, 2),
    ("qa", 2, 2), ("ka", 2, 2), ("va", 2, 2), ("oa", 2, 2), ("za", 2, 2),
    ("a_out", HA, 0),
    ("y0", 2, 4), ("turn2", 1, 0),
    ("mix", 4, 5),
    ("y1", 2, 4), ("turn3", 1, 0),
    ("wq", 1, 2), ("wkv", 1, 2), ("gq", 1, 2), ("gk", 1, 2),
    ("gv", 2, 2), ("gr", 2, 2), ("ga", 2, 2), ("gb", 2, 2),
    ("bra", 2, 1), ("brb", 2, 2), ("y2", 2, 2), ("turn5", 1, 0),
    ("ffn", FI, 2), ("y3", 2, 6),
]
UNIT, GROUP = {}, {}
_u = _g = 0
for _name, _n, _per in PLAN:
    UNIT[_name], GROUP[_name] = _u, _g
    _u += _n * _per
    _g += _n * (3 if _name == "mix" else 1)
UNITS = _u
assert UNITS % 2 == 0
TURNS = {"turn0": 0, "turn2": 1, "turn3": 2, "turn5": 3}

VECS = [("pre", 16), ("lnmix", 8), ("lnffn", 8), ("convqk", 64), ("pscale", 16), ("bgk", 4),
        ("hn", 8), ("qn", 1), ("kn", 1), ("gla", 2)]
VECS2 = [("cw", 66), ("cb", 22)]
COL = {}
_c = 0
for _name, _n in VECS + VECS2:
    COL[_name] = _c
    _c += _n
NV1 = sum(n for _, n in VECS)
NV2 = sum(n for _, n in VECS2)
assert NV1 == P

IN_AB_B = 5 * D + 2 * HA
C2 = {"qa": 0, "kv": 512, "gq": 768, "gk": 1280, "gv": 1792, "gr": 2816, "lr": 3840, "ga": 3856, "gb": 4880}
SEG_T = {3: 0, 2: 512, 0: 896, 1: 1024}
SEG_S = {0: 0, 1: 512, 3: 896, 2: 1024}
CAUSAL = 1280


A_OFF = (0, 512, 896, 1152)
STEPS_NEAR = len(LEVELS) * HG
FAR = STEPS_NEAR


def near_steps(slot):
    return STEPS_NEAR * slot // 16


class Line:

    def __init__(self, engine, sem):
        self.engine, self.sem, self.base, self.k = engine, sem, 0, 0

    def step(self, ins):
        ins.then_inc(self.sem, 1)
        self.k += 1
        self.engine.wait_ge(self.sem, self.base + self.k)

    def tell(self, ins, sem, value):
        ins.then_inc(sem, 1)
        self.engine.wait_ge(sem, value)

    def enter(self, i, per):
        self.start = self.base + self.k
        self.base, self.k, self.per = self.start + i * per, 0, per

    def leave(self, times):
        assert self.k == self.per, (self.k, self.per)
        self.base, self.k = self.start + times * self.per, 0


def build(nc, A, out, dbg=None, upto=None):
    with ExitStack() as ctx:
        def sem(name):
            return ctx.enter_context(nc.semaphore(name))

        base = (nc.sbuf_base + 31) // 32 * 32

        def at(name, shape, dtype, kb):
            off = base + int(kb * KB) // 32 * 32
            return nc.alloc_sbuf_tensor_at(name, shape, dtype, offset=off)

        raw = [at(f"raw{s}", [P, 4, 512], F32, 8 * s) for s in range(2)]
        whi = [at(f"whi{s}", [P, 4, 512], F32R, 16 + 8 * s) for s in range(2)]
        wlo = [at(f"wlo{s}", [P, 4, 512], F32R, 32 + 8 * s) for s in range(2)]
        h_hi = at("h_hi", [P, KC, S], F32R, 48)
        h_lo = at("h_lo", [P, KC, S], F32R, 64)
        x = at("x", [P, NT, D], F32, 80)
        C0 = 96
        ident = at("ident", [P, P], F32, C0)
        tri = at("tri", [P, P], F32, C0 + .5)
        below = at("below", [P, P], F32, C0 + 1)
        band = at("band", [P, 2 * P], F32, C0 + 1.5)
        level = at("level", [P, 7, P], F32, C0 + 2.5)
        vcol = at("vcol", [P, NV1 + NV2], F32, C0 + 6)
        invc = at("invc", [P, 16], F32, C0 + 6.875)
        small = at("small", [P, 256], F32, C0 + 7)
        postg = at("postg", [P, D], F32, C0 + 8)
        g_lf = at("g_lf", [HA, S], F32, C0 + 8)
        sel = at("sel", [HA, HA, P], F32, C0 + 10)
        y32 = at("y32", [P, S], F32, C0 + 12)
        AR = C0 + 14
        ss, var, std, rs, nwt = (small[:, 40 * i:40 * i + 40] for i in range(5))
        sinkb = small[:, 200:208]
        den, rden = small[:, 208:212], small[:, 212:216]
        cT = small[:, 216:232].rearrange("p (t h) -> p t h", h=HA)
        emT = small[:, 232:248].rearrange("p (t h) -> p t h", h=HA)
        spare = small[:, 248:256]
        diag = at("diag", [P, NT, P], F32, AR + 80)
        yg = at("yg", [P, NT, D], F32, AR + 64)
        g_ig, g_t, g_b, g_m = (at(n, [HA, S], F32, AR + 82 + 2 * i)
                               for i, n in enumerate(("g_ig", "g_t", "g_b", "g_m")))
        wgate = at("wgate", [P, KC, 36], F32, AR + 16)
        wg_hi = at("wg_hi", [P, KC, 36], F32R, AR + 18)
        wg_lo = at("wg_lo", [P, KC, 36], F32R, AR + 20)
        bias4 = at("bias4", [HA, 2], F32, AR + 92.75)
        qB = at("qB", [P, HB, S], F32, AR + 32)
        kB = at("kB", [P, HB, S], F32, AR + 48)
        yB_hi = at("yB_hi", [P, HB, S], F32R, AR + 32)
        yB_lo = at("yB_lo", [P, HB, S], F32R, AR + 48)
        vB = at("vB", [P, NT, D], F32, 80)
        szB = at("szB", [P, HB, S], F32, AR + 64)
        tB1 = at("tB1", [P, CAUSAL], F32, AR + 80)
        tB2 = at("tB2", [P, CAUSAL], F32, AR + 85)
        aTB = at("aTB", [P, CAUSAL], F32, AR + 90)
        qA = at("qA", [P, KC, S], F32, AR)
        kA = at("kA", [P, KC, S], F32, AR + 16)
        soA = at("soA", [P, NT, D], F32, AR + 64)
        vA = at("vA", [P, NT, HA, DA + 1], F32, AR + 80)
        szA = at("szA", [P, NT, D], F32, 80)
        WA = [at(f"WA{b}", [P, CAUSAL], F32, 48 + 5 * b) for b in range(2)]
        junkA = at("junkA", [P, DA], F32, 60)
        nMb = at("nMb", [P, HA, S], F32, 64)
        yA_hi = at("yA_hi", [P, KC, S], F32R, AR)
        yA_lo = at("yA_lo", [P, KC, S], F32R, AR + 16)
        rawv = at("rawv", [P, 2, P], F32, AR + 72)
        junk = at("junk", [P, D], F32, AR + 93.75)
        notfirst = at("notfirst", [P, S], F32, AR + 94)
        m_hi = at("m_hi", [P, 16, S], F32R, AR)
        m_lo = at("m_lo", [P, 16, S], F32R, AR + 32)
        pool_hi = at("pool_hi", [P, 4, S], F32R, AR + 64)
        pool_lo = at("pool_lo", [P, 4, S], F32R, AR + 72)
        PAD = 16
        pw = [at(f"pw{b}", [P, PAD + S], F32, AR + 80 + 2.0625 * b) for b in range(3)]
        szC = at("szC", [P, 4, S], F32, AR + 86.25)
        ya32 = at("ya32", [P, 4, S], F32, AR)
        qG = at("qG", [P, HG, S], F32, AR + 8)
        kG = at("kG", [P, HG, S], F32, AR + 16)
        bG = at("bG", [P, HG, S], F32, AR + 24)
        vG = at("vG", [P, NT, D], F32, 80)
        rG = at("rG", [P, NT, D], F32, AR + 48)
        atD = at("atD", [P, HG, 4, P], F32, AR + 64)
        atO = at("atO", [P, HG, 6, P], F32, AR + 72)
        dG = [at(f"dG{b}", [P, S], F32, AR + 84 + 2 * b) for b in range(2)]
        qE = [at(f"qE{b}", [P, S], F32, AR + 88 + 2 * b) for b in range(2)]
        kE = [at(f"kE{b}", [P, S], F32, AR + 92 + 2 * b) for b in range(2)]
        qkT = at("qkT", [P, 5, S], F32, AR + 32)
        junk2 = at("junk2", [P, 5 * P], F32, AR + 36)
        sm = at("sm", [P, 4, 2 * P], F32, AR + 42)
        gln = at("gln", [P, S], F32, AR + 42)
        lrT = at("lrT", [RANK, S], F32, AR + 46)
        qkv = at("qkv", [P, NT, 768], F32, AR + 64)
        qn = at("qn", [P, NT, 640], F32, AR + 76)
        wup = at("wup", [RANK, HG * DK], F32, AR + 86)
        gtmp = [at(f"gtmp{b}", [P, S], F32, AR + 88 + 2 * b) for b in range(2)]
        pT = at("pT", [P, 2, 4, P], F32, AR + 88)
        wlr = at("wlr", [P, KC, RANK], F32, AR + 96.25)
        wlr_hi = at("wlr_hi", [P, KC, RANK], F32R, AR + 45)
        wlr_lo = at("wlr_lo", [P, KC, RANK], F32R, AR + 45.5)
        junkG = at("junkG", [P, DV], F32, AR + 96)
        wstat = at("wstat", [P, 4, 4], F32, AR + 97)
        bend = at("bend", [P, 2, HG, NT], F32, AR + 97.25)
        sga = at("sga", [P, KC, S], F32, AR + 32)
        sgb = at("sgb", [P, KC, S], F32, AR + 8)
        ya_hi = at("ya_hi", [P, 4, S], F32R, AR + 24)
        ya_lo = at("ya_lo", [P, 4, S], F32R, AR + 88)
        mg_hi = at("mg_hi", [P, KC, S], F32R, AR + 64)
        mg_lo = at("mg_lo", [P, KC, S], F32R, AR + 48)
        f_hi = at("f_hi", [P, FC, S], F32R, AR)
        f_lo = at("f_lo", [P, FC, S], F32R, AR + 44)
        facc = [at(f"facc{b}", [P, S], F32, AR + 88 + 2 * b) for b in range(2)]

        ps = ctx.enter_context(nc.psum_tensor("ps", [P, 8, 512], F32))
        psf = ps[:].rearrange("p b n -> p (b n)")

        x_in = [sem(f"x_in{t}") for t in range(NT)]
        small_in = sem("small_in")
        postg_in = sem("postg_in")
        lr_in = sem("lr_in")
        padded = sem("padded")
        const_made = sem("const_made")
        raw_full = [sem(f"raw_full{s}") for s in range(2)]
        hi_made = sem("hi_made")
        unit_taken = sem("unit_taken")
        split_ready = sem("split_ready")
        steps = sem("steps")
        bank_free = [sem(f"bank_free{j}") for j in range(4)]
        act_line = sem("act_line")
        dve_line = sem("dve_line")
        pool_line = sem("pool_line")
        vt_done = sem("vt_done")
        vcol_ready = sem("vcol_ready")
        ss_ready, var_ready, std_ready = sem("ss_ready"), sem("var_ready"), sem("std_ready")
        src_ready = sem("src_ready")
        turned_pe, turned_hi, turned_lo = sem("turned_pe"), sem("turned_hi"), sem("turned_lo")
        x_ready = sem("x_ready")
        gate_pe, gate_dve, gate_act = sem("gate_pe"), sem("gate_dve"), sem("gate_act")
        qk_ready = sem("qk_ready")
        a_s, a_arg, a_exp, a_st, a_o = sem("a_s"), sem("a_arg"), sem("a_exp"), sem("a_st"), sem("a_o")
        y_src, y_turned, y_hi, y_lo = sem("y_src"), sem("y_turned"), sem("y_hi"), sem("y_lo")
        b_z, b_rest, b_beta, b_a, b_t, b_copied, b_o, b_y, b_hi, b_lo = (
            sem(n) for n in ("b_z", "b_rest", "b_beta", "b_a", "b_t", "b_copied", "b_o", "b_y", "b_hi", "b_lo"))
        p_in, p_out, pool_h, pool_ready, m_y, m_hi_done, m_lo_done = (
            sem(n) for n in ("p_in", "p_out", "pool_h", "pool_ready", "m_y", "m_hi_done", "m_lo_done"))
        w_qkv, w_sq, w_n, w_tp, w_qk, w_s, w_neg, w_exp, w_p, w_t, w_copied, w_o, w_ya = (
            sem(n) for n in ("w_qkv", "w_sq", "w_n", "w_tp", "w_qk", "w_s", "w_neg", "w_exp", "w_p", "w_t",
                             "w_copied", "w_o", "w_ya"))
        l_pe, l_dve, l_act = sem("l_pe"), sem("l_dve"), sem("l_act")
        e_d, e_exp, e_qk, e_pe, e_at = sem("e_d"), sem("e_exp"), sem("e_qk"), sem("e_pe"), sem("e_at")
        g_o, g_taken = sem("g_o"), sem("g_taken")
        kept = sem("kept")
        c_y, c_hi, c_lo = sem("c_y"), sem("c_hi"), sem("c_lo")
        f_acc, f_silu, f_y, f_hi_done, f_lo_done = (
            sem(n) for n in ("f_acc", "f_silu", "f_y", "f_hi_done", "f_lo_done"))
        stored = sem("stored")

        def col(name, k=0):
            return vcol[:, COL[name] + k:COL[name] + k + 1]

        def rows(v, n):
            return v.rearrange("(r p) -> r p", p=P)

        def wview(w):
            return w.rearrange("(k p) n -> p k n", p=P)

        w_ab, w_oab, w_c, w_pool, w_oc = (
            wview(A["w_in_ab"][0]), wview(A["w_out_ab"][0]), wview(A["w_in_c"][0]), A["pool_w"][0],
            wview(A["w_out_c"][0]))
        w_2, w_ba, w_bb, w_o2, w_fi, w_fo = (
            wview(A[n][0]) for n in ("w_in_2", "w_branch_a_2", "w_branch_b_2", "w_out_2", "w_ffn_in_2",
                                     "w_ffn_out_2"))

        def cols(w, k0, nk, c0, n=512):
            return w[:, k0:k0 + nk, c0:c0 + n]

        block = ctx.enter_context(nc.Block())

        @block.sync
        def _(sp):
            for t in range(NT):
                sp.dma_start(x[:, t], A["x"][0, t * P:(t + 1) * P, :]).then_inc(x_in[t], 16)

            vec_rows = [(A["pre_norm_g"].rearrange("a (r p) -> (a r) p", p=P), 16),
                        (rows(A["ln_mix_g_2"][0], 8), 8), (rows(A["ln_ffn_g_2"][0], 8), 8),
                        (A["conv_qk"][0].rearrange("w (r p) -> (w r) p", p=P), 64),
                        (rows(A["pool_scale"][0], 16), 16), (rows(A["b_gk_2"][0], 4), 4),
                        (rows(A["head_norm_g"][0], 8), 8)]
            r = 0
            for src, n in vec_rows:
                sp.dma_start(rawv[r:r + n, 0, :], src).then_inc(small_in, 16)
                r += n
            for g in ("q_norm_g_2", "k_norm_g_2"):
                for half in range(2):
                    sp.dma_start(rawv[r:r + 1, 0, DH * half:DH * half + DH], A[g]).then_inc(small_in, 16)
                r += 1
            sp.dma_start(rawv[r:r + 2, 0, :], rows(A["gla_norm_g_2"][0], 2)).then_inc(small_in, 16)
            sp.dma_start(rawv[0:66, 1, :], A["conv_w_2"][0].rearrange("w (r p) -> (w r) p", p=P)).then_inc(small_in, 16)
            sp.dma_start(rawv[66:88, 1, :], rows(A["conv_b_2"][0], 22)).then_inc(small_in, 16)
            sp.dma_start(sinkb, A["sinks_2"][0].partition_broadcast(P)).then_inc(small_in, 16)
            sp.wait_ge(padded, 1)
            for n in range(2):
                sp.dma_start(wgate[:, :, 32 * n:32 * n + HA], cols(w_ab, 0, KC, 5 * D + HA * n, HA))\
                    .then_inc(small_in, 16)
            for n, b in enumerate(("bias_i", "bias_f")):
                sp.dma_start(bias4[:, n:n + 1], A[b].rearrange("a h -> h a")).then_inc(small_in, 16)

            def load(u, slot, src, width=512, nk=4, c0=0, inc=32):
                if isinstance(u, int):
                    if u >= 2:
                        sp.wait_ge(split_ready, u - 1)
                else:
                    sp.wait_ge(split_ready, u - 1)
                sp.dma_start(raw[slot][:, 0:nk, c0:c0 + width], src).then_inc(raw_full[slot], inc)

            def stream(name, w, c0, per, groups):
                u0 = UNIT[name]

                def one(i):
                    for q in range(per):
                        load(u0 + i * per + q, (u0 + q) % 2,
                             w[:, 4 * q:4 * q + 4, bass.ds(c0 + i * 512, 512)])
                if groups == 1:
                    one(0)
                elif u0 == 0:
                    one(0)
                    with sp.Fori(1, groups) as i:
                        one(i)
                else:
                    with sp.Fori(0, groups) as i:
                        one(i)

            stream("qb", w_ab, IN_AB_B, 2, 8)
            stream("qa", w_ab, 0, 2, 10)
            for n in range(2):
                for q in range(4):
                    load(UNIT["y0"] + 4 * n + q, q % 2, cols(w_oab, 4 * (q ^ 2), 4, 512 * n))
            for G in range(4):
                u = UNIT["mix"] + 5 * G
                load(u, u % 2, cols(w_c, 0, 4, 512 * G))
                load(u + 1, (u + 1) % 2, cols(w_c, 4, 4, 512 * G))
                load(u + 2, u % 2, cols(w_c, 0, 4, 2048 + 512 * G))
                load(u + 3, (u + 1) % 2, cols(w_c, 4, 4, 2048 + 512 * G))
                load(u + 4, u % 2, w_pool[G].rearrange("(k p) n -> p k n", p=P))
            stream("y1", w_oc, 0, 4, 2)
            stream("wq", w_2, C2["qa"], 2, 1)
            for q in range(2):
                load(UNIT["wkv"] + q, q, cols(w_2, 4 * q, 4, C2["kv"], 256), width=256)
            stream("gq", w_2, C2["gq"], 2, 1)
            stream("gk", w_2, C2["gk"], 2, 1)
            stream("gv", w_2, C2["gv"], 2, 4)
            stream("ga", w_2, C2["ga"], 2, 4)
            stream("bra", w_ba, 0, 1, 1)
            load(UNIT["bra"] + 1, 1, cols(w_ba, 0, 4, 512))
            stream("brb", w_bb, 0, 2, 2)
            stream("y2", w_o2, 0, 2, 2)
            with sp.Fori(0, FI) as i:
                for q in range(2):
                    u = UNIT["ffn"] + 2 * i + q
                    load(u, q, w_fi[:, 4 * q:4 * q + 4, bass.ds(i * 256, 256)], width=256, inc=16)
                    sp.dma_start(raw[q][:, :, 256:512], w_fi[:, 4 * q:4 * q + 4, bass.ds(DFF + i * 256, 256)])\
                        .then_inc(raw_full[q], 16)
            for n in range(2):
                for q in range(6):
                    nk = min(4, FC - 4 * q)
                    load(UNIT["y3"] + 6 * n + q, q % 2, cols(w_fo, 4 * q, nk, 512 * n), nk=nk)
            for n in range(2):
                for t in range(NT):
                    sp.wait_ge(bank_free[t], GROUP["y3"] + n + 1)
                    sp.dma_start(out[0, t * P:(t + 1) * P, n * 512:(n + 1) * 512],
                                 x[:, t, n * 512:(n + 1) * 512]).then_inc(stored, 16)
            sp.wait_ge(stored, 16 * 2 * NT)

        @block.gpsimd
        def _(pool):
            line = Line(pool, pool_line)

            def select(view, pattern, base, channel, compare=ALU.is_ge, fill=0.0):
                line.step(pool.affine_select(out=view, in_=view, pattern=pattern, base=base,
                                             channel_multiplier=channel, compare_op=compare, fill=fill))

            line.step(pool.memset(ident[:], 0.0))
            select(ident[:], [[-1, P]], 0, 1, ALU.not_equal, 1.0)
            line.step(pool.memset(sel[:], 0.0))
            pool.affine_select(out=sel[:], in_=sel[:], pattern=[[-1, HA], [0, P]], base=0, channel_multiplier=1,
                               compare_op=ALU.not_equal, fill=1.0).then_inc(const_made, 1)

            def split(u, slot, first=False):
                pool.wait_ge(raw_full[slot], (u // 2) * 32 + 32 if isinstance(u, int) else (u[0]) * 32 + 32)
                n = u if isinstance(u, int) else 2 * u[0] + u[1]
                if not first:
                    pool.wait_ge(steps, 4 * (n - 1))
                    pool.sem_inc(unit_taken, 1)
                pool.tensor_scalar(whi[slot][:], raw[slot][:], 1.0, 0.0, ALU.mult, ALU.add).then_inc(hi_made, 1)
                pool.wait_ge(hi_made, n + 1)
                pool.tensor_tensor(wlo[slot][:], raw[slot][:], whi[slot][:].bitcast(F32), ALU.subtract)\
                    .then_inc(split_ready, 1)

            split(0, 0, first=True)
            split(1, 1, first=True)
            line.step(pool.memset(tri[:], 1.0))
            select(tri[:], [[1, P]], 0, -1)
            line.step(pool.memset(below[:], 1.0))
            select(below[:], [[-1, P]], -1, 1)
            line.step(pool.memset(band[:], 0.0))
            select(band[:, 0:P], [[1, P]], -1, -1, fill=-1e30)
            select(band[:, P:], [[-1, P]], 0, 1, fill=-1e30)
            line.step(pool.memset(level[:], 0.0))
            for n, L in enumerate(LEVELS):
                v = level[:, n, :].rearrange("p (a two l) -> p a two l", two=2, l=L)[:, :, 1, :]
                line.step(pool.memset(v, 1.0))
                select(v, [[-2 * L, P // (2 * L)], [0, L]], 0, 1)
                select(v, [[2 * L, P // (2 * L)], [0, L]], L - 1, -1)
            pool.memset(spare[:, 0:4], 1.0).then_inc(const_made, 1)
            with pool.Fori(1, UNITS // 2) as i:
                split((i, 0), 0)
                split((i, 1), 1)

        @block.scalar
        def _(act):
            line = Line(act, act_line)
            stats = [0]

            def fn(out_, in_, f, **kw):
                return act.activation(out_, in_, f, **kw)

            def copy(out_, in_, **kw):
                return act.activation(out_, in_, ACT.Copy, **kw)

            def root(width):
                stats[0] += 1
                act.wait_ge(var_ready, stats[0])
                line.tell(fn(std[:, 0:width], var[:, 0:width], ACT.Sqrt), std_ready, stats[0])

            squares = [0]

            def square(in_, col_, width=D, junk=junk):
                squares[0] += 1
                line.tell(fn(junk[:, 0:width], in_, ACT.Square, accum_out=ss[:, col_:col_ + 1]), ss_ready, squares[0])

            def turn_hi(name, dst, c0, gname):
                T = TURNS[name]
                for c in range(KC):
                    act.wait_ge(turned_pe, 8 * T + c + 1)
                    line.tell(copy(dst[:, c0 + c], ps[:, c], scale=gname(c)), turned_hi, 8 * T + c + 1)

            for t in range(NT):
                act.wait_ge(x_in[t], 16)
                square(x[:, t], t)
            root(NT)
            act.wait_ge(vcol_ready, 1)
            turn_hi("turn0", h_hi, 0, lambda c: col("pre", c))

            for name, dst, f, sc in (("qb", qB, ACT.Copy, DB ** -0.5), ("kb", kB, ACT.Copy, 1.0),
                                     ("vb", vB, ACT.Copy, 1.0), ("zb", szB, ACT.Silu, 1.0)):
                for n in range(2):
                    u, g = UNIT[name] + 2 * n + 1, GROUP[name] + n
                    for j in range(4):
                        act.wait_ge(steps, 4 * u + j + 1)
                        o = vB[:, j, n * 512:n * 512 + 512] if name == "vb" else dst[:, 4 * n + j]
                        line.tell(fn(o, ps[:, j], f, scale=sc), bank_free[j], g + 1)
                if name == "qb":
                    act.wait_ge(gate_dve, 3)
                    line.tell(fn(g_t[:], g_lf[:], ACT.Abs), gate_act, 1)
                    line.tell(fn(g_t[:], g_t[:], ACT.Exp, scale=-1.0), gate_act, 2)
                    line.tell(fn(g_t[:], g_t[:], ACT.Ln, bias=1.0), gate_act, 3)
                elif name == "kb":
                    act.wait_ge(gate_dve, 8)
                    line.tell(fn(g_t[:], g_m[:], ACT.Exp, scale=-1.0), gate_act, 4)

            def qk_silu(c):
                act.wait_ge(bank_free[c % 4], GROUP["qa"] + c // 4 + 1)
                dst = (qA if c < 8 else kA)[:, c % 8]
                line.tell(fn(dst, dst, ACT.Silu), qk_ready, c + 1)

            zps = psf[:, 2048:2048 + CAUSAL]
            for h in range(HB):
                act.wait_ge(b_z, h + 1)
                line.tell(fn(tB1[:], zps, ACT.Sigmoid, scale=-1.0), b_rest, h + 1)
                line.tell(fn(tB2[:], zps, ACT.Sigmoid), b_beta, h + 1)
                act.wait_ge(b_t, h + 1)
                line.tell(copy(aTB[:], zps), b_copied, h + 1)
                if h % 2:
                    for j in range(3):
                        qk_silu(2 * (h - 1) + j)
                act.wait_ge(b_y, h + 1)
                line.tell(copy(yB_hi[:, h], y32[:]), b_hi, h + 1)
                if h % 2:
                    qk_silu(2 * (h - 1) + 3)
            for name, dst, f in (("va", vA, ACT.Copy), ("oa", soA, ACT.Sigmoid), ("za", szA, ACT.Silu)):
                for n in range(2):
                    u, g = UNIT[name] + 2 * n + 1, GROUP[name] + n
                    for j in range(4):
                        act.wait_ge(steps, 4 * u + j + 1)
                        if name == "va":
                            o = vA[:, j, 2 * n:2 * n + 2, 0:DA]
                            i = ps[:, j].rearrange("p (h d) -> p h d", d=DA)
                        else:
                            o, i = dst[:, j, n * 512:n * 512 + 512], ps[:, j]
                        line.tell(fn(o, i, f), bank_free[j], g + 1)
            act.wait_ge(gate_pe, 7)
            line.tell(copy(nMb[:, 0:HA], ps[:, 4:8]), gate_act, 5)
            act.dma_start(postg[:], A["post_norm_g"][0].partition_broadcast(P)).then_inc(postg_in, 16)

            def a_weights(h):
                for j in range(NT):
                    act.wait_ge(a_arg, 4 * h + j + 1)
                    w = WA[h % 2][:, A_OFF[j]:A_OFF[j] + S - P * j]
                    line.tell(fn(w, w, ACT.Exp), a_exp, 4 * h + j + 1)

            def a_squares(h):
                for t in range(NT):
                    act.wait_ge(bank_free[t], GROUP["a_out"] + h + 1)
                    square(soA[:, t, h * DA:h * DA + DA], 4 * h + t, width=DA, junk=junkA)

            a_weights(0)
            a_weights(1)
            for h in range(HA):
                a_squares(h)
                if h + 2 < HA:
                    a_weights(h + 2)
            root(16)
            def y_turn_hi(use, dst, gname):
                for c in range(KC):
                    n = KC * use + c + 1
                    act.wait_ge(y_turned, n)
                    line.tell(copy(dst[:, c], ps[:, 4 + c % 4], scale=gname(c)), y_hi, n)

            y_turn_hi(0, yA_hi, lambda c: col("hn", c))
            act.wait_ge(y_src, NT)
            for t in range(NT):
                act.dma_start(x[:, t], A["x"][0, t * P:(t + 1) * P, :]).then_inc(x_in[t], 16)

            def y_post(name):
                u, per = UNIT[name], 4
                for t in range(NT):
                    act.wait_ge(steps, 4 * (u + per - 1) + t + 1)
                    square(ps[:, t], t, width=512)
                for t in range(NT + 1):
                    if t < NT:
                        act.wait_ge(steps, 4 * (u + 2 * per - 1) + t + 1)
                        square(ps[:, t], 4 + t, width=512)
                    root(1 if t in (0, NT) else 2)
                    if t < NT:
                        act.wait_ge(x_ready, NT * (1 if name == "y0" else 2) - NT + t + 1)
                        square(x[:, t], 21)

            y_post("y0")
            act.wait_ge(x_ready, NT)
            act.dma_start(postg[:], A["post_norm_g"][1].partition_broadcast(P)).then_inc(postg_in, 16)
            turn_hi("turn2", h_hi, 0, lambda c: col("pre", 8 + c))

            for G in range(4):
                u, g = UNIT["mix"] + 5 * G, GROUP["mix"] + 3 * G
                for j in range(4):
                    n = 4 * G + j
                    act.wait_ge(steps, 4 * (u + 1) + j + 1)
                    if n >= 1:
                        act.wait_ge(p_out, n)
                    line.tell(copy(pw[0][:, PAD:], ps[:, j]), bank_free[j], g + 1)
                    act.wait_ge(pool_ready, 2 * n + 1)
                    line.tell(copy(pool_hi[:, j], y32[:]), pool_h, n + 1)
                for j in range(4):
                    act.wait_ge(steps, 4 * (u + 3) + j + 1)
                    line.tell(fn(szC[:, j], ps[:, j], ACT.Silu), bank_free[j], g + 2)
                for j in range(4):
                    n = 4 * G + j
                    act.wait_ge(bank_free[j], g + 3)
                    line.tell(copy(m_hi[:, n], szC[:, j]), m_hi_done, n + 1)
            y_post("y1")
            act.dma_start(wlr[:], cols(w_2, 0, KC, C2["lr"], RANK)).then_inc(lr_in, 16)
            act.dma_start(wup[:], A["w_gk_up_2"][0]).then_inc(lr_in, 16)
            turn_hi("turn3", h_hi, 0, lambda c: col("lnmix", c))
            for t in range(NT):
                act.dma_start(out[0, t * P:(t + 1) * P, :], x[:, t]).then_inc(kept, 16)

            for name, c0, w in (("wq", 0, 512), ("wkv", 512, 256)):
                u, g = UNIT[name] + 1, GROUP[name]
                for j in range(4):
                    act.wait_ge(steps, 4 * u + j + 1)
                    line.tell(copy(qkv[:, j, c0:c0 + w], ps[:, j, 0:w]), bank_free[j], g + 1)
            for t in range(NT):
                if t:
                    act.wait_ge(w_sq, t)
                line.tell(fn(junk2[:], qkv[:, t, 0:640], ACT.Square), w_qkv, t + 1)
            root(40)
            def project_out(name, dst, sc):
                u, g = UNIT[name] + 1, GROUP[name]
                for j in range(4):
                    act.wait_ge(steps, 4 * u + j + 1)
                    line.tell(copy(dst[:, j], ps[:, j], scale=sc), bank_free[j], g + 1)

            project_out("gq", qG, DK ** -0.5)
            for h in range(HG):
                act.wait_ge(l_dve, 3 + 2 * h)
                line.step(fn(gln[:], gtmp[h % 2][:], ACT.Abs))
                line.step(fn(gln[:], gln[:], ACT.Exp, scale=-1.0))
                line.tell(fn(gln[:], gln[:], ACT.Ln, bias=1.0), l_act, h + 1)
                act.wait_ge(l_dve, 4 + 2 * h)
            for b in range(5):
                act.wait_ge(w_tp, b + 1)
                line.tell(copy(qkT[:, b], ps[:, 4 + b % 4], scale=col("qn" if b < 4 else "kn")), w_qk, b + 1)
            project_out("gk", kG, 1.0)

            def evacuate(name, n, j):
                act.wait_ge(steps, 4 * (UNIT[name] + 2 * n + 1) + j + 1)
                if name == "gv":
                    if n == 0 and j == 0:
                        act.wait_ge(kept, 16 * NT)
                    ins = copy(vG[:, j, n * 512:n * 512 + 512], ps[:, j])
                elif name == "gr":
                    ins = fn(rG[:, j, n * 512:n * 512 + 512], ps[:, j], ACT.Silu)
                else:
                    ins = fn((sga if name == "ga" else sgb)[:, 4 * n + j], ps[:, j], ACT.Sigmoid)
                line.tell(ins, bank_free[j], GROUP[name] + n + 1)

            for n in range(2 * NT):
                i, c = n // 2, n % 2
                k0 = 0 if i else P
                group = ("gv" if n < 4 else "gr", n // 2 % 2)
                act.wait_ge(w_neg, n + 1)
                for b in range(4):
                    line.tell(fn(sm[:, b, k0:], sm[:, b, k0:], ACT.Exp, bias=wstat[:, 1, b:b + 1],
                                 accum_out=wstat[:, 2, b:b + 1]), w_exp, 5 * n + b + 1)
                line.tell(fn(wstat[:, 3], wstat[:, 3], ACT.Exp), w_exp, 5 * n + 5)
                if n % 2:
                    for j in range(3):
                        evacuate(*group, j)
                act.wait_ge(w_t, n + 1)
                line.tell(copy(pT[:, k0 // P:].rearrange("p k b q -> p (k b q)"), psf[:, 3072 + 4 * k0:]), w_copied, n + 1)
                if n % 2:
                    evacuate(*group, 3)
                act.wait_ge(w_o, n + 1)
                o = ps[0:DH, 6].rearrange("p (b two q) -> p b two q", two=2, q=P)
                for odd in range(2):
                    line.tell(copy(ya32[DH * odd:DH * odd + DH, 2 * c:2 * c + 2, i * P:i * P + P], o[:, :, odd, :]),
                              w_ya, 2 * n + odd + 1)

            def decay(s):
                act.wait_ge(e_d, s + 1)
                line.step(fn(dG[s % 2][:], dG[s % 2][:], ACT.Abs))
                line.tell(fn(dG[s % 2][:], dG[s % 2][:], ACT.Exp, scale=-1.0 / GATE), e_exp, s + 1)

            s = 0
            for slot in (4, 5, 6, 7, 12, 13, 14, 15):
                while s < min(STEPS_NEAR, near_steps(slot) + 2):
                    decay(s)
                    s += 1
                evacuate("ga", slot // 8, slot % 4)
            assert s == STEPS_NEAR
            for h in range(HG):
                s = FAR + 2 * h
                d = dG[0][:].rearrange("p (b t) -> p b t", t=P)
                bb = bG[:, h].rearrange("p (b t) -> p b t", t=P)
                act.wait_ge(e_qk, s)
                line.step(fn(d[:, 0:2], bb[:, 1::2], ACT.Exp, scale=1.0 / GATE))
                line.step(fn(d[:, 2], bb[:, 2], ACT.Exp, scale=1.0 / GATE))
                line.tell(fn(d[:, 3], bb[:, 3], ACT.Exp, scale=1.0 / GATE, bias=bend[:, 0, h, 2:3]), e_exp, s + 1)
                d = dG[1][:].rearrange("p (b t) -> p b t", t=P)
                line.step(fn(d[:, 0], bb[:, 0], ACT.Exp, scale=-1.0 / GATE, bias=bend[:, 0, h, 0:1]))
                line.step(fn(d[:, 1], bb[:, 2], ACT.Exp, scale=-1.0 / GATE, bias=bend[:, 0, h, 2:3]))
                line.step(fn(d[:, 2], bb[:, 0], ACT.Exp, scale=-1.0 / GATE, bias=bend[:, 1, h, 0:1]))
                line.tell(fn(d[:, 3], bb[:, 1], ACT.Exp, scale=-1.0 / GATE, bias=bend[:, 0, h, 1:2]), e_exp, s + 2)
            for c in range(4):
                line.tell(copy(ya_hi[:, c], ya32[:, c]), c_hi, c + 1)
            act.wait_ge(e_qk, FAR + 2 * HG)

            def g_squares(h):
                act.wait_ge(g_o, h + 1)
                for t in range(NT):
                    o = 2048 + 1024 * (h % 2) + DV * t
                    square(psf[:, o:o + DV], t, width=DV, junk=junkG)
                root(4)

            evacuate("gb", 0, 0)
            evacuate("gb", 0, 1)
            g_squares(0)
            evacuate("gb", 0, 2)
            evacuate("gb", 0, 3)
            for h in range(1, HG):
                g_squares(h)
            act.wait_ge(g_o, HG)
            for t in range(NT):
                act.dma_start(x[:, t], out[0, t * P:(t + 1) * P, :]).then_inc(x_in[t], 16)
            for j in range(4):
                evacuate("gb", 1, j)
            y_turn_hi(1, h_hi, lambda c: col("gla", c % 2))
            for c in range(KC):
                act.wait_ge(c_y, c + 1)
                line.tell(copy(mg_hi[:, c], y32[:]), c_hi, 4 + c + 1)
            for t in range(NT):
                act.wait_ge(bank_free[t], GROUP["y2"] + 2)
                square(x[:, t], t)
                root(1)
            turn_hi("turn5", h_hi, 0, lambda c: col("lnffn", c))
            with act.Fori(0, FI) as i:
                for j in range(2):
                    act.wait_ge(f_acc, 2 * i + j + 1)
                    line.tell(fn(facc[j][:], facc[j][:], ACT.Silu), f_silu, 2 * i + j + 1)
                for j in range(2):
                    act.wait_ge(bank_free[2 + j], GROUP["ffn"] + i + 1)
                    line.tell(copy(f_hi[:, bass.ds(2 * i + j, 1)], facc[j][:].unsqueeze(1)), f_hi_done, 2 * i + j + 1)

        @block.vector
        def _(dve):
            line = Line(dve, dve_line)
            seen = {"ss": 0, "root": 0, "src": 0}

            def tt(o, a, b, op):
                return dve.tensor_tensor(o, a, b, op)

            def stt(o, a, sc, b, op0, op1):
                return dve.scalar_tensor_tensor(o, a, sc, b, op0, op1)

            def squared(n=1):
                seen["ss"] += n
                dve.wait_ge(ss_ready, seen["ss"])

            def deviation(width, over, at_=0):
                r = seen["root"] = seen["root"] + 1
                a = slice(0, width)
                line.tell(dve.tensor_scalar(var[:, a], ss[:, at_:at_ + width], 1.0 / over, EPS, ALU.mult, ALU.add),
                          var_ready, r)
                dve.wait_ge(std_ready, r)
                line.step(dve.reciprocal(rs[:, a], std[:, a]))
                line.step(tt(nwt[:, a], rs[:, a], rs[:, a], ALU.mult))
                line.step(tt(nwt[:, a], nwt[:, a], var[:, a], ALU.mult))
                line.step(dve.tensor_scalar(nwt[:, a], nwt[:, a], -0.5, 1.5, ALU.mult, ALU.add))
                line.step(tt(rs[:, a], rs[:, a], nwt[:, a], ALU.mult))

            def src_done(ins):
                seen["src"] += 1
                line.tell(ins, src_ready, seen["src"])

            def turn_lo(name, dst, hi, c0, gname):
                T = TURNS[name]
                for c in range(KC):
                    dve.wait_ge(turned_hi, 8 * T + c + 1)
                    ins = stt(dst[:, c0 + c], ps[:, c], gname(c), hi[:, c0 + c].bitcast(F32), ALU.mult, ALU.subtract)
                    if c < 4:
                        line.tell(ins, bank_free[c], GROUP[name] + 1)
                    else:
                        line.tell(ins, turned_lo, 4 * T + c - 3)

            def scaled(t, k):
                src_done(dve.tensor_scalar(diag[:, t], ident[:], rs[:, k:k + 1], None, ALU.mult))

            line.tell(dve.memset(wgate[:], 0.0), padded, 1)
            for c in range(16):
                line.step(dve.memset(invc[:, c:c + 1], 1.0 / (c + 1)))
            dve.wait_ge(vt_done, 2)
            line.step(dve.tensor_copy(vcol[:, 0:NV1], ps[:, 4, 0:NV1]))
            line.tell(dve.tensor_copy(vcol[:, NV1:], ps[:, 5, 0:NV2]), vcol_ready, 1)

            dve.wait_ge(small_in, 16 * 19)
            line.step(dve.tensor_copy(wg_hi[:], wgate[:]))
            line.tell(tt(wg_lo[:], wgate[:], wg_hi[:].bitcast(F32), ALU.subtract), gate_dve, 1)
            squared(NT)
            deviation(NT, D)
            for t in range(NT):
                scaled(t, t)
            turn_lo("turn0", h_lo, h_hi, 0, lambda c: col("pre", c))

            dve.wait_ge(gate_pe, 1)
            line.tell(dve.tensor_scalar(g_ig[:], ps[0:HA, 4], bias4[:, 0:1], None, ALU.add), gate_dve, 2)
            line.step(dve.tensor_copy(g_lf[:], ps[32:32 + HA, 4]))
            line.tell(dve.tensor_scalar(g_lf[:], g_lf[:], bias4[:, 1:2], None, ALU.add), gate_dve, 3)
            dve.wait_ge(gate_act, 3)
            line.tell(stt(g_lf[:], g_lf[:], 0.0, g_t[:], ALU.min, ALU.subtract), gate_dve, 4)
            line.tell(dve.tensor_tensor_scan(g_b[:], g_lf[:], g_lf[:], 0.0, ALU.add, ALU.bypass), gate_dve, 5)
            line.tell(tt(g_ig[:], g_ig[:], g_b[:], ALU.subtract), gate_dve, 6)
            line.tell(dve.tensor_tensor_scan(g_lf[:], g_ig[:], g_ig[:], 0.0, ALU.max, ALU.bypass), gate_dve, 7)
            line.tell(tt(g_m[:], g_b[:], g_lf[:], ALU.add), gate_dve, 8)
            line.tell(dve.tensor_scalar(g_lf[:], g_lf[:], -1.0, None, ALU.mult), gate_dve, 9)
            dve.wait_ge(gate_pe, 2)
            line.tell(dve.tensor_copy(small[:, 216:232], ps[:, 4, 0:NT * HA]), gate_dve, 10)
            dve.wait_ge(gate_pe, 3)
            line.tell(dve.tensor_copy(small[:, 232:248], ps[:, 5, 0:NT * HA]), gate_dve, 11)

            def convolve(c):
                u, g = UNIT["qa"] + 2 * (c // 4) + 1, GROUP["qa"] + c // 4
                acc, p = (qA if c < 8 else kA)[:, c % 8], ps[:, c % 4]
                dve.wait_ge(steps, 4 * u + c % 4 + 1)
                line.step(dve.tensor_scalar(acc, p, col("convqk", 48 + c), None, ALU.mult))
                for sft in (1, 2, 3):
                    ins = stt(acc[:, sft:], p[:, 0:S - sft], col("convqk", 16 * (3 - sft) + c), acc[:, sft:],
                              ALU.mult, ALU.add)
                    if sft < 3:
                        line.step(ins)
                    else:
                        line.tell(ins, bank_free[c % 4], g + 1)

            def diagonals(t_):
                return (t_[:, SEG_T[0]:SEG_T[0] + P].unsqueeze(1),
                        t_[:, P:].rearrange("p (n c) -> p n c", c=3 * P)[:, :, 2 * P:])

            dve.wait_ge(const_made, 2)
            for h in range(HB):
                dve.wait_ge(b_rest, h + 1)
                for v in diagonals(tB1):
                    line.step(tt(v, v, tri[:].unsqueeze(1).broadcast_to([P, v.shape[1], P]), ALU.max))
                for i in range(NT):
                    r = tB1[:, SEG_T[i]:SEG_T[i] + P * (i + 1)][:, ::-1]
                    line.step(dve.tensor_tensor_scan(r, r, r, 1.0, ALU.mult, ALU.bypass))
                dve.wait_ge(b_beta, h + 1)
                line.step(tt(tB2[:, 0:CAUSAL - 1], tB2[:, 0:CAUSAL - 1], tB1[:, 1:CAUSAL], ALU.mult))
                one, three = diagonals(tB2)
                line.step(tt(one, one, below[:].unsqueeze(1), ALU.mult))
                line.tell(tt(three, three, below[:].unsqueeze(1).broadcast_to([P, 3, P]), ALU.mult), b_a, h + 1)
                if h % 2:
                    for j in range(3):
                        convolve(2 * (h - 1) + j)
                dve.wait_ge(b_o, h + 1)
                line.tell(tt(y32[:], ps[:, 7], szB[:, h], ALU.mult), b_y, h + 1)
                if h % 2:
                    convolve(2 * (h - 1) + 3)
                dve.wait_ge(b_hi, h + 1)
                line.tell(tt(yB_lo[:, h], y32[:], yB_hi[:, h].bitcast(F32), ALU.subtract), b_lo, h + 1)
            line.step(dve.memset(vA[:, :, :, DA:DA + 1], 1.0))

            def a_args(h):
                if h >= 2:
                    dve.wait_ge(a_o, 4 * (h - 1))
                for j in range(NT):
                    w = WA[h % 2][:, A_OFF[j]:A_OFF[j] + S - P * j]
                    line.tell(dve.tensor_scalar(w, nMb[:, h, P * j:], cT[:, j, h:h + 1], 0.0, ALU.add, ALU.min),
                              a_arg, 4 * h + j + 1)

            def a_scores(h):
                for j in range(NT):
                    dve.wait_ge(a_exp, 4 * h + j + 1)
                    w = WA[h % 2][:, A_OFF[j]:A_OFF[j] + S - P * j]
                    line.step(tt(w[:, 0:P], w[:, 0:P], tri[:], ALU.mult))
                    dve.wait_ge(a_s, 4 * h + j + 1)
                    line.tell(stt(w, ps[:, 4 + j, 0:S - P * j], DA ** -0.5, w, ALU.mult, ALU.mult),
                              a_st, 4 * h + j + 1)

            def a_outputs(h):
                dve.wait_ge(a_o, 4 * h + 4)
                line.step(dve.tensor_copy(den, ps[:, 0:4, DA]))
                line.step(stt(rden, den, -1.0, den, ALU.mult, ALU.max))
                line.step(tt(rden, rden, emT[:, :, h], ALU.max))
                line.step(dve.reciprocal(rden, rden))
                for t in range(NT):
                    so = soA[:, t, h * DA:h * DA + DA]
                    line.tell(stt(so, ps[:, t, 0:DA], rden[:, t:t + 1], so, ALU.mult, ALU.mult), bank_free[t],
                              GROUP["a_out"] + h + 1)

            dve.wait_ge(gate_act, 5)
            a_args(0)
            a_args(1)
            a_scores(0)
            for h in range(HA):
                if h + 1 < HA:
                    a_scores(h + 1)
                a_outputs(h)
                if h + 2 < HA:
                    a_args(h + 2)
            squared(16)
            deviation(16, DA)
            for t in range(NT):
                for h in range(HA):
                    so = soA[:, t, h * DA:h * DA + DA]
                    ins = stt(so, so, rs[:, 4 * h + t:4 * h + t + 1], szA[:, t, h * DA:h * DA + DA], ALU.mult, ALU.mult)
                    if h < HA - 1:
                        line.step(ins)
                    else:
                        line.tell(ins, y_src, t + 1)

            def y_turn_lo(use, c, dst, hi, weight):
                n = KC * use + c + 1
                dve.wait_ge(y_hi, n)
                line.tell(stt(dst[:, c], ps[:, 4 + c % 4], weight, hi[:, c].bitcast(F32), ALU.mult, ALU.subtract),
                          y_lo, n)

            for c in range(KC):
                y_turn_lo(0, c, yA_lo, yA_hi, col("hn", c))

            def y_post(name, posts, then):
                g = GROUP[name]
                dve.wait_ge(postg_in, 16 * posts)
                for t in range(NT):
                    squared()
                    line.tell(tt(yg[:, t, 0:512], ps[:, t], postg[:, 0:512], ALU.mult), bank_free[t], g + 1)
                for t in range(NT + 1):
                    squared(1 if t in (0, NT) else 2)
                    if t < NT:
                        line.tell(tt(yg[:, t, 512:], ps[:, t], postg[:, 512:], ALU.mult), bank_free[t], g + 2)
                        line.step(tt(ss[:, 20:21], ss[:, t:t + 1], ss[:, 4 + t:5 + t], ALU.add))
                    a = 21 if t == NT else 20
                    deviation(1 if t in (0, NT) else 2, D, a)
                    if t < NT:
                        dve.wait_ge(x_in[t], 32)
                        line.tell(stt(x[:, t], yg[:, t], rs[:, 0:1], x[:, t], ALU.mult, ALU.add), x_ready,
                                  NT * (posts - 1) + t + 1)
                    if t:
                        scaled(t - 1, 21 - a)
                turn_lo(then[0], h_lo, h_hi, 0, then[1])

            y_post("y0", 1, ("turn2", lambda c: col("pre", 8 + c)))

            for b in range(3):
                line.step(dve.memset(pw[b][:, 0:PAD], 0.0))
            for G in range(4):
                w, u, g = WINDOWS[G], UNIT["mix"] + 5 * G, GROUP["mix"] + 3 * G
                for j in range(4):
                    n = 4 * G + j
                    dve.wait_ge(bank_free[j], g + 1)
                    src = 0
                    for k in range(G + 1):
                        dst = 1 + k % 2
                        line.step(tt(pw[dst][:, PAD:], pw[src][:, PAD:], pw[src][:, PAD - (1 << k):PAD - (1 << k) + S],
                                     ALU.add))
                        src = dst
                    if n:
                        dve.wait_ge(pool_h, n)
                    line.step(tt(pw[3 - src][:, PAD:PAD + w], pw[src][:, PAD:PAD + w], invc[:, 0:w], ALU.mult))
                    line.step(stt(y32[:], pw[src][:, PAD:], 1.0 / w, pw[0][:, PAD:], ALU.mult, ALU.subtract))
                    line.tell(tt(y32[:, 0:w], pw[3 - src][:, PAD:PAD + w], pw[0][:, PAD:PAD + w], ALU.subtract),
                              pool_ready, 2 * n + 1)
                    dve.wait_ge(pool_h, n + 1)
                    line.tell(tt(pool_lo[:, j], y32[:], pool_hi[:, j].bitcast(F32), ALU.subtract), pool_ready, 2 * n + 2)
                    line.tell(dve.memset(pw[0][:, 0:1], 0.0), p_out, n + 1)
                for j in range(4):
                    n = 4 * G + j
                    dve.wait_ge(steps, 4 * (u + 4) + j + 1)
                    dve.wait_ge(bank_free[j], g + 2)
                    line.tell(stt(szC[:, j], ps[:, j], col("pscale", n), szC[:, j], ALU.mult, ALU.mult),
                              bank_free[j], g + 3)
                    dve.wait_ge(m_hi_done, n + 1)
                    line.tell(tt(m_lo[:, n], szC[:, j], m_hi[:, n].bitcast(F32), ALU.subtract), m_lo_done, n + 1)
            y_post("y1", 2, ("turn3", lambda c: col("lnmix", c)))

            dve.wait_ge(lr_in, 32)
            line.step(dve.tensor_copy(wlr_hi[:], wlr[:]))
            line.tell(tt(wlr_lo[:], wlr[:], wlr_hi[:].bitcast(F32), ALU.subtract), l_dve, 1)
            for t in range(NT):
                dve.wait_ge(w_qkv, t + 1)
                line.tell(dve.tensor_reduce(ss[:, 10 * t:10 * t + 10], junk2[:].rearrange("p (h d) -> p h d", d=DH),
                                            AX, ALU.add), w_sq, t + 1)
            deviation(40, DH)
            for t in range(NT):
                r = rs[:, 10 * t:10 * t + 10]
                for c in range(HKV):
                    line.step(tt(
                        qn[:, t, 0:512].rearrange("p (b c d) -> p b c d", c=HKV, d=DH)[:, :, c, :],
                        qkv[:, t, 256 * c:256 * c + 256].rearrange("p (b d) -> p b d", d=DH),
                        r[:, 4 * c:4 * c + 4].unsqueeze(2).broadcast_to([P, 4, DH]), ALU.mult))
                line.tell(tt(qn[:, t, 512:640].rearrange("p (c d) -> p c d", d=DH),
                             qkv[:, t, 512:640].rearrange("p (c d) -> p c d", d=DH),
                             r[:, 8:10].unsqueeze(2).broadcast_to([P, HKV, DH]), ALU.mult), w_n, t + 1)
            line.step(dve.memset(notfirst[:], 1.0))
            line.step(dve.memset(notfirst[:].rearrange("p (b t) -> p b t", t=P)[:, :, 0:1], 0.0))
            dve.wait_ge(l_pe, 1)
            line.tell(dve.tensor_copy(lrT[:], ps[0:RANK, 4]), l_dve, 2)
            for h in range(HG):
                dve.wait_ge(l_pe, 2 + h)
                gt = gtmp[h % 2]
                line.tell(dve.tensor_scalar(gt[:], ps[:, 4 + h], col("bgk", h), None, ALU.add), l_dve, 3 + 2 * h)
                dve.wait_ge(l_act, h + 1)
                line.tell(stt(gt[:], gt[:], 0.0, gln[:], ALU.min, ALU.subtract), l_dve, 4 + 2 * h)
                line.step(dve.tensor_tensor_scan(bG[:, h], notfirst[:], gt[:], 0.0, ALU.mult, ALU.add))
            line.tell(dve.tensor_scalar(bend[:, 0], bG[:].rearrange("p h (b t) -> p h b t", t=P)[:, :, :, P - 1],
                                        1.0 / GATE, None, ALU.mult), l_dve, 11)
            line.tell(tt(bend[:, 1, :, 0:1], bend[:, 0, :, 0:1], bend[:, 0, :, 1:2], ALU.add), l_dve, 12)
            sc4 = psf[:, 2048:3072].rearrange("p (h k) -> p h k", k=2 * P)
            for n in range(2 * NT):
                i, c = n // 2, n % 2
                k0 = 0 if i else P
                nk = 2 * P - k0
                sinks = sinkb[:, 4 * c:4 * c + 4]
                s_ = sm[:, :, k0:]
                dve.wait_ge(w_s, n + 1)
                line.step(stt(s_, sc4[:, :, k0:], DH ** -0.5, band[:, k0:].unsqueeze(1).broadcast_to([P, 4, nk]),
                              ALU.mult, ALU.add))
                line.step(dve.tensor_reduce(wstat[:, 0], s_, AX, ALU.max))
                line.step(tt(wstat[:, 0], wstat[:, 0], sinks, ALU.max))
                line.step(tt(wstat[:, 3], sinks, wstat[:, 0], ALU.subtract))
                line.tell(dve.tensor_scalar(wstat[:, 1], wstat[:, 0], -1.0, None, ALU.mult), w_neg, n + 1)
                dve.wait_ge(w_exp, 5 * n + 5)
                line.step(tt(wstat[:, 2], wstat[:, 2], wstat[:, 3], ALU.add))
                line.step(dve.reciprocal(wstat[:, 2], wstat[:, 2]))
                line.tell(tt(s_, s_, wstat[:, 2].unsqueeze(2).broadcast_to([P, 4, nk]), ALU.mult), w_p, n + 1)

            for h in range(HG):
                dve.wait_ge(e_pe, h + 1)
                line.tell(tt(atD[:, h], ps[:, 4 + h].rearrange("p (b t) -> p b t", t=P),
                             ident[:].unsqueeze(1).broadcast_to([P, 4, P]), ALU.mult), e_at, h + 1)
            for b in range(2):
                line.step(dve.memset(qE[b][:], 0.0))
                line.step(dve.memset(kE[b][:], 0.0))

            def pairs(v, L):
                return v.rearrange("p (a two l) -> p a two l", two=2, l=L)

            def distance(s):
                L, h = LEVELS[s // HG], s % HG
                v = bG[:, h].rearrange("p (a l) -> p a l", l=2 * L)
                line.tell(tt(dG[s % 2][:].rearrange("p (a l) -> p a l", l=2 * L), v,
                             v[:, :, L - 1:L].broadcast_to([P, S // (2 * L), 2 * L]), ALU.subtract), e_d, s + 1)

            def weighted(s):
                L, h = LEVELS[s // HG], s % HG
                dve.wait_ge(e_exp, s + 1)
                if s >= 2:
                    dve.wait_ge(e_pe, HG + s - 1)
                d = pairs(dG[s % 2][:], L)
                line.step(tt(pairs(qE[s % 2][:], L)[:, :, 1], pairs(qG[:, h], L)[:, :, 1], d[:, :, 1], ALU.mult))
                line.tell(tt(pairs(kE[s % 2][:], L)[:, :, 0], pairs(kG[:, h], L)[:, :, 0], d[:, :, 0], ALU.mult),
                          e_qk, s + 1)

            def take(s):
                n, h = s // HG, s % HG
                dve.wait_ge(e_pe, HG + s + 1)
                line.tell(dve.copy_predicated(atD[:, h], level[:, n].unsqueeze(1).broadcast_to([P, 4, P]).bitcast(I32),
                                              ps[:, 4 + s % 4].rearrange("p (b t) -> p b t", t=P)), e_at, HG + s + 1)

            for s in range(STEPS_NEAR + 2):
                if s < STEPS_NEAR:
                    distance(s)
                if 1 <= s <= STEPS_NEAR:
                    weighted(s - 1)
                if s >= 2:
                    take(s - 2)
            def blocks(v):
                return v.rearrange("p (b t) -> p b t", t=P)

            for h in range(HG):
                s, b = FAR + 2 * h, h % 2
                dve.wait_ge(e_exp, s + 1)
                dve.wait_ge(e_pe, HG + FAR + max(0, h - 1))
                line.step(tt(blocks(qE[b][:])[:, 0:2], blocks(qG[:, h])[:, 1::2], blocks(dG[0][:])[:, 0:2], ALU.mult))
                line.tell(tt(blocks(qE[b][:])[:, 2:4], blocks(qG[:, h])[:, 2:4], blocks(dG[0][:])[:, 2:4], ALU.mult),
                          e_qk, s + 1)
                dve.wait_ge(e_exp, s + 2)
                line.step(tt(blocks(kE[b][:])[:, 0:2], blocks(kG[:, h])[:, 0::2], blocks(dG[1][:])[:, 0:2], ALU.mult))
                line.tell(tt(blocks(kE[b][:])[:, 2:4], blocks(kG[:, h])[:, 0:2], blocks(dG[1][:])[:, 2:4], ALU.mult),
                          e_qk, s + 2)
                if h >= 1:
                    dve.wait_ge(e_pe, HG + FAR + h)
                    line.tell(dve.tensor_copy(atO[:, h - 1].rearrange("p b t -> p (b t)"),
                                              psf[:, 2048 + 1024 * ((h - 1) % 2):2048 + 1024 * ((h - 1) % 2) + 768]),
                              e_at, HG + FAR + h)
            dve.wait_ge(e_pe, HG + FAR + HG)
            line.tell(dve.tensor_copy(atO[:, HG - 1].rearrange("p b t -> p (b t)"),
                                      psf[:, 2048 + 1024:2048 + 1024 + 768]), e_at, HG + FAR + HG)
            for c in range(4):
                dve.wait_ge(c_hi, c + 1)
                line.tell(tt(ya_lo[:, c], ya32[:, c], ya_hi[:, c].bitcast(F32), ALU.subtract), c_lo, c + 1)
            for h in range(HG):
                squared(4)
                deviation(4, DV)
                for t in range(NT):
                    r_ = rG[:, t, h * DV:h * DV + DV]
                    o = 2048 + 1024 * (h % 2) + DV * t
                    ins = stt(r_, psf[:, o:o + DV], rs[:, t:t + 1], r_, ALU.mult, ALU.mult)
                    if h < HG - 1:
                        if t < NT - 1:
                            line.step(ins)
                        else:
                            line.tell(ins, g_taken, h + 1)
                    else:
                        line.tell(ins, y_src, NT + t + 1)

            def branch_a(c):
                u, g, j = UNIT["bra"] + c // 4, GROUP["bra"] + c // 4, c % 4
                dve.wait_ge(steps, 4 * u + j + 1)
                line.tell(tt(sga[:, c], ps[:, j], sga[:, c], ALU.mult), bank_free[j], g + 1)

            for c0 in (0, 4):
                for c in range(c0, c0 + 4):
                    y_turn_lo(1, c, h_lo, h_hi, col("gla", c % 2))
                for c in range(c0, c0 + 4):
                    branch_a(c)
            for c in range(KC):
                u, g, j = UNIT["brb"] + 2 * (c // 4) + 1, GROUP["brb"] + c // 4, c % 4
                dve.wait_ge(steps, 4 * u + j + 1)
                line.tell(tt(sgb[:, c], ps[:, j], sgb[:, c], ALU.mult), bank_free[j], g + 1)
                line.tell(tt(y32[:], sgb[:, c], sga[:, c], ALU.add), c_y, c + 1)
                dve.wait_ge(c_hi, 4 + c + 1)
                line.tell(tt(mg_lo[:, c], y32[:], mg_hi[:, c].bitcast(F32), ALU.subtract), c_lo, 4 + c + 1)

            def normed(t):
                squared()
                deviation(1, D, t)
                scaled(t, 0)

            def residual(name, per):
                for n in range(2):
                    for t in range(NT):
                        dve.wait_ge(steps, 4 * (UNIT[name] + per * n + per - 1) + t + 1)
                        xs = x[:, t, 512 * n:512 * n + 512]
                        if name == "y2" and n == 0:
                            dve.wait_ge(x_in[t], 48)
                        line.tell(tt(xs, xs, ps[:, t], ALU.add), bank_free[t], GROUP[name] + n + 1)
                        if name == "y2" and n and t:
                            normed(t - 1)

            residual("y2", 2)
            normed(NT - 1)
            turn_lo("turn5", h_lo, h_hi, 0, lambda c: col("lnffn", c))

            for i in range(FI):
                for j in range(2):
                    c = 2 * i + j
                    dve.wait_ge(steps, 4 * (UNIT["ffn"] + 2 * i + 1) + j + 1)
                    line.step(dve.tensor_scalar(facc[j][:], ps[:, j], col("cw", 44 + c), col("cb", c), ALU.mult, ALU.add))
                    line.step(stt(facc[j][:, 1:], ps[:, j, 0:S - 1], col("cw", 22 + c), facc[j][:, 1:], ALU.mult, ALU.add))
                    line.step(stt(facc[j][:, 2:], ps[:, j, 0:S - 2], col("cw", c), facc[j][:, 2:], ALU.mult, ALU.add))
                    line.tell(dve.memset(spare[:, 4 + j:5 + j], 0.0), f_acc, 2 * i + j + 1)
                    line.tell(dve.memset(spare[:, 6 + j:7 + j], 0.0), bank_free[j], GROUP["ffn"] + i + 1)
                for j in range(2):
                    c = 2 * i + j
                    dve.wait_ge(steps, 4 * (UNIT["ffn"] + 2 * i + 1) + 2 + j + 1)
                    dve.wait_ge(f_silu, c + 1)
                    line.tell(tt(facc[j][:], ps[:, 2 + j], facc[j][:], ALU.mult), bank_free[2 + j], GROUP["ffn"] + i + 1)
                    dve.wait_ge(f_hi_done, c + 1)
                    line.tell(tt(f_lo[:, c], facc[j][:], f_hi[:, c].bitcast(F32), ALU.subtract), f_lo_done, c + 1)
            residual("y3", 6)

        @block.tensor
        def _(pe):
            def mm(o, l, r, start=True, stop=True):
                return pe.matmul(o, l, r, start=start, stop=stop)

            def unit(slot, mode, act, k0, nk, first, last, u, g, width=512, after={}):
                pe.wait_ge(split_ready, u + 1)
                n_mm = 3 * nk
                for j in range(4):
                    if first:
                        pe.wait_ge(bank_free[j], g)
                    n = 0
                    for kk in range(nk):
                        a_hi, a_lo = act(k0 + kk)
                        w_hi, w_lo = whi[slot][:, kk], wlo[slot][:, kk]
                        for w, a in ((w_hi, a_hi), (w_hi, a_lo), (w_lo, a_hi)):
                            if mode == "F":
                                ins = mm(ps[:, j], w[:, j * P:j * P + P], a, first and n == 0, last and n == n_mm - 1)
                            else:
                                ins = mm(ps[:, j, 0:width], a[:, j * P:j * P + P], w[:, 0:width],
                                         first and n == 0, last and n == n_mm - 1)
                            n += 1
                    ins.then_inc(steps, 1)
                    if j in after:
                        after[j]()

            def groups(name, mode, act, width=512, total=None, waits=None):
                n, per = next((n, per) for m, n, per in PLAN if m == name)
                total = total or 4 * per

                def one(i):
                    for q in range(per):
                        if waits:
                            waits(q)
                        unit((UNIT[name] + q + (per % 2) * (i if isinstance(i, int) else 0)) % 2, mode, act, 4 * q,
                             min(4, total - 4 * q), q == 0, q == per - 1, UNIT[name] + i * per + q, GROUP[name] + i,
                             width)
                if n > 1 and per % 2 == 0:
                    with pe.Fori(0, n) as i:
                        one(i)
                else:
                    for i in range(n):
                        one(i)

            def h_parts(k):
                return h_hi[:, k], h_lo[:, k]

            seen = {"src": 0}

            def turn(name):
                g = GROUP[name]
                for t in range(NT):
                    seen["src"] += 1
                    pe.wait_ge(src_ready, seen["src"])
                    for c in range(KC):
                        if t == 0 and c < 4 and g:
                            pe.wait_ge(bank_free[c], g)
                        ins = mm(ps[:, c, t * P:t * P + P], x[:, t, c * P:c * P + P], diag[:, t])
                        if t == NT - 1:
                            ins.then_inc(turned_pe, 1)

            def first_unit(name, after, mode):
                for j in range(4):
                    pe.wait_ge(bank_free[j], GROUP[after] + 1)
                unit(UNIT[name] % 2, mode, h_parts, 0, 4, True, False, UNIT[name], GROUP[name])
                pe.wait_ge(turned_lo, 4 * TURNS[after] + 4)

            pe.wait_ge(const_made, 1)
            pe.wait_ge(small_in, 16 * 19)
            pe.transpose(ps[:, 4, 0:NV1], rawv[:, 0, :], ident[:]).then_inc(vt_done, 1)
            pe.transpose(ps[:, 5, 0:NV2], rawv[0:NV2, 1, :], ident[0:NV2, 0:NV2]).then_inc(vt_done, 1)
            pe.wait_ge(vcol_ready, 1)

            turn("turn0")

            def thin(w_hi, w_lo, n):
                k2 = 0
                for k in range(KC):
                    for w, a in ((w_hi, h_hi), (w_hi, h_lo), (w_lo, h_hi)):
                        ins = mm(ps[0:n, 4], w[:, k], a[:, k], k2 == 0, k2 == 3 * KC - 1)
                        k2 += 1
                return ins

            first_unit("qb", "turn0", "F")
            pe.wait_ge(gate_dve, 1)
            thin(wg_hi, wg_lo, 36).then_inc(gate_pe, 1)
            unit(1, "F", h_parts, 4, 4, False, True, UNIT["qb"] + 1, GROUP["qb"])
            for q in range(2):
                unit(q, "F", h_parts, 4 * q, 4, q == 0, q == 1, UNIT["qb"] + 2 + q, GROUP["qb"] + 1)
            groups("kb", "F", h_parts)
            unit(0, "T", h_parts, 0, 4, True, False, UNIT["vb"], GROUP["vb"])
            pe.wait_ge(gate_act, 4)
            for b, rows_ in ((4, g_ig), (5, g_t)):
                for t in range(NT):
                    ins = pe.transpose(ps[:, b, t * HA:t * HA + HA], rows_[:, t * P:t * P + P], ident[0:HA, 0:HA])
                ins.then_inc(gate_pe, 1)
            unit(1, "T", h_parts, 4, 4, False, True, UNIT["vb"] + 1, GROUP["vb"])
            for q in range(2):
                unit(q, "T", h_parts, 4 * q, 4, q == 0, q == 1, UNIT["vb"] + 2 + q, GROUP["vb"] + 1)
            groups("zb", "F", h_parts)

            def b_scores(h):
                if h:
                    pe.wait_ge(b_copied, h)
                else:
                    pe.wait_ge(gate_dve, 11)
                for i in range(NT):
                    a = 2048 + SEG_T[i]
                    ins = mm(psf[:, a:a + P * (i + 1)], qB[:, h, i * P:i * P + P], kB[:, h, 0:P * (i + 1)])
                ins.then_inc(b_z, 1)

            def b_transpose(h):
                pe.wait_ge(b_a, h + 1)
                for j in range(NT):
                    for i in range(j, NT):
                        a, o = SEG_T[i] + j * P, 2048 + SEG_S[j] + (i - j) * P
                        ins = pe.transpose(psf[:, o:o + P], tB2[:, a:a + P], ident[:])
                ins.then_inc(b_t, 1)

            def b_outputs(h):
                pe.wait_ge(b_copied, h + 1)
                if h:
                    pe.wait_ge(b_y, h)
                for j in range(NT):
                    ins = mm(ps[:, 7, P * j:], vB[:, j, h * DB:h * DB + DB], aTB[:, SEG_S[j]:SEG_S[j] + S - P * j],
                             j == 0, j == NT - 1)
                ins.then_inc(b_o, 1)

            b_scores(0)
            for h in range(HB):
                q = h % 2
                unit(q, "F", h_parts, 4 * q, 4, q == 0, q == 1, UNIT["qa"] + h, GROUP["qa"] + h // 2,
                     after={2: lambda: b_transpose(h)})
                b_outputs(h)
                if h + 1 < HB:
                    b_scores(h + 1)
            groups("va", "T", h_parts)
            groups("oa", "T", h_parts)
            groups("za", "T", h_parts)

            def a_scores(h):
                for j in range(NT):
                    if h:
                        pe.wait_ge(a_st, 4 * h - 4 + j + 1)
                    for c in range(2):
                        ins = mm(ps[:, 4 + j, 0:S - P * j], kA[:, 2 * h + c, j * P:j * P + P], qA[:, 2 * h + c, P * j:],
                                 c == 0, c == 1)
                    ins.then_inc(a_s, 1)

            def a_outputs(h):
                pe.wait_ge(a_st, 4 * h + 4)
                for t in range(NT):
                    pe.wait_ge(bank_free[t], GROUP["a_out"] + h)
                    for j in range(t + 1):
                        a = A_OFF[j] + (t - j) * P
                        ins = mm(ps[:, t, 0:DA + 1], WA[h % 2][:, a:a + P], vA[:, j, h], j == 0, j == t)
                    ins.then_inc(a_o, 1)

            pe.wait_ge(b_y, HB)
            for h in range(HA):
                mm(ps[:, 4 + h], sel[:, h, :], g_lf[:]).then_inc(gate_pe, 1)
            pe.wait_ge(qk_ready, 16)
            pe.wait_ge(gate_act, 5)
            a_scores(0)
            for h in range(HA):
                if h + 1 < HA:
                    a_scores(h + 1)
                a_outputs(h)

            def y_turn(use, half, src):
                for t in range(NT):
                    pe.wait_ge(y_src, NT * use + t + 1)
                    for c in range(4 * half, 4 * half + 4):
                        if half and t == 0:
                            pe.wait_ge(y_lo, KC * use + c - 3)
                        ins = pe.transpose(ps[:, 4 + c % 4, t * P:t * P + P], src[:, t, c * P:c * P + P], ident[:])
                        if t == NT - 1:
                            ins.then_inc(y_turned, 1)

            def y0_parts(k):
                return (yB_hi[:, k], yB_lo[:, k]) if k < HB else (yA_hi[:, k - HB], yA_lo[:, k - HB])

            pe.wait_ge(b_lo, HB)
            for n in range(2):
                for q in range(4):
                    if n == 0 and q >= 2:
                        pe.wait_ge(y_lo, 4 * q - 4)
                    unit(q % 2, "T", y0_parts, 4 * q, 4, q == 0, q == 3, UNIT["y0"] + 4 * n + q, GROUP["y0"] + n,
                         after={1: lambda: y_turn(0, 0, soA), 3: lambda: y_turn(0, 1, soA)} if n == 0 and q == 1 else {})
            turn("turn2")

            def pool_parts(k):
                return pool_hi[:, k], pool_lo[:, k]

            for G in range(4):
                u, g = UNIT["mix"] + 5 * G, GROUP["mix"] + 3 * G
                for q in range(4):
                    if G == 0 and q == 0:
                        first_unit("mix", "turn2", "F")
                        continue
                    unit((u + q) % 2, "F", h_parts, 4 * (q % 2), 4, q % 2 == 0, q % 2 == 1, u + q, g + q // 2)
                pe.wait_ge(pool_ready, 8 * (G + 1))
                unit(u % 2, "F", pool_parts, 0, 4, True, True, u + 4, g + 2)
            pe.wait_ge(m_lo_done, 16)
            groups("y1", "T", lambda k: (m_hi[:, k], m_lo[:, k]))
            turn("turn3")

            first_unit("wq", "turn3", "T")
            unit(1, "T", h_parts, 4, 4, False, True, UNIT["wq"] + 1, GROUP["wq"])
            groups("wkv", "T", h_parts, width=256)
            def pair(name, n, q, mode, after={}):
                unit(q, mode, h_parts, 4 * q, 4, q == 0, q == 1, UNIT[name] + 2 * n + q, GROUP[name] + n, after=after)

            pair("gq", 0, 0, "F")
            pe.wait_ge(l_dve, 1)
            thin(wlr_hi, wlr_lo, RANK).then_inc(l_pe, 1)
            pair("gq", 0, 1, "F")
            pe.wait_ge(l_dve, 2)
            for h in range(HG):
                mm(ps[:, 4 + h], wup[:, h * DK:h * DK + DK], lrT[:]).then_inc(l_pe, 1)
            pair("gk", 0, 0, "F")
            pe.wait_ge(w_n, NT)
            for b in range(5):
                if b < 4:
                    pe.wait_ge(l_dve, 3 + 2 * b)
                else:
                    pe.wait_ge(w_qk, 1)
                for t in range(NT):
                    ins = pe.transpose(ps[:, 4 + b % 4, t * P:t * P + P], qn[:, t, b * P:b * P + P], ident[:])
                ins.then_inc(w_tp, 1)
            pair("gk", 0, 1, "F")

            def w_scores(n):
                i, c = n // 2, n % 2
                k0 = (i - 1) * P if i else 0
                for b in range(4):
                    o = psf[:, 2048 + 256 * b + (0 if i else P):2048 + 256 * b + 256]
                    ins = mm(o, qkT[DH * c:DH * c + DH, b, i * P:i * P + P], qkT[DH * c:DH * c + DH, 4, k0:(i + 1) * P])
                ins.then_inc(w_s, 1)

            def w_transpose(n):
                pe.wait_ge(w_p, n + 1)
                if n:
                    pe.wait_ge(w_ya, 2 * n)
                for kb in range(0 if n >= 2 else 1, 2):
                    for b in range(4):
                        ins = pe.transpose(ps[:, 6 + kb, b * P:b * P + P], sm[:, b, kb * P:kb * P + P], ident[:])
                ins.then_inc(w_t, 1)

            def w_outputs(n):
                i, c = n // 2, n % 2
                pe.wait_ge(w_copied, n + 1)
                for kb in range(0 if i else 1, 2):
                    v = qkv[:, i - 1 + kb, 640 + DH * c:640 + DH * c + DH]
                    ins = mm(ps[0:DH, 6], v, pT[:, kb].rearrange("p b q -> p (b q)"), kb == (0 if i else 1), kb == 1)
                ins.then_inc(w_o, 1)

            pe.wait_ge(w_qk, 5)
            w_scores(0)
            for n in range(2 * NT):
                pair("gv" if n < 4 else "gr", n // 2 % 2, n % 2, "T", after={2: lambda: w_transpose(n)})
                w_outputs(n)
                if n + 1 < 2 * NT:
                    w_scores(n + 1)

            pe.wait_ge(w_ya, 4 * NT)
            for h in range(HG):
                for b in range(NT):
                    ins = mm(ps[:, 4 + h, b * P:b * P + P], kG[:, h, b * P:b * P + P], qG[:, h, b * P:b * P + P])
                ins.then_inc(e_pe, 1)

            def level_steps(slot):
                for s in range(near_steps(slot), near_steps(slot + 1)):
                    pe.wait_ge(e_qk, s + 1)
                    pe.wait_ge(e_at, s + 1)
                    for b in range(NT):
                        ins = mm(ps[:, 4 + s % 4, b * P:b * P + P], kE[s % 2][:, b * P:b * P + P],
                                 qE[s % 2][:, b * P:b * P + P])
                    ins.then_inc(e_pe, 1)

            for u in range(4):
                pair("ga", u // 2, u % 2, "F", after={j: lambda j=j: level_steps(4 * u + j) for j in range(4)})

            def far_products(h):
                o, b = 2048 + 1024 * (h % 2), h % 2
                pe.wait_ge(e_qk, FAR + 2 * h + 2)
                pe.wait_ge(e_at, HG + FAR + max(0, h - 1))
                mm(psf[:, o:o + P], kE[b][:, 0:P], qE[b][:, 0:P])
                mm(psf[:, o + P:o + 2 * P], kE[b][:, P:2 * P], qE[b][:, P:2 * P])
                mm(psf[:, o + 2 * P:o + 4 * P], kE[b][:, 2 * P:3 * P], qE[b][:, 2 * P:])
                mm(psf[:, o + 4 * P:o + 6 * P], kE[b][:, 3 * P:], qE[b][:, 2 * P:]).then_inc(e_pe, 1)

            far_block = {(0, 1): 0, (2, 3): 1, (0, 2): 2, (0, 3): 3, (1, 2): 4, (1, 3): 5}

            def g_outputs(h):
                pe.wait_ge(e_at, HG + FAR + HG)
                if h >= 2:
                    pe.wait_ge(g_taken, h - 1)
                for t in range(NT):
                    o = 2048 + 1024 * (h % 2) + DV * t
                    for j in range(t + 1):
                        w = atD[:, h, t] if j == t else atO[:, h, far_block[j, t]]
                        ins = mm(psf[:, o:o + DV], w, vG[:, j, h * DV:h * DV + DV], j == 0, j == t)
                ins.then_inc(g_o, 1)

            pair("gb", 0, 0, "F", after={j: lambda j=j: far_products(j) for j in range(4)})
            pair("gb", 0, 1, "F", after={1: lambda: g_outputs(0), 3: lambda: g_outputs(1)})
            pair("gb", 1, 0, "F", after={1: lambda: g_outputs(2), 3: lambda: g_outputs(3)})
            pair("gb", 1, 1, "F")

            def ya_parts(k):
                return ya_hi[:, k], ya_lo[:, k]

            pe.wait_ge(y_src, 2 * NT)
            y_turn(1, 0, rG)
            pe.wait_ge(c_lo, 4)
            for n in range(2):
                unit(n, "F", ya_parts, 0, 4, True, True, UNIT["bra"] + n, GROUP["bra"] + n,
                     after={3: lambda: y_turn(1, 1, rG)} if n == 0 else {})
            pe.wait_ge(y_lo, 2 * KC)
            groups("brb", "F", h_parts)
            pe.wait_ge(c_lo, 4 + KC)
            groups("y2", "T", lambda k: (mg_hi[:, k], mg_lo[:, k]))
            turn("turn5")
            first_unit("ffn", "turn5", "F")
            unit(1, "F", h_parts, 4, 4, False, True, UNIT["ffn"] + 1, GROUP["ffn"])
            with pe.Fori(1, FI) as i:
                for q in range(2):
                    unit(q, "F", h_parts, 4 * q, 4, q == 0, q == 1, UNIT["ffn"] + i * 2 + q, GROUP["ffn"] + i)
            pe.wait_ge(f_lo_done, FC)
            groups("y3", "T", lambda k: (f_hi[:, k], f_lo[:, k]), total=FC)
        if dbg:
            return dict(locals())


_INS = ["x", "pre_norm_g", "post_norm_g", "w_in_ab", "conv_qk", "bias_i", "bias_f", "head_norm_g", "w_out_ab",
        "w_in_c", "pool_w", "pool_scale", "w_out_c", "ln_mix_g_2", "w_in_2", "q_norm_g_2", "k_norm_g_2", "sinks_2",
        "w_gk_up_2", "b_gk_2", "gla_norm_g_2", "w_branch_a_2", "w_branch_b_2", "w_out_2", "ln_ffn_g_2",
        "w_ffn_in_2", "conv_w_2", "conv_b_2", "w_ffn_out_2"]


def kernel(**inputs):
    import concourse.bacc as bacc
    from concourse.bass_utils import run_bass_kernel_spmd

    nc = bacc.Bacc("TRN2", target_bir_lowering=False, num_devices=1)
    arrays, A = {}, {}
    for name in _INS:
        a = np.ascontiguousarray(inputs[name])
        arrays[f"in_{name}"] = a
        A[name] = nc.dram_tensor(f"in_{name}", a.shape, mybir.dt.from_np(a.dtype), kind="ExternalInput").ap()
    out = nc.dram_tensor("out_x", (1, S, D), F32, kind="ExternalOutput").ap()
    build(nc, A, out)
    r = run_bass_kernel_spmd(nc, [arrays], core_ids=[0])
    return r.results[0]["out_x"]
```

```python
from contextlib import ExitStack

import numpy as np

import concourse.bass as bass
from concourse import mybir

F32 = mybir.dt.float32
F32R = mybir.dt.float32r
I32 = mybir.dt.int32
ALU = mybir.AluOpType
ACT = mybir.ActivationFunctionType
AX = mybir.AxisListType.X

P = 128
S = 512
NT = S // P
D = 1024
KC = D // P
EPS = 1e-6
KB = 1024

HA, DA = 4, 256
HB, DB = 8, 128
WINDOWS = (2, 4, 8, 16)
HKV, DH = 2, 64
HG, DK, DV, RANK = 4, 128, 256, 16
GATE = 16.0
LEVELS = (64, 32, 16, 8, 4, 2, 1)
DFF = 2816
FC = DFF // P
FI = FC // 2

PLAN = [
    ("turn0", 1, 0),
    ("qb", 2, 2), ("kb", 2, 2), ("vb", 2, 2), ("zb", 2, 2),
    ("qa", 2, 2), ("ka", 2, 2), ("va", 2, 2), ("oa", 2, 2), ("za", 2, 2),
    ("a_out", HA, 0),
    ("y0", 2, 4), ("turn2", 1, 0),
    ("mix", 4, 5),
    ("y1", 2, 4), ("turn3", 1, 0),
    ("wq", 1, 2), ("wkv", 1, 2), ("gq", 1, 2), ("gk", 1, 2),
    ("gv", 2, 2), ("gr", 2, 2), ("ga", 2, 2), ("gb", 2, 2),
    ("bra", 2, 1), ("brb", 2, 2), ("y2", 2, 2), ("turn5", 1, 0),
    ("ffn", FI, 2), ("y3", 2, 6),
]
UNIT, GROUP = {}, {}
_u = _g = 0
for _name, _n, _per in PLAN:
    UNIT[_name], GROUP[_name] = _u, _g
    _u += _n * _per
    _g += _n * (3 if _name == "mix" else 1)
UNITS = _u
assert UNITS % 2 == 0
TURNS = {"turn0": 0, "turn2": 1, "turn3": 2, "turn5": 3}

VECS = [("pre", 16), ("lnmix", 8), ("lnffn", 8), ("convqk", 64), ("pscale", 16), ("bgk", 4),
        ("hn", 8), ("qn", 1), ("kn", 1), ("gla", 2)]
VECS2 = [("cw", 66), ("cb", 22)]
COL = {}
_c = 0
for _name, _n in VECS + VECS2:
    COL[_name] = _c
    _c += _n
NV1 = sum(n for _, n in VECS)
NV2 = sum(n for _, n in VECS2)
assert NV1 == P

IN_AB_B = 5 * D + 2 * HA
C2 = {"qa": 0, "kv": 512, "gq": 768, "gk": 1280, "gv": 1792, "gr": 2816, "lr": 3840, "ga": 3856, "gb": 4880}
SEG_T = {3: 0, 2: 512, 0: 896, 1: 1024}
SEG_S = {0: 0, 1: 512, 3: 896, 2: 1024}
CAUSAL = 1280


A_OFF = (0, 512, 896, 1152)
STEPS_NEAR = len(LEVELS) * HG // 2
FAR = STEPS_NEAR


def near_steps(slot):
    return STEPS_NEAR * slot // 16


def rounds():
    blocks = [(), (0,), (1, 2), (3,), (), ()]
    return [(blocks[r], blocks[r - 1], blocks[r + 1]) for r in range(1, 5)]


class Line:

    def __init__(self, engine, sem):
        self.engine, self.sem, self.base, self.k = engine, sem, 0, 0

    def step(self, ins):
        ins.then_inc(self.sem, 1)
        self.k += 1
        self.engine.wait_ge(self.sem, self.base + self.k)

    def tell(self, ins, sem, value):
        ins.then_inc(sem, 1)
        self.engine.wait_ge(sem, value)


def build(nc, A, out):
    with ExitStack() as ctx:
        def sem(name):
            return ctx.enter_context(nc.semaphore(name))

        base = (nc.sbuf_base + 31) // 32 * 32

        def at(name, shape, dtype, kb):
            off = base + int(kb * KB) // 32 * 32
            return nc.alloc_sbuf_tensor_at(name, shape, dtype, offset=off)

        raw = [at(f"raw{s}", [P, 4, 512], F32, 8 * s) for s in range(2)]
        whi = [at(f"whi{s}", [P, 4, 512], F32R, 16 + 8 * s) for s in range(2)]
        wlo = [at(f"wlo{s}", [P, 4, 512], F32R, 32 + 8 * s) for s in range(2)]
        h_hi = at("h_hi", [P, KC, S], F32R, 48)
        h_lo = at("h_lo", [P, KC, S], F32R, 64)
        x = at("x", [P, NT, D], F32, 80)
        C0 = 96
        ident = at("ident", [P, P], F32, C0)
        tri = at("tri", [P, P], F32, C0 + .5)
        below = at("below", [P, P], F32, C0 + 1)
        band = at("band", [P, 2 * P], F32, C0 + 1.5)
        level = at("level", [P, 7, P], F32, C0 + 2.5)
        vcol = at("vcol", [P, NV1 + NV2], F32, C0 + 6)
        invc = at("invc", [P, 16], F32, C0 + 6.875)
        small = at("small", [P, 256], F32, C0 + 7)
        postg = at("postg", [P, D], F32, C0 + 8)
        g_lf = at("g_lf", [HA, S], F32, C0 + 8)
        sel = at("sel", [HA, HA, P], F32, C0 + 10)
        y32 = at("y32", [P, S], F32, C0 + 12)
        AR = C0 + 14
        ss, var, std, rs, nwt = (small[:, 40 * i:40 * i + 40] for i in range(5))
        sinkb = small[:, 200:208]
        den, rden = small[:, 208:212], small[:, 212:216]
        cT = small[:, 216:232].rearrange("p (t h) -> p t h", h=HA)
        emT = small[:, 232:248].rearrange("p (t h) -> p t h", h=HA)
        spare = small[:, 248:256]
        diag = at("diag", [P, NT, P], F32, AR + 80)
        yg = at("yg", [P, NT, D], F32, AR + 64)
        g_ig, g_t, g_b, g_m = (at(n, [HA, S], F32, AR + 82 + 2 * i)
                               for i, n in enumerate(("g_ig", "g_t", "g_b", "g_m")))
        wgate = at("wgate", [P, KC, 36], F32, AR + 16)
        wg_hi = at("wg_hi", [P, KC, 36], F32R, AR + 18)
        wg_lo = at("wg_lo", [P, KC, 36], F32R, AR + 20)
        bias4 = at("bias4", [HA, 2], F32, AR + 92.75)
        qB = at("qB", [P, HB, S], F32, AR + 32)
        kB = at("kB", [P, HB, S], F32, AR + 48)
        yB_hi = at("yB_hi", [P, HB, S], F32R, AR + 32)
        yB_lo = at("yB_lo", [P, HB, S], F32R, AR + 48)
        vB = at("vB", [P, NT, D], F32, 80)
        szB = at("szB", [P, HB, S], F32, AR + 64)
        tB1 = at("tB1", [P, CAUSAL], F32, AR + 80)
        tB2 = at("tB2", [P, CAUSAL], F32, AR + 85)
        aTB = at("aTB", [P, CAUSAL], F32, AR + 90)
        qA = at("qA", [P, KC, S], F32, AR)
        kA = at("kA", [P, KC, S], F32, AR + 16)
        soA = at("soA", [P, NT, D], F32, AR + 64)
        vA = at("vA", [P, NT, HA, DA + 1], F32, AR + 80)
        szA = at("szA", [P, NT, D], F32, 80)
        WA = [at(f"WA{b}", [P, CAUSAL], F32, 48 + 5 * b) for b in range(2)]
        junkA = at("junkA", [P, DA], F32, 60)
        nMb = at("nMb", [P, HA, S], F32, 64)
        yA_hi = at("yA_hi", [P, KC, S], F32R, AR)
        yA_lo = at("yA_lo", [P, KC, S], F32R, AR + 16)
        rawv = at("rawv", [P, 2, P], F32, AR + 72)
        junk = at("junk", [P, D], F32, AR + 93.75)
        notfirst = at("notfirst", [P, S], F32, AR)
        m_hi = at("m_hi", [P, 16, S], F32R, AR)
        m_lo = at("m_lo", [P, 16, S], F32R, AR + 32)
        pool_hi = at("pool_hi", [P, 4, S], F32R, AR + 64)
        pool_lo = at("pool_lo", [P, 4, S], F32R, AR + 72)
        PAD = 16
        pw = [at(f"pw{b}", [P, PAD + S], F32, AR + 80 + 2.0625 * b) for b in range(3)]
        pin = [pw[0], at("pw3", [P, PAD + S], F32, AR + 94.25)]
        szC = at("szC", [P, 4, S], F32, AR + 86.25)
        ya32 = at("ya32", [P, 4, S], F32, AR)
        qG = at("qG", [P, HG, S], F32, AR + 8)
        kG = at("kG", [P, HG, S], F32, AR + 16)
        bG = at("bG", [P, HG, S], F32, AR + 24)
        vG = at("vG", [P, NT, D], F32, 80)
        rG = at("rG", [P, NT, D], F32, AR + 48)
        atD = at("atD", [P, HG, 4, P], F32, AR + 64)
        atO = at("atO", [P, HG, 6, P], F32, AR + 72)
        dG = [at(f"dG{b}", [P, S], F32, AR + 84 + 2 * b) for b in range(2)]
        qE = [at(f"qE{b}", [P, S], F32, AR + 88 + 2 * b) for b in range(2)]
        kE = [at(f"kE{b}", [P, S], F32, AR + 92 + 2 * b) for b in range(2)]
        dN = [at(f"dN{b}", [P, 2, S], F32, AR + 76 - 4 * b) for b in range(2)]
        qN = [at(f"qN{b}", [P, 2, S], F32, AR + 80 + 4 * b) for b in range(2)]
        kN = [at(f"kN{b}", [P, 2, S], F32, AR + 88 + 4 * b) for b in range(2)]
        qkT = at("qkT", [P, 5, S], F32, AR + 32)
        junk2 = at("junk2", [P, 5 * P], F32, AR + 36)
        sm = at("sm", [P, 4, 2 * P], F32, AR + 42)
        lrT = at("lrT", [RANK, S], F32, AR + 46)
        qkv = at("qkv", [P, NT, 768], F32, AR + 64)
        qn = at("qn", [P, NT, 640], F32, AR + 76)
        wup = at("wup", [RANK, HG * DK], F32, AR + 86)
        gtmp = at("gtmp", [P, HG, S], F32, AR + 88)
        pT = at("pT", [P, 2, 4, P], F32, AR + 84)
        wlr = at("wlr", [P, KC, RANK], F32, AR + 96.25)
        wlr_hi = at("wlr_hi", [P, KC, RANK], F32R, AR + 45)
        wlr_lo = at("wlr_lo", [P, KC, RANK], F32R, AR + 45.5)
        junkG = at("junkG", [P, DV], F32, AR + 96)
        wstat = at("wstat", [P, 4, 4], F32, AR + 97)
        bend = at("bend", [P, 2, HG, NT], F32, AR + 97.25)
        sga = at("sga", [P, KC, S], F32, AR + 32)
        sgb = at("sgb", [P, KC, S], F32, AR + 8)
        ya_hi = at("ya_hi", [P, 4, S], F32R, AR + 24)
        ya_lo = at("ya_lo", [P, 4, S], F32R, AR + 88)
        mg_hi = at("mg_hi", [P, KC, S], F32R, AR + 64)
        mg_lo = at("mg_lo", [P, KC, S], F32R, AR + 48)
        f_hi = at("f_hi", [P, FC, S], F32R, AR)
        f_lo = at("f_lo", [P, FC, S], F32R, AR + 44)
        facc = [at(f"facc{b}", [P, S], F32, AR + 88 + 2 * b) for b in range(2)]

        ps = ctx.enter_context(nc.psum_tensor("ps", [P, 8, 512], F32))
        psf = ps[:].rearrange("p b n -> p (b n)")

        x_in = [sem(f"x_in{t}") for t in range(NT)]
        rows_in, small_in = sem("rows_in"), sem("small_in")
        postg_in = sem("postg_in")
        lr_in = sem("lr_in")
        padded = sem("padded")
        const_made = sem("const_made")
        raw_full = [sem(f"raw_full{s}") for s in range(2)]
        hi_made = sem("hi_made")
        unit_taken = sem("unit_taken")
        split_ready = sem("split_ready")
        steps = sem("steps")
        bank_free = [sem(f"bank_free{j}") for j in range(4)]
        act_line = sem("act_line")
        dve_line = sem("dve_line")
        pool_line = sem("pool_line")
        vt_done = sem("vt_done")
        vcol_ready = sem("vcol_ready")
        ss_ready, var_ready, std_ready = sem("ss_ready"), sem("var_ready"), sem("std_ready")
        src_ready = sem("src_ready")
        turned_pe, turned_hi, turned_lo = sem("turned_pe"), sem("turned_hi"), sem("turned_lo")
        x_ready = sem("x_ready")
        gate_pe, gate_dve, gate_act = sem("gate_pe"), sem("gate_dve"), sem("gate_act")
        tap_ready, qk_ready = sem("tap_ready"), sem("qk_ready")
        a_s, a_arg, a_exp, a_st, a_o = sem("a_s"), sem("a_arg"), sem("a_exp"), sem("a_st"), sem("a_o")
        y_src, y_turned, y_hi, y_lo = sem("y_src"), sem("y_turned"), sem("y_hi"), sem("y_lo")
        b_z, b_rest, b_beta, b_a, b_t, b_copied, b_o, b_y, b_hi, b_lo = (
            sem(n) for n in ("b_z", "b_rest", "b_beta", "b_a", "b_t", "b_copied", "b_o", "b_y", "b_hi", "b_lo"))
        pool_h, pool_ready, m_hi_done, m_lo_done = (
            sem(n) for n in ("pool_h", "pool_ready", "m_hi_done", "m_lo_done"))
        w_qkv, w_sq, w_n, w_tp, w_qk, w_s, w_neg, w_exp, w_p, w_t, w_copied, w_o, w_ya = (
            sem(n) for n in ("w_qkv", "w_sq", "w_n", "w_tp", "w_qk", "w_s", "w_neg", "w_exp", "w_p", "w_t",
                             "w_copied", "w_o", "w_ya"))
        l_pe, l_dve, l_act = sem("l_pe"), sem("l_dve"), sem("l_act")
        e_d, e_exp, e_qk, e_pe, e_at = sem("e_d"), sem("e_exp"), sem("e_qk"), sem("e_pe"), sem("e_at")
        g_o, g_taken = sem("g_o"), sem("g_taken")
        kept = sem("kept")
        gates_ready = sem("gates_ready")
        c_y, c_hi, c_lo = sem("c_y"), sem("c_hi"), sem("c_lo")
        f_silu, f_hi_done, f_lo_done = sem("f_silu"), sem("f_hi_done"), sem("f_lo_done")
        stored = sem("stored")

        def col(name, k=0):
            return vcol[:, COL[name] + k:COL[name] + k + 1]

        def rows(v, n):
            return v.rearrange("(r p) -> r p", p=P)

        def wview(w):
            return w.rearrange("(k p) n -> p k n", p=P)

        w_ab, w_oab, w_c, w_pool, w_oc = (
            wview(A["w_in_ab"][0]), wview(A["w_out_ab"][0]), wview(A["w_in_c"][0]), A["pool_w"][0],
            wview(A["w_out_c"][0]))
        w_2, w_ba, w_bb, w_o2, w_fi, w_fo = (
            wview(A[n][0]) for n in ("w_in_2", "w_branch_a_2", "w_branch_b_2", "w_out_2", "w_ffn_in_2",
                                     "w_ffn_out_2"))

        def cols(w, k0, nk, c0, n=512):
            return w[:, k0:k0 + nk, c0:c0 + n]

        block = ctx.enter_context(nc.Block())

        @block.sync
        def _(sp):
            vec_rows = [(A["pre_norm_g"].rearrange("a (r p) -> (a r) p", p=P), 16),
                        (rows(A["ln_mix_g_2"][0], 8), 8), (rows(A["ln_ffn_g_2"][0], 8), 8),
                        (A["conv_qk"][0].rearrange("w (r p) -> (w r) p", p=P), 64),
                        (rows(A["pool_scale"][0], 16), 16), (rows(A["b_gk_2"][0], 4), 4),
                        (rows(A["head_norm_g"][0], 8), 8)]
            r = 0
            for src, n in vec_rows:
                sp.dma_start(rawv[r:r + n, 0, :], src).then_inc(rows_in, 16)
                r += n
            for g in ("q_norm_g_2", "k_norm_g_2"):
                for half in range(2):
                    sp.dma_start(rawv[r:r + 1, 0, DH * half:DH * half + DH], A[g]).then_inc(rows_in, 16)
                r += 1
            sp.dma_start(rawv[r:r + 2, 0, :], rows(A["gla_norm_g_2"][0], 2)).then_inc(rows_in, 16)
            sp.dma_start(rawv[0:66, 1, :], A["conv_w_2"][0].rearrange("w (r p) -> (w r) p", p=P)).then_inc(rows_in, 16)
            sp.dma_start(rawv[66:88, 1, :], rows(A["conv_b_2"][0], 22)).then_inc(rows_in, 16)
            sp.dma_start(sinkb, A["sinks_2"][0].partition_broadcast(P)).then_inc(small_in, 16)
            sp.wait_ge(padded, 1)
            for n in range(2):
                sp.dma_start(wgate[:, :, 32 * n:32 * n + HA], cols(w_ab, 0, KC, 5 * D + HA * n, HA))\
                    .then_inc(small_in, 16)
            for n, b in enumerate(("bias_i", "bias_f")):
                sp.dma_start(bias4[:, n:n + 1], A[b].rearrange("a h -> h a")).then_inc(small_in, 16)

            def load(u, slot, src, width=512, nk=4, c0=0, inc=32):
                if isinstance(u, int):
                    if u >= 2:
                        sp.wait_ge(split_ready, u - 1)
                else:
                    sp.wait_ge(split_ready, u - 1)
                sp.dma_start(raw[slot][:, 0:nk, c0:c0 + width], src).then_inc(raw_full[slot], inc)

            def stream(name, w, c0, per, groups):
                u0 = UNIT[name]

                def one(i):
                    for q in range(per):
                        load(u0 + i * per + q, (u0 + q) % 2,
                             w[:, 4 * q:4 * q + 4, bass.ds(c0 + i * 512, 512)])
                if groups == 1:
                    one(0)
                elif u0 == 0:
                    one(0)
                    with sp.Fori(1, groups) as i:
                        one(i)
                else:
                    with sp.Fori(0, groups) as i:
                        one(i)

            stream("qb", w_ab, IN_AB_B, 2, 8)
            stream("qa", w_ab, 0, 2, 10)
            for n in range(2):
                for q in range(4):
                    load(UNIT["y0"] + 4 * n + q, q % 2, cols(w_oab, 4 * (q ^ 2), 4, 512 * n))
            for G in range(4):
                u = UNIT["mix"] + 5 * G
                load(u, u % 2, cols(w_c, 0, 4, 512 * G))
                load(u + 1, (u + 1) % 2, cols(w_c, 4, 4, 512 * G))
                load(u + 2, u % 2, cols(w_c, 0, 4, 2048 + 512 * G))
                load(u + 3, (u + 1) % 2, cols(w_c, 4, 4, 2048 + 512 * G))
                load(u + 4, u % 2, w_pool[G].rearrange("(k p) n -> p k n", p=P))
            stream("y1", w_oc, 0, 4, 2)
            stream("wq", w_2, C2["qa"], 2, 1)
            for q in range(2):
                load(UNIT["wkv"] + q, q, cols(w_2, 4 * q, 4, C2["kv"], 256), width=256)
            stream("gq", w_2, C2["gq"], 2, 1)
            stream("gk", w_2, C2["gk"], 2, 1)
            stream("gv", w_2, C2["gv"], 2, 4)
            stream("ga", w_2, C2["ga"], 2, 4)
            stream("bra", w_ba, 0, 1, 1)
            load(UNIT["bra"] + 1, 1, cols(w_ba, 0, 4, 512))
            stream("brb", w_bb, 0, 2, 2)
            stream("y2", w_o2, 0, 2, 2)
            with sp.Fori(0, FI) as i:
                for q in range(2):
                    u = UNIT["ffn"] + 2 * i + q
                    load(u, q, w_fi[:, 4 * q:4 * q + 4, bass.ds(i * 256, 256)], width=256, inc=16)
                    sp.dma_start(raw[q][:, :, 256:512], w_fi[:, 4 * q:4 * q + 4, bass.ds(DFF + i * 256, 256)])\
                        .then_inc(raw_full[q], 16)
            for n in range(2):
                for q in range(6):
                    nk = min(4, FC - 4 * q)
                    load(UNIT["y3"] + 6 * n + q, q % 2, cols(w_fo, 4 * q, nk, 512 * n), nk=nk)
            for n in range(2):
                for t in range(NT):
                    sp.wait_ge(bank_free[t], GROUP["y3"] + n + 1)
                    sp.dma_start(out[0, t * P:(t + 1) * P, n * 512:(n + 1) * 512],
                                 x[:, t, n * 512:(n + 1) * 512]).then_inc(stored, 16)
            sp.wait_ge(stored, 16 * 2 * NT)

        @block.gpsimd
        def _(pool):
            line = Line(pool, pool_line)

            def select(view, pattern, base, channel, compare=ALU.is_ge, fill=0.0):
                line.step(pool.affine_select(out=view, in_=view, pattern=pattern, base=base,
                                             channel_multiplier=channel, compare_op=compare, fill=fill))

            line.step(pool.memset(ident[:], 0.0))
            select(ident[:], [[-1, P]], 0, 1, ALU.not_equal, 1.0)
            line.step(pool.memset(sel[:], 0.0))
            pool.affine_select(out=sel[:], in_=sel[:], pattern=[[-1, HA], [0, P]], base=0, channel_multiplier=1,
                               compare_op=ALU.not_equal, fill=1.0).then_inc(const_made, 1)

            def split(u, slot, first=False):
                pool.wait_ge(raw_full[slot], (u // 2) * 32 + 32 if isinstance(u, int) else (u[0]) * 32 + 32)
                n = u if isinstance(u, int) else 2 * u[0] + u[1]
                if not first:
                    pool.wait_ge(steps, 4 * (n - 1))
                    pool.sem_inc(unit_taken, 1)
                pool.tensor_scalar(whi[slot][:], raw[slot][:], 1.0, 0.0, ALU.mult, ALU.add).then_inc(hi_made, 1)
                pool.wait_ge(hi_made, n + 1)
                pool.tensor_tensor(wlo[slot][:], raw[slot][:], whi[slot][:].bitcast(F32), ALU.subtract)\
                    .then_inc(split_ready, 1)

            split(0, 0, first=True)
            split(1, 1, first=True)
            line.step(pool.memset(tri[:], 1.0))
            select(tri[:], [[1, P]], 0, -1)
            line.step(pool.memset(below[:], 1.0))
            select(below[:], [[-1, P]], -1, 1)
            line.step(pool.memset(band[:], 0.0))
            select(band[:, 0:P], [[1, P]], -1, -1, fill=-1e30)
            select(band[:, P:], [[-1, P]], 0, 1, fill=-1e30)
            line.step(pool.memset(level[:], 0.0))
            for n, L in enumerate(LEVELS):
                v = level[:, n, :].rearrange("p (a two l) -> p a two l", two=2, l=L)[:, :, 1, :]
                line.step(pool.memset(v, 1.0))
                select(v, [[-2 * L, P // (2 * L)], [0, L]], 0, 1)
                select(v, [[2 * L, P // (2 * L)], [0, L]], L - 1, -1)
            pool.memset(spare[:, 0:4], 1.0).then_inc(const_made, 1)
            with pool.Fori(1, UNITS // 2) as i:
                split((i, 0), 0)
                split((i, 1), 1)

        @block.scalar
        def _(act):
            line = Line(act, act_line)
            stats = [0]

            def fn(out_, in_, f, **kw):
                return act.activation(out_, in_, f, **kw)

            def copy(out_, in_, **kw):
                return act.activation(out_, in_, ACT.Copy, **kw)

            def root(width):
                stats[0] += 1
                act.wait_ge(var_ready, stats[0])
                line.tell(fn(std[:, 0:width], var[:, 0:width], ACT.Sqrt), std_ready, stats[0])

            squares = [0]

            def square(in_, col_, width=D, junk=junk):
                squares[0] += 1
                line.tell(fn(junk[:, 0:width], in_, ACT.Square, accum_out=ss[:, col_:col_ + 1]), ss_ready, squares[0])

            def turn_hi(name, dst, c0, gname):
                T = TURNS[name]
                for c in range(KC):
                    act.wait_ge(turned_pe, 8 * T + c + 1)
                    line.tell(copy(dst[:, c0 + c], ps[:, c], scale=gname(c)), turned_hi, 8 * T + c + 1)

            for t in range(NT):
                act.dma_start(x[:, t], A["x"][0, t * P:(t + 1) * P, :]).then_inc(x_in[t], 16)

            act.wait_ge(padded, 1)
            line.step(fn(spare[:, 4:5], wgate[:, 0, 8:9], ACT.Sqrt))
            for t in range(NT):
                act.wait_ge(x_in[t], 16)
                square(x[:, t], t)
            root(NT)
            act.wait_ge(vcol_ready, 1)
            turn_hi("turn0", h_hi, 0, lambda c: col("pre", c))

            for name, dst, f, sc in (("qb", qB, ACT.Copy, DB ** -0.5), ("kb", kB, ACT.Copy, 1.0),
                                     ("vb", vB, ACT.Copy, 1.0), ("zb", szB, ACT.Silu, 1.0)):
                for n in range(2):
                    u, g = UNIT[name] + 2 * n + 1, GROUP[name] + n
                    for j in range(4):
                        act.wait_ge(steps, 4 * u + j + 1)
                        o = vB[:, j, n * 512:n * 512 + 512] if name == "vb" else dst[:, 4 * n + j]
                        line.tell(fn(o, ps[:, j], f, scale=sc), bank_free[j], g + 1)
                if name == "qb":
                    act.wait_ge(gate_dve, 3)
                    line.tell(fn(g_t[:], g_lf[:], ACT.Abs), gate_act, 1)
                    line.tell(fn(g_t[:], g_t[:], ACT.Exp, scale=-1.0), gate_act, 2)
                    line.tell(fn(g_t[:], g_t[:], ACT.Ln, bias=1.0), gate_act, 3)
                elif name == "kb":
                    act.wait_ge(gate_dve, 8)
                    line.tell(fn(g_t[:], g_m[:], ACT.Exp, scale=-1.0), gate_act, 4)

            def qk_tap(c):
                act.wait_ge(steps, 4 * (UNIT["qa"] + 2 * (c // 4) + 1) + c % 4 + 1)
                line.tell(copy((qA if c < 8 else kA)[:, c % 8], ps[:, c % 4], scale=col("convqk", 48 + c)),
                          tap_ready, c + 1)

            zps = psf[:, 2048:2048 + CAUSAL]
            for h in range(HB):
                act.wait_ge(b_z, h + 1)
                line.tell(fn(tB1[:], zps, ACT.Sigmoid, scale=-1.0), b_rest, h + 1)
                line.tell(fn(tB2[:], zps, ACT.Sigmoid), b_beta, h + 1)
                if h % 2:
                    for j in range(3):
                        qk_tap(2 * (h - 1) + j)
                act.wait_ge(b_t, h + 1)
                line.tell(copy(aTB[:], zps), b_copied, h + 1)
                if h % 2:
                    qk_tap(2 * (h - 1) + 3)
                act.wait_ge(b_y, h + 1)
                line.tell(copy(yB_hi[:, h], y32[:]), b_hi, h + 1)
            for c in range(16):
                act.wait_ge(bank_free[c % 4], GROUP["qa"] + c // 4 + 1)
                dst = (qA if c < 8 else kA)[:, c % 8]
                line.tell(fn(dst, dst, ACT.Silu), qk_ready, c + 1)
            for name, dst, f in (("va", vA, ACT.Copy), ("oa", soA, ACT.Sigmoid), ("za", szA, ACT.Silu)):
                for n in range(2):
                    u, g = UNIT[name] + 2 * n + 1, GROUP[name] + n
                    for j in range(4):
                        act.wait_ge(steps, 4 * u + j + 1)
                        if name == "va":
                            o = vA[:, j, 2 * n:2 * n + 2, 0:DA]
                            i = ps[:, j].rearrange("p (h d) -> p h d", d=DA)
                        else:
                            o, i = dst[:, j, n * 512:n * 512 + 512], ps[:, j]
                        line.tell(fn(o, i, f), bank_free[j], g + 1)
            act.wait_ge(gate_pe, 7)
            line.tell(copy(nMb[:, 0:HA], ps[:, 4:8]), gate_act, 5)
            act.dma_start(postg[:], A["post_norm_g"][0].partition_broadcast(P)).then_inc(postg_in, 16)

            def a_weights(h):
                for j in range(NT):
                    act.wait_ge(a_arg, 4 * h + j + 1)
                    w = WA[h % 2][:, A_OFF[j]:A_OFF[j] + S - P * j]
                    line.tell(fn(w, w, ACT.Exp), a_exp, 4 * h + j + 1)

            def a_squares(h):
                for t in range(NT):
                    act.wait_ge(bank_free[t], GROUP["a_out"] + h + 1)
                    square(soA[:, t, h * DA:h * DA + DA], 4 * h + t, width=DA, junk=junkA)

            a_weights(0)
            a_weights(1)
            for h in range(HA):
                a_squares(h)
                if h + 2 < HA:
                    a_weights(h + 2)
            root(16)
            def y_turn_hi(use, chunks, dst, gname):
                for c in chunks:
                    n = KC * use + c + 1
                    act.wait_ge(y_turned, n)
                    line.tell(copy(dst[:, c], ps[:, 4 + c % 4], scale=gname(c)), y_hi, n)

            y_turn_hi(0, range(KC), yA_hi, lambda c: col("hn", c))
            act.wait_ge(y_src, NT)
            for t in range(NT):
                act.dma_start(x[:, t], A["x"][0, t * P:(t + 1) * P, :]).then_inc(x_in[t], 16)

            def y_post(name):
                u, per = UNIT[name], 4
                for t in range(NT):
                    act.wait_ge(steps, 4 * (u + per - 1) + t + 1)
                    square(ps[:, t], t, width=512)
                def square_y(t):
                    act.wait_ge(steps, 4 * (u + 2 * per - 1) + t + 1)
                    square(ps[:, t], 4 + t, width=512)

                square_y(0)
                for now, last, following in rounds():
                    root(len(now) + len(last))
                    for t in following:
                        square_y(t)
                    for k, t in enumerate(now):
                        act.wait_ge(x_ready, NT * (1 if name == "y0" else 2) - NT + t + 1)
                        square(x[:, t], 20 + len(following) + k)

            y_post("y0")
            act.wait_ge(x_ready, NT)
            act.dma_start(postg[:], A["post_norm_g"][1].partition_broadcast(P)).then_inc(postg_in, 16)
            turn_hi("turn2", h_hi, 0, lambda c: col("pre", 8 + c))

            for G in range(4):
                u, g = UNIT["mix"] + 5 * G, GROUP["mix"] + 3 * G
                for j in range(5):
                    n = 4 * G + j
                    if j < 4:
                        act.wait_ge(steps, 4 * (u + 1) + j + 1)
                        if n >= 2:
                            act.wait_ge(pool_ready, 2 * n - 3)
                        line.tell(copy(pin[n % 2][:, PAD:], ps[:, j]), bank_free[j], g + 1)
                    if j:
                        act.wait_ge(pool_ready, 2 * n - 1)
                        line.tell(copy(pool_hi[:, j - 1], y32[:]), pool_h, n)
                for j in range(4):
                    act.wait_ge(steps, 4 * (u + 3) + j + 1)
                    line.tell(fn(szC[:, j], ps[:, j], ACT.Silu), bank_free[j], g + 2)
                for j in range(4):
                    n = 4 * G + j
                    act.wait_ge(bank_free[j], g + 3)
                    line.tell(copy(m_hi[:, n], szC[:, j]), m_hi_done, n + 1)
            y_post("y1")
            act.dma_start(wlr[:], cols(w_2, 0, KC, C2["lr"], RANK)).then_inc(lr_in, 16)
            act.dma_start(wup[:], A["w_gk_up_2"][0]).then_inc(lr_in, 16)
            turn_hi("turn3", h_hi, 0, lambda c: col("lnmix", c))
            for t in range(NT):
                act.dma_start(out[0, t * P:(t + 1) * P, :], x[:, t]).then_inc(kept, 16)

            for name, c0, w in (("wq", 0, 512), ("wkv", 512, 256)):
                u, g = UNIT[name] + 1, GROUP[name]
                for j in range(4):
                    act.wait_ge(steps, 4 * u + j + 1)
                    line.tell(copy(qkv[:, j, c0:c0 + w], ps[:, j, 0:w]), bank_free[j], g + 1)
            for t in range(NT):
                if t:
                    act.wait_ge(w_sq, t)
                line.tell(fn(junk2[:], qkv[:, t, 0:640], ACT.Square), w_qkv, t + 1)
            root(40)
            def project_out(name, dst, sc):
                u, g = UNIT[name] + 1, GROUP[name]
                for j in range(4):
                    act.wait_ge(steps, 4 * u + j + 1)
                    line.tell(copy(dst[:, j], ps[:, j], scale=sc), bank_free[j], g + 1)

            project_out("gq", qG, DK ** -0.5)
            act.wait_ge(l_dve, 2 + HG)
            line.step(fn(bG[:], gtmp[:], ACT.Abs))
            line.step(fn(bG[:], bG[:], ACT.Exp, scale=-1.0))
            line.tell(fn(bG[:], bG[:], ACT.Ln, bias=1.0), l_act, 1)
            for b in range(5):
                act.wait_ge(w_tp, b + 1)
                line.tell(copy(qkT[:, b], ps[:, 4 + b % 4], scale=col("qn" if b < 4 else "kn")), w_qk, b + 1)
            project_out("gk", kG, 1.0)

            def evacuate(name, n, j):
                act.wait_ge(steps, 4 * (UNIT[name] + 2 * n + 1) + j + 1)
                if name == "gv":
                    if n == 0 and j == 0:
                        act.wait_ge(kept, 16 * NT)
                    ins = copy(vG[:, j, n * 512:n * 512 + 512], ps[:, j])
                elif name == "gr":
                    ins = fn(rG[:, j, n * 512:n * 512 + 512], ps[:, j], ACT.Silu)
                else:
                    ins = copy((sga if name == "ga" else sgb)[:, 4 * n + j], ps[:, j])
                line.tell(ins, bank_free[j], GROUP[name] + n + 1)

            for n in range(2 * NT):
                i, c = n // 2, n % 2
                k0 = 0 if i else P
                group = ("gv" if n < 4 else "gr", n // 2 % 2)
                act.wait_ge(w_neg, n + 1)
                for b in range(4):
                    line.tell(fn(sm[:, b, k0:], sm[:, b, k0:], ACT.Exp, bias=wstat[:, 1, b:b + 1],
                                 accum_out=wstat[:, 2, b:b + 1]), w_exp, 5 * n + b + 1)
                line.tell(fn(wstat[:, 3], wstat[:, 3], ACT.Exp), w_exp, 5 * n + 5)
                if n % 2:
                    for j in range(3):
                        evacuate(*group, j)
                act.wait_ge(w_t, n + 1)
                line.tell(copy(pT[:, k0 // P:].rearrange("p k b q -> p (k b q)"), psf[:, 3072 + 4 * k0:]), w_copied, n + 1)
                if n % 2:
                    evacuate(*group, 3)
                act.wait_ge(w_o, n + 1)
                o = ps[0:DH, 6].rearrange("p (b two q) -> p b two q", two=2, q=P)
                for odd in range(2):
                    line.tell(copy(ya32[DH * odd:DH * odd + DH, 2 * c:2 * c + 2, i * P:i * P + P], o[:, :, odd, :]),
                              w_ya, 2 * n + odd + 1)

            def decay(s):
                act.wait_ge(e_d, s + 1)
                line.step(fn(dN[s % 2][:], dN[s % 2][:], ACT.Abs))
                line.tell(fn(dN[s % 2][:], dN[s % 2][:], ACT.Exp, scale=-1.0 / GATE), e_exp, s + 1)

            s = 0
            for slot in (4, 5, 6, 7, 12, 13, 14, 15):
                while s < min(STEPS_NEAR, near_steps(slot) + 2):
                    decay(s)
                    s += 1
                evacuate("ga", slot // 8, slot % 4)
            assert s == STEPS_NEAR
            act.wait_ge(e_pe, HG + STEPS_NEAR)
            for h in range(HG):
                s = FAR + 2 * h
                d = dG[0][:].rearrange("p (b t) -> p b t", t=P)
                bb = bG[:, h].rearrange("p (b t) -> p b t", t=P)
                act.wait_ge(e_qk, s)
                line.step(fn(d[:, 0:2], bb[:, 1::2], ACT.Exp, scale=1.0 / GATE))
                line.step(fn(d[:, 2], bb[:, 2], ACT.Exp, scale=1.0 / GATE))
                line.tell(fn(d[:, 3], bb[:, 3], ACT.Exp, scale=1.0 / GATE, bias=bend[:, 0, h, 2:3]), e_exp, s + 1)
                d = dG[1][:].rearrange("p (b t) -> p b t", t=P)
                line.step(fn(d[:, 0], bb[:, 0], ACT.Exp, scale=-1.0 / GATE, bias=bend[:, 0, h, 0:1]))
                line.step(fn(d[:, 1], bb[:, 2], ACT.Exp, scale=-1.0 / GATE, bias=bend[:, 0, h, 2:3]))
                line.step(fn(d[:, 2], bb[:, 0], ACT.Exp, scale=-1.0 / GATE, bias=bend[:, 1, h, 0:1]))
                line.tell(fn(d[:, 3], bb[:, 1], ACT.Exp, scale=-1.0 / GATE, bias=bend[:, 0, h, 1:2]), e_exp, s + 2)
            for c in range(4):
                line.tell(copy(ya_hi[:, c], ya32[:, c]), c_hi, c + 1)
            act.wait_ge(e_qk, FAR + 2 * HG)

            def g_squares(h):
                act.wait_ge(g_o, h + 1)
                for t in range(NT):
                    o = 2048 + 1024 * (h % 2) + DV * t
                    square(psf[:, o:o + DV], t, width=DV, junk=junkG)
                root(4)

            evacuate("gb", 0, 0)
            evacuate("gb", 0, 1)
            g_squares(0)
            evacuate("gb", 0, 2)
            evacuate("gb", 0, 3)
            for h in range(1, HG):
                g_squares(h)
            act.wait_ge(g_o, HG)
            for t in range(NT):
                act.dma_start(x[:, t], out[0, t * P:(t + 1) * P, :]).then_inc(x_in[t], 16)
            line.tell(fn(sga[:], sga[:], ACT.Sigmoid), gates_ready, 1)
            for j in range(4):
                evacuate("gb", 1, j)
            y_turn_hi(1, range(4), h_hi, lambda c: col("gla", c % 2))
            line.tell(fn(sgb[:], sgb[:], ACT.Sigmoid), gates_ready, 2)
            y_turn_hi(1, range(4, KC), h_hi, lambda c: col("gla", c % 2))
            for c in range(KC):
                act.wait_ge(c_y, c + 1)
                line.tell(copy(mg_hi[:, c], y32[:]), c_hi, 4 + c + 1)
            for t in range(NT):
                act.wait_ge(bank_free[t], GROUP["y2"] + 2)
                square(x[:, t], t)
                root(1)
            turn_hi("turn5", h_hi, 0, lambda c: col("lnffn", c))
            with act.Fori(0, FI) as i:
                for j in range(2):
                    act.wait_ge(bank_free[j], GROUP["ffn"] + i + 1)
                    line.tell(fn(facc[j][:], facc[j][:], ACT.Silu), f_silu, 2 * i + j + 1)
                for j in range(2):
                    act.wait_ge(bank_free[2 + j], GROUP["ffn"] + i + 1)
                    line.tell(copy(f_hi[:, bass.ds(2 * i + j, 1)], facc[j][:].unsqueeze(1)), f_hi_done, 2 * i + j + 1)

        @block.vector
        def _(dve):
            line = Line(dve, dve_line)
            seen = {"ss": 0, "root": 0, "src": 0}

            def tt(o, a, b, op):
                return dve.tensor_tensor(o, a, b, op)

            def stt(o, a, sc, b, op0, op1):
                return dve.scalar_tensor_tensor(o, a, sc, b, op0, op1)

            def squared(n=1):
                seen["ss"] += n
                dve.wait_ge(ss_ready, seen["ss"])

            def deviation(width, over, at_=0):
                r = seen["root"] = seen["root"] + 1
                a = slice(0, width)
                line.tell(dve.tensor_scalar(var[:, a], ss[:, at_:at_ + width], 1.0 / over, EPS, ALU.mult, ALU.add),
                          var_ready, r)
                dve.wait_ge(std_ready, r)
                line.step(dve.reciprocal(rs[:, a], std[:, a]))
                line.step(tt(nwt[:, a], rs[:, a], rs[:, a], ALU.mult))
                line.step(tt(nwt[:, a], nwt[:, a], var[:, a], ALU.mult))
                line.step(dve.tensor_scalar(nwt[:, a], nwt[:, a], -0.5, 1.5, ALU.mult, ALU.add))
                line.step(tt(rs[:, a], rs[:, a], nwt[:, a], ALU.mult))

            def src_done(ins):
                seen["src"] += 1
                line.tell(ins, src_ready, seen["src"])

            def turn_lo(name, dst, hi, c0, gname):
                T = TURNS[name]
                for c in range(KC):
                    dve.wait_ge(turned_hi, 8 * T + c + 1)
                    ins = stt(dst[:, c0 + c], ps[:, c], gname(c), hi[:, c0 + c].bitcast(F32), ALU.mult, ALU.subtract)
                    if c < 4:
                        line.tell(ins, bank_free[c], GROUP[name] + 1)
                    else:
                        line.tell(ins, turned_lo, 4 * T + c - 3)

            def scaled(t, k):
                src_done(dve.tensor_scalar(diag[:, t], ident[:], rs[:, k:k + 1], None, ALU.mult))

            line.tell(dve.memset(wgate[:], 0.0), padded, 1)
            for c in range(16):
                line.step(dve.memset(invc[:, c:c + 1], 1.0 / (c + 1)))
            squared(NT)
            deviation(NT, D)
            dve.wait_ge(vt_done, 2)
            line.step(dve.tensor_copy(vcol[:, 0:NV1], ps[:, 4, 0:NV1]))
            line.tell(dve.tensor_copy(vcol[:, NV1:], ps[:, 5, 0:NV2]), vcol_ready, 1)
            for t in range(NT):
                scaled(t, t)
            dve.wait_ge(small_in, 16 * 5)
            line.step(dve.tensor_copy(wg_hi[:], wgate[:]))
            line.tell(tt(wg_lo[:], wgate[:], wg_hi[:].bitcast(F32), ALU.subtract), gate_dve, 1)
            turn_lo("turn0", h_lo, h_hi, 0, lambda c: col("pre", c))

            dve.wait_ge(gate_pe, 1)
            line.tell(dve.tensor_scalar(g_ig[:], ps[0:HA, 4], bias4[:, 0:1], None, ALU.add), gate_dve, 2)
            line.step(dve.tensor_copy(g_lf[:], ps[32:32 + HA, 4]))
            line.tell(dve.tensor_scalar(g_lf[:], g_lf[:], bias4[:, 1:2], None, ALU.add), gate_dve, 3)
            dve.wait_ge(gate_act, 3)
            line.tell(stt(g_lf[:], g_lf[:], 0.0, g_t[:], ALU.min, ALU.subtract), gate_dve, 4)
            line.tell(dve.tensor_tensor_scan(g_b[:], g_lf[:], g_lf[:], 0.0, ALU.add, ALU.bypass), gate_dve, 5)
            line.tell(tt(g_ig[:], g_ig[:], g_b[:], ALU.subtract), gate_dve, 6)
            line.tell(dve.tensor_tensor_scan(g_lf[:], g_ig[:], g_ig[:], 0.0, ALU.max, ALU.bypass), gate_dve, 7)
            line.tell(tt(g_m[:], g_b[:], g_lf[:], ALU.add), gate_dve, 8)
            line.tell(dve.tensor_scalar(g_lf[:], g_lf[:], -1.0, None, ALU.mult), gate_dve, 9)
            dve.wait_ge(gate_pe, 2)
            line.tell(dve.tensor_copy(small[:, 216:232], ps[:, 4, 0:NT * HA]), gate_dve, 10)
            dve.wait_ge(gate_pe, 3)
            line.tell(dve.tensor_copy(small[:, 232:248], ps[:, 5, 0:NT * HA]), gate_dve, 11)

            def convolve(c):
                g = GROUP["qa"] + c // 4
                acc, p = (qA if c < 8 else kA)[:, c % 8], ps[:, c % 4]
                dve.wait_ge(tap_ready, c + 1)
                for sft in (1, 2, 3):
                    ins = stt(acc[:, sft:], p[:, 0:S - sft], col("convqk", 16 * (3 - sft) + c), acc[:, sft:],
                              ALU.mult, ALU.add)
                    if sft < 3:
                        line.step(ins)
                    else:
                        line.tell(ins, bank_free[c % 4], g + 1)

            def diagonals(t_):
                return (t_[:, SEG_T[0]:SEG_T[0] + P].unsqueeze(1),
                        t_[:, P:].rearrange("p (n c) -> p n c", c=3 * P)[:, :, 2 * P:])

            dve.wait_ge(const_made, 2)
            for h in range(HB):
                dve.wait_ge(b_rest, h + 1)
                for v in diagonals(tB1):
                    line.step(tt(v, v, tri[:].unsqueeze(1).broadcast_to([P, v.shape[1], P]), ALU.max))
                for i in range(NT):
                    r = tB1[:, SEG_T[i]:SEG_T[i] + P * (i + 1)][:, ::-1]
                    line.step(dve.tensor_tensor_scan(r, r, r, 1.0, ALU.mult, ALU.bypass))
                dve.wait_ge(b_beta, h + 1)
                line.step(tt(tB2[:, 0:CAUSAL - 1], tB2[:, 0:CAUSAL - 1], tB1[:, 1:CAUSAL], ALU.mult))
                one, three = diagonals(tB2)
                line.step(tt(one, one, below[:].unsqueeze(1), ALU.mult))
                line.tell(tt(three, three, below[:].unsqueeze(1).broadcast_to([P, 3, P]), ALU.mult), b_a, h + 1)
                if h % 2:
                    for j in range(3):
                        convolve(2 * (h - 1) + j)
                dve.wait_ge(b_o, h + 1)
                line.tell(tt(y32[:], ps[:, 7], szB[:, h], ALU.mult), b_y, h + 1)
                if h % 2:
                    convolve(2 * (h - 1) + 3)
                dve.wait_ge(b_hi, h + 1)
                line.tell(tt(yB_lo[:, h], y32[:], yB_hi[:, h].bitcast(F32), ALU.subtract), b_lo, h + 1)
            line.step(dve.memset(vA[:, :, :, DA:DA + 1], 1.0))

            def a_args(h):
                if h >= 2:
                    dve.wait_ge(a_o, 4 * (h - 1))
                for j in range(NT):
                    w = WA[h % 2][:, A_OFF[j]:A_OFF[j] + S - P * j]
                    line.tell(dve.tensor_scalar(w, nMb[:, h, P * j:], cT[:, j, h:h + 1], 0.0, ALU.add, ALU.min),
                              a_arg, 4 * h + j + 1)

            def a_scores(h):
                for j in range(NT):
                    dve.wait_ge(a_exp, 4 * h + j + 1)
                    w = WA[h % 2][:, A_OFF[j]:A_OFF[j] + S - P * j]
                    line.step(tt(w[:, 0:P], w[:, 0:P], tri[:], ALU.mult))
                    dve.wait_ge(a_s, 4 * h + j + 1)
                    line.tell(stt(w, ps[:, 4 + j, 0:S - P * j], DA ** -0.5, w, ALU.mult, ALU.mult),
                              a_st, 4 * h + j + 1)

            def a_outputs(h):
                dve.wait_ge(a_o, 4 * h + 4)
                line.step(dve.tensor_copy(den, ps[:, 0:4, DA]))
                line.step(stt(rden, den, -1.0, den, ALU.mult, ALU.max))
                line.step(tt(rden, rden, emT[:, :, h], ALU.max))
                line.step(dve.reciprocal(rden, rden))
                for t in range(NT):
                    so = soA[:, t, h * DA:h * DA + DA]
                    line.tell(stt(so, ps[:, t, 0:DA], rden[:, t:t + 1], so, ALU.mult, ALU.mult), bank_free[t],
                              GROUP["a_out"] + h + 1)

            dve.wait_ge(gate_act, 5)
            a_args(0)
            a_args(1)
            a_scores(0)
            for h in range(HA):
                if h + 1 < HA:
                    a_scores(h + 1)
                a_outputs(h)
                if h + 2 < HA:
                    a_args(h + 2)
            squared(16)
            deviation(16, DA)
            for t in range(NT):
                for h in range(HA):
                    so = soA[:, t, h * DA:h * DA + DA]
                    ins = stt(so, so, rs[:, 4 * h + t:4 * h + t + 1], szA[:, t, h * DA:h * DA + DA], ALU.mult, ALU.mult)
                    if h < HA - 1:
                        line.step(ins)
                    else:
                        line.tell(ins, y_src, t + 1)

            def y_turn_lo(use, c, dst, hi, weight):
                n = KC * use + c + 1
                dve.wait_ge(y_hi, n)
                line.tell(stt(dst[:, c], ps[:, 4 + c % 4], weight, hi[:, c].bitcast(F32), ALU.mult, ALU.subtract),
                          y_lo, n)

            for c in range(KC):
                y_turn_lo(0, c, yA_lo, yA_hi, col("hn", c))

            def y_post(name, posts, then):
                g = GROUP[name]
                dve.wait_ge(postg_in, 16 * posts)
                for t in range(NT):
                    squared()
                    line.tell(tt(yg[:, t, 0:512], ps[:, t], postg[:, 0:512], ALU.mult), bank_free[t], g + 1)
                def weigh(t, k):
                    squared()
                    line.tell(tt(yg[:, t, 512:], ps[:, t], postg[:, 512:], ALU.mult), bank_free[t], g + 2)
                    line.step(tt(ss[:, k:k + 1], ss[:, t:t + 1], ss[:, 4 + t:5 + t], ALU.add))

                weigh(0, 20)
                for now, last, following in rounds():
                    deviation(len(now) + len(last), D, 20)
                    for k, t in enumerate(now):
                        dve.wait_ge(x_in[t], 32)
                        line.tell(stt(x[:, t], yg[:, t], rs[:, k:k + 1], x[:, t], ALU.mult, ALU.add), x_ready,
                                  NT * (posts - 1) + t + 1)
                    for k, t in enumerate(last):
                        scaled(t, len(now) + k)
                    for k, t in enumerate(following):
                        weigh(t, 20 + k)
                    if now:
                        squared(len(now))
                turn_lo(then[0], h_lo, h_hi, 0, then[1])

            y_post("y0", 1, ("turn2", lambda c: col("pre", 8 + c)))

            for tile in pw + pin[1:]:
                line.step(dve.memset(tile[:, 0:PAD], 0.0))

            def pool_low(n):
                dve.wait_ge(pool_h, n + 1)
                line.tell(tt(pool_lo[:, n % 4], y32[:], pool_hi[:, n % 4].bitcast(F32), ALU.subtract), pool_ready,
                          2 * n + 2)

            for G in range(4):
                w, u, g = WINDOWS[G], UNIT["mix"] + 5 * G, GROUP["mix"] + 3 * G
                for j in range(4):
                    n = 4 * G + j
                    dve.wait_ge(bank_free[j], g + 1)
                    p_ = src = pin[n % 2]
                    for k in range(G + 1):
                        dst = pw[1 + k % 2]
                        line.step(tt(dst[:, PAD:], src[:, PAD:], src[:, PAD - (1 << k):PAD - (1 << k) + S], ALU.add))
                        src = dst
                    if j:
                        pool_low(n - 1)
                    head = pw[2 - G % 2]
                    line.step(tt(head[:, PAD:PAD + w], src[:, PAD:PAD + w], invc[:, 0:w], ALU.mult))
                    line.step(stt(y32[:], src[:, PAD:], 1.0 / w, p_[:, PAD:], ALU.mult, ALU.subtract))
                    line.tell(tt(y32[:, 0:w], head[:, PAD:PAD + w], p_[:, PAD:PAD + w], ALU.subtract),
                              pool_ready, 2 * n + 1)
                pool_low(4 * G + 3)
                for j in range(4):
                    n = 4 * G + j
                    dve.wait_ge(steps, 4 * (u + 4) + j + 1)
                    dve.wait_ge(bank_free[j], g + 2)
                    line.tell(stt(szC[:, j], ps[:, j], col("pscale", n), szC[:, j], ALU.mult, ALU.mult),
                              bank_free[j], g + 3)
                    dve.wait_ge(m_hi_done, n + 1)
                    line.tell(tt(m_lo[:, n], szC[:, j], m_hi[:, n].bitcast(F32), ALU.subtract), m_lo_done, n + 1)
            y_post("y1", 2, ("turn3", lambda c: col("lnmix", c)))

            dve.wait_ge(lr_in, 32)
            line.step(dve.tensor_copy(wlr_hi[:], wlr[:]))
            line.tell(tt(wlr_lo[:], wlr[:], wlr_hi[:].bitcast(F32), ALU.subtract), l_dve, 1)
            for t in range(NT):
                dve.wait_ge(w_qkv, t + 1)
                line.tell(dve.tensor_reduce(ss[:, 10 * t:10 * t + 10], junk2[:].rearrange("p (h d) -> p h d", d=DH),
                                            AX, ALU.add), w_sq, t + 1)
            deviation(40, DH)
            for t in range(NT):
                r = rs[:, 10 * t:10 * t + 10]
                for c in range(HKV):
                    line.step(tt(
                        qn[:, t, 0:512].rearrange("p (b c d) -> p b c d", c=HKV, d=DH)[:, :, c, :],
                        qkv[:, t, 256 * c:256 * c + 256].rearrange("p (b d) -> p b d", d=DH),
                        r[:, 4 * c:4 * c + 4].unsqueeze(2).broadcast_to([P, 4, DH]), ALU.mult))
                line.tell(tt(qn[:, t, 512:640].rearrange("p (c d) -> p c d", d=DH),
                             qkv[:, t, 512:640].rearrange("p (c d) -> p c d", d=DH),
                             r[:, 8:10].unsqueeze(2).broadcast_to([P, HKV, DH]), ALU.mult), w_n, t + 1)
            line.step(dve.memset(notfirst[:], 1.0))
            line.step(dve.memset(notfirst[:].rearrange("p (b t) -> p b t", t=P)[:, :, 0:1], 0.0))
            dve.wait_ge(l_pe, 1)
            line.tell(dve.tensor_copy(lrT[:], ps[0:RANK, 4]), l_dve, 2)
            for h in range(HG):
                dve.wait_ge(l_pe, 2 + h)
                line.tell(dve.tensor_scalar(gtmp[:, h], ps[:, 4 + h], col("bgk", h), None, ALU.add), l_dve, 3 + h)
            dve.wait_ge(l_act, 1)
            line.step(stt(gtmp[:], gtmp[:], 0.0, bG[:], ALU.min, ALU.subtract))
            for h in range(HG):
                line.step(dve.tensor_tensor_scan(bG[:, h], notfirst[:], gtmp[:, h], 0.0, ALU.mult, ALU.add))
            line.step(dve.tensor_scalar(bend[:, 0], bG[:].rearrange("p h (b t) -> p h b t", t=P)[:, :, :, P - 1],
                                        1.0 / GATE, None, ALU.mult))
            line.step(tt(bend[:, 1, :, 0:1], bend[:, 0, :, 0:1], bend[:, 0, :, 1:2], ALU.add))
            for b in range(2):
                line.step(dve.memset(kN[b][:], 0.0))
            sc4 = psf[:, 2048:3072].rearrange("p (h k) -> p h k", k=2 * P)
            for n in range(2 * NT):
                i, c = n // 2, n % 2
                k0 = 0 if i else P
                nk = 2 * P - k0
                sinks = sinkb[:, 4 * c:4 * c + 4]
                s_ = sm[:, :, k0:]
                dve.wait_ge(w_s, n + 1)
                line.step(stt(s_, sc4[:, :, k0:], DH ** -0.5, band[:, k0:].unsqueeze(1).broadcast_to([P, 4, nk]),
                              ALU.mult, ALU.add))
                line.step(dve.tensor_reduce(wstat[:, 0], s_, AX, ALU.max))
                line.step(tt(wstat[:, 0], wstat[:, 0], sinks, ALU.max))
                line.step(tt(wstat[:, 3], sinks, wstat[:, 0], ALU.subtract))
                line.tell(dve.tensor_scalar(wstat[:, 1], wstat[:, 0], -1.0, None, ALU.mult), w_neg, n + 1)
                dve.wait_ge(w_exp, 5 * n + 5)
                line.step(tt(wstat[:, 2], wstat[:, 2], wstat[:, 3], ALU.add))
                line.step(dve.reciprocal(wstat[:, 2], wstat[:, 2]))
                line.tell(tt(s_, s_, wstat[:, 2].unsqueeze(2).broadcast_to([P, 4, nk]), ALU.mult), w_p, n + 1)

            def pairs(v, L):
                return v.rearrange("p (a two l) -> p a two l", two=2, l=L)

            def heads(s):
                return s // (HG // 2), 2 * (s % (HG // 2))

            def flat(v):
                return v.rearrange("p h t -> p (h t)")

            def distance(s):
                n, h = heads(s)
                L = LEVELS[n]
                v = flat(bG[:, h:h + 2]).rearrange("p (a l) -> p a l", l=2 * L)
                line.tell(tt(flat(dN[s % 2][:]).rearrange("p (a l) -> p a l", l=2 * L), v,
                             v[:, :, L - 1:L].broadcast_to([P, S // L, 2 * L]), ALU.subtract), e_d, s + 1)

            def weighted(s):
                n, h = heads(s)
                dve.wait_ge(e_exp, s + 1)
                if s >= 2:
                    dve.wait_ge(e_pe, HG + s - 1)
                d, q, k, qo, ko = (pairs(flat(v), LEVELS[n]) for v in (
                    dN[s % 2][:], qG[:, h:h + 2], kG[:, h:h + 2], qN[s % 2][:], kN[s % 2][:]))
                line.step(tt(qo[:, :, 1], q[:, :, 1], d[:, :, 1], ALU.mult))
                line.tell(tt(ko[:, :, 0], k[:, :, 0], d[:, :, 0], ALU.mult), e_qk, s + 1)

            def take(s):
                n, h = heads(s)
                L, b = LEVELS[n], 4 + 2 * (s % 2)
                dve.wait_ge(e_pe, HG + s + 1)

                def second(v):
                    return v.rearrange("p b (a two l) -> p b a two l", two=2, l=L)[:, :, :, 1]

                mask = pairs(level[:, n], L)[:, :, 1].unsqueeze(1).broadcast_to([P, 2 * NT, P // (2 * L), L])
                line.tell(dve.copy_predicated(second(atD[:, h:h + 2].rearrange("p h b t -> p (h b) t")),
                                              mask.bitcast(I32),
                                              second(flat(ps[:, b:b + 2]).rearrange("p (b t) -> p b t", t=P))),
                          e_at, HG + s + 1)

            distance(0)
            dve.wait_ge(w_o, 2 * NT)
            distance(1)
            weighted(0)
            for h in range(HG):
                dve.wait_ge(e_pe, h + 1)
                line.tell(tt(atD[:, h], ps[:, 4 + h].rearrange("p (b t) -> p b t", t=P),
                             ident[:].unsqueeze(1).broadcast_to([P, 4, P]), ALU.mult), e_at, h + 1)
            for s in range(2, STEPS_NEAR + 2):
                if s < STEPS_NEAR:
                    distance(s)
                if s <= STEPS_NEAR:
                    weighted(s - 1)
                take(s - 2)
            def blocks(v):
                return v.rearrange("p (b t) -> p b t", t=P)

            for h in range(HG):
                s, b = FAR + 2 * h, h % 2
                dve.wait_ge(e_exp, s + 1)
                dve.wait_ge(e_pe, HG + FAR + max(0, h - 1))
                line.step(tt(blocks(qE[b][:])[:, 0:2], blocks(qG[:, h])[:, 1::2], blocks(dG[0][:])[:, 0:2], ALU.mult))
                line.tell(tt(blocks(qE[b][:])[:, 2:4], blocks(qG[:, h])[:, 2:4], blocks(dG[0][:])[:, 2:4], ALU.mult),
                          e_qk, s + 1)
                dve.wait_ge(e_exp, s + 2)
                line.step(tt(blocks(kE[b][:])[:, 0:2], blocks(kG[:, h])[:, 0::2], blocks(dG[1][:])[:, 0:2], ALU.mult))
                line.tell(tt(blocks(kE[b][:])[:, 2:4], blocks(kG[:, h])[:, 0:2], blocks(dG[1][:])[:, 2:4], ALU.mult),
                          e_qk, s + 2)
                if h >= 1:
                    dve.wait_ge(e_pe, HG + FAR + h)
                    line.tell(dve.tensor_copy(atO[:, h - 1].rearrange("p b t -> p (b t)"),
                                              psf[:, 2048 + 1024 * ((h - 1) % 2):2048 + 1024 * ((h - 1) % 2) + 768]),
                              e_at, HG + FAR + h)
            dve.wait_ge(e_pe, HG + FAR + HG)
            line.tell(dve.tensor_copy(atO[:, HG - 1].rearrange("p b t -> p (b t)"),
                                      psf[:, 2048 + 1024:2048 + 1024 + 768]), e_at, HG + FAR + HG)
            for c in range(4):
                dve.wait_ge(c_hi, c + 1)
                line.tell(tt(ya_lo[:, c], ya32[:, c], ya_hi[:, c].bitcast(F32), ALU.subtract), c_lo, c + 1)
            for h in range(HG):
                squared(4)
                deviation(4, DV)
                for t in range(NT):
                    r_ = rG[:, t, h * DV:h * DV + DV]
                    o = 2048 + 1024 * (h % 2) + DV * t
                    ins = stt(r_, psf[:, o:o + DV], rs[:, t:t + 1], r_, ALU.mult, ALU.mult)
                    if h < HG - 1:
                        if t < NT - 1:
                            line.step(ins)
                        else:
                            line.tell(ins, g_taken, h + 1)
                    else:
                        line.tell(ins, y_src, NT + t + 1)

            def branch_a(c):
                u, g, j = UNIT["bra"] + c // 4, GROUP["bra"] + c // 4, c % 4
                if c == 0:
                    dve.wait_ge(gates_ready, 1)
                dve.wait_ge(steps, 4 * u + j + 1)
                line.tell(tt(sga[:, c], ps[:, j], sga[:, c], ALU.mult), bank_free[j], g + 1)

            for c0 in (0, 4):
                for c in range(c0, c0 + 4):
                    y_turn_lo(1, c, h_lo, h_hi, col("gla", c % 2))
                for c in range(c0, c0 + 4):
                    branch_a(c)
            for c in range(KC):
                u, g, j = UNIT["brb"] + 2 * (c // 4) + 1, GROUP["brb"] + c // 4, c % 4
                if c == 0:
                    dve.wait_ge(gates_ready, 2)
                dve.wait_ge(steps, 4 * u + j + 1)
                line.tell(tt(sgb[:, c], ps[:, j], sgb[:, c], ALU.mult), bank_free[j], g + 1)
                line.tell(tt(y32[:], sgb[:, c], sga[:, c], ALU.add), c_y, c + 1)
                dve.wait_ge(c_hi, 4 + c + 1)
                line.tell(tt(mg_lo[:, c], y32[:], mg_hi[:, c].bitcast(F32), ALU.subtract), c_lo, 4 + c + 1)

            def normed(t):
                squared()
                deviation(1, D, t)
                scaled(t, 0)

            def residual(name, per):
                for n in range(2):
                    for t in range(NT):
                        dve.wait_ge(steps, 4 * (UNIT[name] + per * n + per - 1) + t + 1)
                        xs = x[:, t, 512 * n:512 * n + 512]
                        if name == "y2" and n == 0:
                            dve.wait_ge(x_in[t], 48)
                        line.tell(tt(xs, xs, ps[:, t], ALU.add), bank_free[t], GROUP[name] + n + 1)
                        if name == "y2" and n and t:
                            normed(t - 1)

            residual("y2", 2)
            normed(NT - 1)
            turn_lo("turn5", h_lo, h_hi, 0, lambda c: col("lnffn", c))

            for i in range(FI):
                for j in range(2):
                    c = 2 * i + j
                    dve.wait_ge(steps, 4 * (UNIT["ffn"] + 2 * i + 1) + j + 1)
                    line.step(dve.tensor_scalar(facc[j][:], ps[:, j], col("cw", 44 + c), col("cb", c), ALU.mult, ALU.add))
                    line.step(stt(facc[j][:, 1:], ps[:, j, 0:S - 1], col("cw", 22 + c), facc[j][:, 1:], ALU.mult, ALU.add))
                    line.tell(stt(facc[j][:, 2:], ps[:, j, 0:S - 2], col("cw", c), facc[j][:, 2:], ALU.mult, ALU.add),
                              bank_free[j], GROUP["ffn"] + i + 1)
                for j in range(2):
                    c = 2 * i + j
                    dve.wait_ge(steps, 4 * (UNIT["ffn"] + 2 * i + 1) + 2 + j + 1)
                    dve.wait_ge(f_silu, c + 1)
                    line.tell(tt(facc[j][:], ps[:, 2 + j], facc[j][:], ALU.mult), bank_free[2 + j], GROUP["ffn"] + i + 1)
                    dve.wait_ge(f_hi_done, c + 1)
                    line.tell(tt(f_lo[:, c], facc[j][:], f_hi[:, c].bitcast(F32), ALU.subtract), f_lo_done, c + 1)
            residual("y3", 6)

        @block.tensor
        def _(pe):
            def mm(o, l, r, start=True, stop=True):
                return pe.matmul(o, l, r, start=start, stop=stop)

            def unit(slot, mode, act, k0, nk, first, last, u, g, width=512, after={}, chunk_wait=None):
                pe.wait_ge(split_ready, u + 1)
                n_mm = 3 * nk
                for j in range(4):
                    if first:
                        pe.wait_ge(bank_free[j], g)
                    n = 0
                    for kk in range(nk):
                        if chunk_wait and j == 0:
                            chunk_wait(kk)
                        a_hi, a_lo = act(k0 + kk)
                        w_hi, w_lo = whi[slot][:, kk], wlo[slot][:, kk]
                        for w, a in ((w_hi, a_hi), (w_hi, a_lo), (w_lo, a_hi)):
                            if mode == "F":
                                ins = mm(ps[:, j], w[:, j * P:j * P + P], a, first and n == 0, last and n == n_mm - 1)
                            else:
                                ins = mm(ps[:, j, 0:width], a[:, j * P:j * P + P], w[:, 0:width],
                                         first and n == 0, last and n == n_mm - 1)
                            n += 1
                    ins.then_inc(steps, 1)
                    if j in after:
                        after[j]()

            def groups(name, mode, act, width=512, total=None, ready=None):
                n, per = next((n, per) for m, n, per in PLAN if m == name)
                total = total or 4 * per

                def one(i):
                    for q in range(per):
                        if ready and isinstance(i, int):
                            ready(min(4 * q + 4, total))
                        unit((UNIT[name] + q + (per % 2) * (i if isinstance(i, int) else 0)) % 2, mode, act, 4 * q,
                             min(4, total - 4 * q), q == 0, q == per - 1, UNIT[name] + i * per + q, GROUP[name] + i,
                             width)
                if n > 1 and per % 2 == 0:
                    if ready:
                        one(0)
                    with pe.Fori(1 if ready else 0, n) as i:
                        one(i)
                else:
                    for i in range(n):
                        one(i)

            def h_parts(k):
                return h_hi[:, k], h_lo[:, k]

            seen = {"src": 0}

            def turn(name):
                g = GROUP[name]
                for t in range(NT):
                    seen["src"] += 1
                    pe.wait_ge(src_ready, seen["src"])
                    for c in range(KC):
                        if t == 0 and c < 4 and g:
                            pe.wait_ge(bank_free[c], g)
                        ins = mm(ps[:, c, t * P:t * P + P], x[:, t, c * P:c * P + P], diag[:, t])
                        if t == NT - 1:
                            ins.then_inc(turned_pe, 1)

            def first_unit(name, after, mode):
                unit(UNIT[name] % 2, mode, h_parts, 0, 4, True, False, UNIT[name], GROUP[name],
                     chunk_wait=lambda k: pe.wait_ge(bank_free[k], GROUP[after] + 1))
                pe.wait_ge(turned_lo, 4 * TURNS[after] + 4)

            pe.wait_ge(const_made, 1)
            pe.wait_ge(rows_in, 16 * 14)
            pe.transpose(ps[:, 4, 0:NV1], rawv[:, 0, :], ident[:]).then_inc(vt_done, 1)
            pe.transpose(ps[:, 5, 0:NV2], rawv[0:NV2, 1, :], ident[0:NV2, 0:NV2]).then_inc(vt_done, 1)
            pe.wait_ge(vcol_ready, 1)

            turn("turn0")

            def thin(w_hi, w_lo, n):
                k2 = 0
                for k in range(KC):
                    for w, a in ((w_hi, h_hi), (w_hi, h_lo), (w_lo, h_hi)):
                        ins = mm(ps[0:n, 4], w[:, k], a[:, k], k2 == 0, k2 == 3 * KC - 1)
                        k2 += 1
                return ins

            first_unit("qb", "turn0", "F")
            pe.wait_ge(gate_dve, 1)
            thin(wg_hi, wg_lo, 36).then_inc(gate_pe, 1)
            unit(1, "F", h_parts, 4, 4, False, True, UNIT["qb"] + 1, GROUP["qb"])
            for q in range(2):
                unit(q, "F", h_parts, 4 * q, 4, q == 0, q == 1, UNIT["qb"] + 2 + q, GROUP["qb"] + 1)
            groups("kb", "F", h_parts)
            unit(0, "T", h_parts, 0, 4, True, False, UNIT["vb"], GROUP["vb"])
            pe.wait_ge(gate_act, 4)
            for b, rows_ in ((4, g_ig), (5, g_t)):
                for t in range(NT):
                    ins = pe.transpose(ps[:, b, t * HA:t * HA + HA], rows_[:, t * P:t * P + P], ident[0:HA, 0:HA])
                ins.then_inc(gate_pe, 1)
            unit(1, "T", h_parts, 4, 4, False, True, UNIT["vb"] + 1, GROUP["vb"])
            for q in range(2):
                unit(q, "T", h_parts, 4 * q, 4, q == 0, q == 1, UNIT["vb"] + 2 + q, GROUP["vb"] + 1)
            groups("zb", "F", h_parts)

            def b_scores(h):
                if h:
                    pe.wait_ge(b_copied, h)
                else:
                    pe.wait_ge(gate_dve, 11)
                for i in range(NT):
                    a = 2048 + SEG_T[i]
                    ins = mm(psf[:, a:a + P * (i + 1)], qB[:, h, i * P:i * P + P], kB[:, h, 0:P * (i + 1)])
                ins.then_inc(b_z, 1)

            def b_transpose(h):
                pe.wait_ge(b_a, h + 1)
                for j in range(NT):
                    for i in range(j, NT):
                        a, o = SEG_T[i] + j * P, 2048 + SEG_S[j] + (i - j) * P
                        ins = pe.transpose(psf[:, o:o + P], tB2[:, a:a + P], ident[:])
                ins.then_inc(b_t, 1)

            def b_outputs(h):
                pe.wait_ge(b_copied, h + 1)
                if h:
                    pe.wait_ge(b_y, h)
                for j in range(NT):
                    ins = mm(ps[:, 7, P * j:], vB[:, j, h * DB:h * DB + DB], aTB[:, SEG_S[j]:SEG_S[j] + S - P * j],
                             j == 0, j == NT - 1)
                ins.then_inc(b_o, 1)

            b_scores(0)
            for h in range(HB):
                q = h % 2
                unit(q, "F", h_parts, 4 * q, 4, q == 0, q == 1, UNIT["qa"] + h, GROUP["qa"] + h // 2,
                     after={2: lambda: b_transpose(h)})
                b_outputs(h)
                if h + 1 < HB:
                    b_scores(h + 1)
            groups("va", "T", h_parts)
            groups("oa", "T", h_parts)
            groups("za", "T", h_parts)

            def a_scores(h):
                for j in range(NT):
                    if h:
                        pe.wait_ge(a_st, 4 * h - 4 + j + 1)
                    for c in range(2):
                        ins = mm(ps[:, 4 + j, 0:S - P * j], kA[:, 2 * h + c, j * P:j * P + P], qA[:, 2 * h + c, P * j:],
                                 c == 0, c == 1)
                    ins.then_inc(a_s, 1)

            def a_outputs(h):
                pe.wait_ge(a_st, 4 * h + 4)
                for t in range(NT):
                    pe.wait_ge(bank_free[t], GROUP["a_out"] + h)
                    for j in range(t + 1):
                        a = A_OFF[j] + (t - j) * P
                        ins = mm(ps[:, t, 0:DA + 1], WA[h % 2][:, a:a + P], vA[:, j, h], j == 0, j == t)
                    ins.then_inc(a_o, 1)

            pe.wait_ge(b_y, HB)
            for h in range(HA):
                mm(ps[:, 4 + h], sel[:, h, :], g_lf[:]).then_inc(gate_pe, 1)
            pe.wait_ge(qk_ready, 16)
            pe.wait_ge(gate_act, 5)
            a_scores(0)
            for h in range(HA):
                if h + 1 < HA:
                    a_scores(h + 1)
                a_outputs(h)

            def y_turn(use, half, src):
                for t in range(NT):
                    pe.wait_ge(y_src, NT * use + t + 1)
                    for c in range(4 * half, 4 * half + 4):
                        if half and t == 0:
                            pe.wait_ge(y_lo, KC * use + c - 3)
                        ins = pe.transpose(ps[:, 4 + c % 4, t * P:t * P + P], src[:, t, c * P:c * P + P], ident[:])
                        if t == NT - 1:
                            ins.then_inc(y_turned, 1)

            def y0_parts(k):
                return (yB_hi[:, k], yB_lo[:, k]) if k < HB else (yA_hi[:, k - HB], yA_lo[:, k - HB])

            pe.wait_ge(b_lo, HB)
            for n in range(2):
                for q in range(4):
                    if n == 0 and q >= 2:
                        pe.wait_ge(y_lo, 4 * q - 4)
                    unit(q % 2, "T", y0_parts, 4 * q, 4, q == 0, q == 3, UNIT["y0"] + 4 * n + q, GROUP["y0"] + n,
                         after={1: lambda: y_turn(0, 0, soA), 3: lambda: y_turn(0, 1, soA)} if n == 0 and q == 1 else {})
            turn("turn2")

            def pool_parts(k):
                return pool_hi[:, k], pool_lo[:, k]

            for G in range(4):
                u, g = UNIT["mix"] + 5 * G, GROUP["mix"] + 3 * G
                for q in range(4):
                    if G == 0 and q == 0:
                        first_unit("mix", "turn2", "F")
                        continue
                    unit((u + q) % 2, "F", h_parts, 4 * (q % 2), 4, q % 2 == 0, q % 2 == 1, u + q, g + q // 2)
                pe.wait_ge(pool_ready, 8 * (G + 1))
                unit(u % 2, "F", pool_parts, 0, 4, True, True, u + 4, g + 2)
            groups("y1", "T", lambda k: (m_hi[:, k], m_lo[:, k]), ready=lambda k: pe.wait_ge(m_lo_done, k))
            turn("turn3")

            first_unit("wq", "turn3", "T")
            unit(1, "T", h_parts, 4, 4, False, True, UNIT["wq"] + 1, GROUP["wq"])
            groups("wkv", "T", h_parts, width=256)
            def pair(name, n, q, mode, after={}):
                unit(q, mode, h_parts, 4 * q, 4, q == 0, q == 1, UNIT[name] + 2 * n + q, GROUP[name] + n, after=after)

            pair("gq", 0, 0, "F")
            pe.wait_ge(l_dve, 1)
            thin(wlr_hi, wlr_lo, RANK).then_inc(l_pe, 1)

            def decay_up():
                pe.wait_ge(l_dve, 2)
                for h in range(HG):
                    mm(ps[:, 4 + h], wup[:, h * DK:h * DK + DK], lrT[:]).then_inc(l_pe, 1)

            pair("gq", 0, 1, "F", after={0: decay_up})
            pair("gk", 0, 0, "F")
            pe.wait_ge(w_n, NT)
            for b in range(5):
                if b < 4:
                    pe.wait_ge(l_dve, 3 + b)
                else:
                    pe.wait_ge(w_qk, 1)
                for t in range(NT):
                    ins = pe.transpose(ps[:, 4 + b % 4, t * P:t * P + P], qn[:, t, b * P:b * P + P], ident[:])
                ins.then_inc(w_tp, 1)
            pair("gk", 0, 1, "F")

            def w_scores(n):
                i, c = n // 2, n % 2
                k0 = (i - 1) * P if i else 0
                for b in range(4):
                    o = psf[:, 2048 + 256 * b + (0 if i else P):2048 + 256 * b + 256]
                    ins = mm(o, qkT[DH * c:DH * c + DH, b, i * P:i * P + P], qkT[DH * c:DH * c + DH, 4, k0:(i + 1) * P])
                ins.then_inc(w_s, 1)

            def w_transpose(n):
                pe.wait_ge(w_p, n + 1)
                if n:
                    pe.wait_ge(w_ya, 2 * n)
                for kb in range(0 if n >= 2 else 1, 2):
                    for b in range(4):
                        ins = pe.transpose(ps[:, 6 + kb, b * P:b * P + P], sm[:, b, kb * P:kb * P + P], ident[:])
                ins.then_inc(w_t, 1)

            def w_outputs(n):
                i, c = n // 2, n % 2
                pe.wait_ge(w_copied, n + 1)
                for kb in range(0 if i else 1, 2):
                    v = qkv[:, i - 1 + kb, 640 + DH * c:640 + DH * c + DH]
                    ins = mm(ps[0:DH, 6], v, pT[:, kb].rearrange("p b q -> p (b q)"), kb == (0 if i else 1), kb == 1)
                ins.then_inc(w_o, 1)

            pe.wait_ge(w_qk, 5)
            w_scores(0)
            for n in range(2 * NT):
                pair("gv" if n < 4 else "gr", n // 2 % 2, n % 2, "T", after={2: lambda: w_transpose(n)})
                w_outputs(n)
                if n + 1 < 2 * NT:
                    w_scores(n + 1)

            for h in range(HG):
                if h == 2:
                    pe.wait_ge(w_ya, 4 * NT)
                for b in range(NT):
                    ins = mm(ps[:, 4 + h, b * P:b * P + P], kG[:, h, b * P:b * P + P], qG[:, h, b * P:b * P + P])
                ins.then_inc(e_pe, 1)

            def level_steps(slot):
                for s in range(near_steps(slot), near_steps(slot + 1)):
                    pe.wait_ge(e_qk, s + 1)
                    pe.wait_ge(e_at, 2 * s + 2 if s < 2 else HG + s - 1)
                    L = LEVELS[s // (HG // 2)]
                    for i in range(2):
                        for b in range(NT):
                            o, q = (v[:, b * P:b * P + P].rearrange("p (a two l) -> p a two l", two=2, l=L)[:, :, 1]
                                    for v in (ps[:, 4 + 2 * (s % 2) + i], qN[s % 2][:, i]))
                            ins = mm(o, kN[s % 2][:, i, b * P:b * P + P], q)
                    ins.then_inc(e_pe, 1)

            for u in range(4):
                pair("ga", u // 2, u % 2, "F", after={j: lambda j=j: level_steps(4 * u + j) for j in range(4)})

            def far_products(h):
                o, b = 2048 + 1024 * (h % 2), h % 2
                pe.wait_ge(e_qk, FAR + 2 * h + 2)
                pe.wait_ge(e_at, HG + FAR + max(0, h - 1))
                mm(psf[:, o:o + P], kE[b][:, 0:P], qE[b][:, 0:P])
                mm(psf[:, o + P:o + 2 * P], kE[b][:, P:2 * P], qE[b][:, P:2 * P])
                mm(psf[:, o + 2 * P:o + 4 * P], kE[b][:, 2 * P:3 * P], qE[b][:, 2 * P:])
                mm(psf[:, o + 4 * P:o + 6 * P], kE[b][:, 3 * P:], qE[b][:, 2 * P:]).then_inc(e_pe, 1)

            far_block = {(0, 1): 0, (2, 3): 1, (0, 2): 2, (0, 3): 3, (1, 2): 4, (1, 3): 5}

            def g_outputs(h):
                pe.wait_ge(e_at, HG + FAR + HG)
                if h >= 2:
                    pe.wait_ge(g_taken, h - 1)
                for t in range(NT):
                    o = 2048 + 1024 * (h % 2) + DV * t
                    for j in range(t + 1):
                        w = atD[:, h, t] if j == t else atO[:, h, far_block[j, t]]
                        ins = mm(psf[:, o:o + DV], w, vG[:, j, h * DV:h * DV + DV], j == 0, j == t)
                ins.then_inc(g_o, 1)

            pair("gb", 0, 0, "F", after={j: lambda j=j: far_products(j) for j in range(4)})
            pair("gb", 0, 1, "F", after={1: lambda: g_outputs(0), 3: lambda: g_outputs(1)})
            pair("gb", 1, 0, "F", after={1: lambda: g_outputs(2), 3: lambda: g_outputs(3)})
            pair("gb", 1, 1, "F")

            def ya_parts(k):
                return ya_hi[:, k], ya_lo[:, k]

            pe.wait_ge(y_src, 2 * NT)
            y_turn(1, 0, rG)
            pe.wait_ge(c_lo, 4)
            for n in range(2):
                unit(n, "F", ya_parts, 0, 4, True, True, UNIT["bra"] + n, GROUP["bra"] + n,
                     after={3: lambda: y_turn(1, 1, rG)} if n == 0 else {})
            pe.wait_ge(y_lo, 2 * KC)
            groups("brb", "F", h_parts)
            groups("y2", "T", lambda k: (mg_hi[:, k], mg_lo[:, k]), ready=lambda k: pe.wait_ge(c_lo, 4 + k))
            turn("turn5")
            first_unit("ffn", "turn5", "F")
            unit(1, "F", h_parts, 4, 4, False, True, UNIT["ffn"] + 1, GROUP["ffn"])
            with pe.Fori(1, FI) as i:
                for q in range(2):
                    unit(q, "F", h_parts, 4 * q, 4, q == 0, q == 1, UNIT["ffn"] + i * 2 + q, GROUP["ffn"] + i)
            groups("y3", "T", lambda k: (f_hi[:, k], f_lo[:, k]), total=FC, ready=lambda k: pe.wait_ge(f_lo_done, k))


_INS = ["x", "pre_norm_g", "post_norm_g", "w_in_ab", "conv_qk", "bias_i", "bias_f", "head_norm_g", "w_out_ab",
        "w_in_c", "pool_w", "pool_scale", "w_out_c", "ln_mix_g_2", "w_in_2", "q_norm_g_2", "k_norm_g_2", "sinks_2",
        "w_gk_up_2", "b_gk_2", "gla_norm_g_2", "w_branch_a_2", "w_branch_b_2", "w_out_2", "ln_ffn_g_2",
        "w_ffn_in_2", "conv_w_2", "conv_b_2", "w_ffn_out_2"]


def kernel(**inputs):
    import concourse.bacc as bacc
    from concourse.bass_utils import run_bass_kernel_spmd

    nc = bacc.Bacc("TRN2", target_bir_lowering=False, num_devices=1)
    arrays, A = {}, {}
    for name in _INS:
        a = np.ascontiguousarray(inputs[name])
        arrays[f"in_{name}"] = a
        A[name] = nc.dram_tensor(f"in_{name}", a.shape, mybir.dt.from_np(a.dtype), kind="ExternalInput").ap()
    out = nc.dram_tensor("out_x", (1, S, D), F32, kind="ExternalOutput").ap()
    build(nc, A, out)
    r = run_bass_kernel_spmd(nc, [arrays], core_ids=[0])
    return r.results[0]["out_x"]
```
